# Optimizing a Trainium2 kernel written in Bass

```python
import jax, jax.numpy as jnp
from jax import lax
import numpy as np
import math

D_MODEL = 1024
BATCH = 1
SEQ = 512
DEPTH = 1

CHUNK = 64
Q_BLOCK = 128
SB_WIDTH = D_MODEL // 2
SB_HEAD_DIM = 64
SB_HEADS = SB_WIDTH // SB_HEAD_DIM
ML_WIDTH = D_MODEL - SB_WIDTH
ML_HEADS = 4
ML_HEAD_DIM = ML_WIDTH // ML_HEADS
MIX_WIDTH = SB_WIDTH + ML_WIDTH
CONV_WIDTH = 4
IN_SIZES = (SB_WIDTH, SB_WIDTH, SB_WIDTH, 2 * ML_WIDTH, ML_WIDTH, ML_WIDTH, ML_HEADS, ML_HEADS)
IN_WIDTH = 3 * SB_WIDTH + 4 * ML_WIDTH + 2 * ML_HEADS
PEER_HEADS = 8
PEER_NKEYS = 128
PEER_EXPERTS = PEER_NKEYS * PEER_NKEYS
PEER_TOPK = 16
PEER_QDIM = 256
PEER_HALF = PEER_QDIM // 2
PEER_TOKEN_BLOCK = 128
N_MOD = 6
EPS = 1e-6


def rms_norm(x, g):
    x32 = x.astype(jnp.float32)
    y = x32 * lax.rsqrt(jnp.mean(x32 * x32, axis=-1, keepdims=True) + EPS)
    return (y * g.astype(jnp.float32)).astype(x.dtype)

def causal_depthwise_conv(x, w):
    return lax.conv_general_dilated(
        x, w[:, None, :].astype(x.dtype), window_strides=(1,),
        padding=[(CONV_WIDTH - 1, 0)], dimension_numbers=('NWC', 'WIO', 'NWC'),
        feature_group_count=x.shape[-1])

def stick_breaking(q, k, v):
    s_len, d = q.shape[2], q.shape[-1]
    scale = d ** -0.5
    outs = []
    for t0 in range(0, s_len, Q_BLOCK):
        t1 = t0 + Q_BLOCK
        z = jnp.einsum('bhtd,bhsd->bhts', q[:, :, t0:t1], k[:, :, :t1]).astype(jnp.float32) * scale
        visible = jnp.arange(t1)[None, :] < jnp.arange(t0, t1)[:, None]
        log_keep = jnp.where(visible, jax.nn.log_sigmoid(-z), 0.0)
        log_between = lax.cumsum(log_keep, axis=3, reverse=True) - log_keep
        w = jnp.where(visible, jnp.exp(jax.nn.log_sigmoid(z) + log_between), 0.0)
        outs.append(jnp.einsum('bhts,bhsd->bhtd', w, v[:, :, :t1].astype(jnp.float32)))
    return jnp.concatenate(outs, axis=2).astype(v.dtype)

def mlstm(q, k, v, i_pre, f_pre):
    b, nh, s_len, d = q.shape
    nc = s_len // CHUNK
    f32 = jnp.float32

    def to_chunks(t):
        t = t.reshape((b, nh, nc, CHUNK) + t.shape[3:])
        return jnp.moveaxis(t, 2, 0)

    qc = to_chunks(q.astype(f32))
    kc = to_chunks(k.astype(f32) * (d ** -0.5))
    vc = to_chunks(v.astype(f32))
    a = jnp.cumsum(to_chunks(jax.nn.log_sigmoid(f_pre.astype(f32))), axis=-1)
    li = to_chunks(i_pre.astype(f32))
    causal = jnp.tril(jnp.ones((CHUNK, CHUNK), dtype=bool))

    def step(carry, inp):
        c_state, n_state, m_state = carry
        q_c, k_c, v_c, a_c, i_c = inp
        log_d = jnp.where(causal, a_c[..., :, None] - a_c[..., None, :] + i_c[..., None, :], -jnp.inf)
        log_inter = a_c + m_state[..., None]
        m_row = jnp.maximum(jnp.max(log_d, axis=-1), log_inter)
        w_intra = jnp.exp(log_d - m_row[..., None])
        w_inter = jnp.exp(log_inter - m_row)
        s_qk = jnp.einsum('bhtk,bhsk->bhts', q_c, k_c) * w_intra
        num = (jnp.einsum('bhts,bhsv->bhtv', s_qk, v_c)
               + w_inter[..., None] * jnp.einsum('bhvk,bhtk->bhtv', c_state, q_c))
        den = jnp.sum(s_qk, axis=-1) + w_inter * jnp.einsum('bhk,bhtk->bht', n_state, q_c)
        h = num / jnp.maximum(jnp.abs(den), jnp.exp(-m_row))[..., None]
        a_end = a_c[..., -1]
        log_w = a_end[..., None] - a_c + i_c
        m_new = jnp.maximum(a_end + m_state, jnp.max(log_w, axis=-1))
        w_s = jnp.exp(log_w - m_new[..., None])
        decay = jnp.exp(a_end + m_state - m_new)
        c_new = decay[..., None, None] * c_state + jnp.einsum('bhs,bhsv,bhsk->bhvk', w_s, v_c, k_c)
        n_new = decay[..., None] * n_state + jnp.einsum('bhs,bhsk->bhk', w_s, k_c)
        return (c_new, n_new, m_new), h

    init = (jnp.zeros((b, nh, d, d), f32), jnp.zeros((b, nh, d), f32), jnp.zeros((b, nh), f32))
    _, h = lax.scan(step, init, (qc, kc, vc, a, li))
    h = jnp.moveaxis(h, 0, 2).reshape(b, nh, s_len, d)
    return h.astype(v.dtype)

def peer(h, w_q, sub_keys, expert_u, expert_v):
    b, s_len, d = h.shape
    q = jnp.einsum('bsd,dq->bsq', h, w_q).reshape(b, s_len, PEER_HEADS, 2, PEER_HALF)
    scores = jnp.einsum('bshpc,hpnc->bshpn', q, sub_keys).astype(jnp.float32)
    top_s, top_i = lax.top_k(scores, PEER_TOPK)
    cand_s = (top_s[..., 0, :, None] + top_s[..., 1, None, :]).reshape(b, s_len, PEER_HEADS, PEER_TOPK * PEER_TOPK)
    cand_i = (top_i[..., 0, :, None] * PEER_NKEYS + top_i[..., 1, None, :]).reshape(b, s_len, PEER_HEADS, PEER_TOPK * PEER_TOPK)
    best_s, best_pos = lax.top_k(cand_s, PEER_TOPK)
    best_i = jnp.take_along_axis(cand_i, best_pos, axis=-1)
    gate = jax.nn.softmax(best_s, axis=-1)
    n_sel = PEER_HEADS * PEER_TOPK
    nb = (b * s_len) // PEER_TOKEN_BLOCK
    xs = h.reshape(nb, PEER_TOKEN_BLOCK, d)
    idx = best_i.reshape(nb, PEER_TOKEN_BLOCK, n_sel)
    gs = gate.reshape(nb, PEER_TOKEN_BLOCK, n_sel)

    def token_block(args):
        xb, ib, gb = args
        u = jnp.take(expert_u, ib, axis=0)
        act = jax.nn.gelu(jnp.einsum('td,tkd->tk', xb, u).astype(jnp.float32), approximate=False)
        vv = jnp.take(expert_v, ib, axis=0)
        return jnp.einsum('tk,tkd->td', (gb * act).astype(h.dtype), vv)

    y = lax.map(token_block, (xs, idx, gs))
    return y.reshape(b, s_len, d)

def first_inputs(seed: int = 0) -> dict:
    key = jax.random.key(seed)
    ks = jax.random.split(key, 20)
    nrm = jax.random.normal
    D = D_MODEL
    return {
        "x": nrm(ks[0], (BATCH, SEQ, D), jnp.float32),
        "c": nrm(ks[1], (BATCH, D), jnp.float32),
        "w_ada": nrm(ks[2], (DEPTH, D, N_MOD * D), jnp.float32) * (0.5 * D ** -0.5),
        "b_ada": nrm(ks[3], (DEPTH, N_MOD * D), jnp.float32) * 0.02,
        "g_norm1": 1.0 + 0.02 * nrm(ks[4], (DEPTH, D), jnp.float32),
        "w_in": nrm(ks[5], (DEPTH, D, IN_WIDTH), jnp.float32) * D ** -0.5,
        "b_igate": 0.1 * nrm(ks[6], (DEPTH, ML_HEADS), jnp.float32),
        "b_fgate": 3.0 + 3.0 * jax.random.uniform(ks[7], (DEPTH, ML_HEADS), jnp.float32),
        "conv_w": nrm(ks[8], (DEPTH, CONV_WIDTH, 2 * ML_WIDTH), jnp.float32) * CONV_WIDTH ** -0.5,
        "g_q_sb": 1.0 + 0.02 * nrm(ks[9], (DEPTH, SB_HEAD_DIM), jnp.float32),
        "g_k_sb": 1.0 + 0.02 * nrm(ks[10], (DEPTH, SB_HEAD_DIM), jnp.float32),
        "g_out_sb": 1.0 + 0.02 * nrm(ks[11], (DEPTH, SB_HEADS, SB_HEAD_DIM), jnp.float32),
        "g_out_ml": 1.0 + 0.02 * nrm(ks[12], (DEPTH, ML_HEADS, ML_HEAD_DIM), jnp.float32),
        "w_out": nrm(ks[13], (DEPTH, MIX_WIDTH, D), jnp.float32) * MIX_WIDTH ** -0.5,
        "g_norm2": 1.0 + 0.02 * nrm(ks[14], (DEPTH, D), jnp.float32),
        "w_q_peer": nrm(ks[15], (DEPTH, D, PEER_HEADS * PEER_QDIM), jnp.float32) * D ** -0.5,
        "sub_keys": nrm(ks[16], (DEPTH, PEER_HEADS, 2, PEER_NKEYS, PEER_HALF), jnp.float32) * PEER_HALF ** -0.5,
        "expert_u": nrm(ks[17], (DEPTH, PEER_EXPERTS, D), jnp.float32) * D ** -0.5,
        "expert_v": nrm(ks[18], (DEPTH, PEER_EXPERTS, D), jnp.float32),
    }

def first_block(x, c, w_ada, b_ada, g_norm1, w_in, b_igate, b_fgate, conv_w, g_q_sb, g_k_sb,
              g_out_sb, g_out_ml, w_out, g_norm2, w_q_peer, sub_keys, expert_u, expert_v):
    b, s_len, _ = x.shape
    cuts = []
    acc = 0
    for size in IN_SIZES[:-1]:
        acc += size
        cuts.append(acc)

    def to_heads(t, n):
        return t.reshape(b, s_len, n, -1).transpose(0, 2, 1, 3)

    for l in range(DEPTH):
        mod = jnp.einsum('bd,dm->bm', jax.nn.silu(c), w_ada[l]) + b_ada[l]
        shift1, scale1, gate1, shift2, scale2, gate2 = jnp.split(mod[:, None, :], N_MOD, axis=-1)

        h = rms_norm(x, g_norm1[l]) * (1 + scale1) + shift1
        proj = jnp.einsum('bsd,dn->bsn', h, w_in[l])
        q_sb, k_sb, v_sb, qk_ml, v_ml, o_ml, i_ml, f_ml = jnp.split(proj, cuts, axis=-1)

        q_sb = rms_norm(to_heads(q_sb, SB_HEADS), g_q_sb[l])
        k_sb = rms_norm(to_heads(k_sb, SB_HEADS), g_k_sb[l])
        y_sb = stick_breaking(q_sb, k_sb, to_heads(v_sb, SB_HEADS)).transpose(0, 2, 1, 3)
        y_sb = rms_norm(y_sb, g_out_sb[l])

        qk_ml = jax.nn.silu(causal_depthwise_conv(qk_ml, conv_w[l]))
        q_ml, k_ml = jnp.split(qk_ml, 2, axis=-1)
        i_pre = (i_ml + b_igate[l]).transpose(0, 2, 1)
        f_pre = (f_ml + b_fgate[l]).transpose(0, 2, 1)
        y_ml = mlstm(to_heads(q_ml, ML_HEADS), to_heads(k_ml, ML_HEADS), to_heads(v_ml, ML_HEADS), i_pre, f_pre)
        y_ml = rms_norm(y_ml.transpose(0, 2, 1, 3), g_out_ml[l]) * jax.nn.sigmoid(o_ml).reshape(b, s_len, ML_HEADS, ML_HEAD_DIM)

        mixed = jnp.concatenate([y_sb.reshape(b, s_len, SB_WIDTH), y_ml.reshape(b, s_len, ML_WIDTH)], axis=-1)
        x = x + gate1 * jnp.einsum('bsm,md->bsd', mixed, w_out[l])

        h2 = rms_norm(x, g_norm2[l]) * (1 + scale2) + shift2
        x = x + gate2 * peer(h2, w_q_peer[l], sub_keys[l], expert_u[l], expert_v[l])
    return x


DEPTH_2 = 2

N_META = 16
EPS_2 = 1e-5

N_A_LAYERS = DEPTH_2 // 2
N_B_LAYERS = DEPTH_2 - N_A_LAYERS

DIFF_HEAD_DIM = 64
DIFF_HEADS = D_MODEL // (2 * DIFF_HEAD_DIM)
DIFF_V_DIM = 2 * DIFF_HEAD_DIM
ROPE_THETA = 500000.0
ROT_DIM = DIFF_HEAD_DIM // 4

MLA_HEADS = D_MODEL // 64
MLA_NOPE = 64
MLA_ROPE = 32
MLA_V = 64
Q_LORA = 3 * D_MODEL // 8
KV_LORA = D_MODEL // 4
MLA_ROPE_THETA = 10000.0

D_FF = 128 * ((8 * D_MODEL // 3 + 127) // 128)
CONV_W = 3


def rms_norm_2(x, g):
    xf = x.astype(jnp.float32)
    y = xf * lax.rsqrt(jnp.mean(xf * xf, axis=-1, keepdims=True) + EPS_2)
    return (y * g.astype(jnp.float32)).astype(x.dtype)

def rotary(x, pos, theta, rot_dim):
    half = rot_dim // 2
    inv = 1.0 / (theta ** (jnp.arange(half, dtype=jnp.float32) / half))
    ang = pos.astype(jnp.float32)[:, None] * inv[None, :]
    cos = jnp.cos(ang)[None, :, None, :]
    sin = jnp.sin(ang)[None, :, None, :]
    xr = x[..., :rot_dim].astype(jnp.float32)
    x1, x2 = xr[..., :half], xr[..., half:]
    rot = jnp.concatenate([x1 * cos - x2 * sin, x2 * cos + x1 * sin], axis=-1).astype(x.dtype)
    return jnp.concatenate([rot, x[..., rot_dim:]], axis=-1)

def chunk_ids(pos):
    return jnp.where(pos < N_META, 0, 1 + (pos - N_META) // CHUNK)

def to_query_blocks(q, n_blocks):
    B, L, H, d = q.shape
    q = jnp.pad(q, ((0, 0), (0, n_blocks * Q_BLOCK - L), (0, 0), (0, 0)))
    return q.reshape(B, n_blocks, Q_BLOCK, H, d).transpose(1, 0, 2, 3, 4)

def from_query_blocks(o, L):
    nb, B, qb, H, d = o.shape
    return o.transpose(1, 0, 2, 3, 4).reshape(B, nb * qb, H, d)[:, :L]

def diff_attention(q1, q2, k1, k2, v, lam, q_chunk_blocks, k_chunk):
    L = k1.shape[1]
    nb = q_chunk_blocks.shape[0]
    scale = DIFF_HEAD_DIM ** -0.5

    def block(args):
        qb1, qb2, qc = args
        mask = k_chunk[None, :] <= qc[:, None]

        def probs(qb, k):
            s = jnp.einsum('bqhd,bkhd->bhqk', qb, k).astype(jnp.float32) * scale
            return jax.nn.softmax(jnp.where(mask, s, -jnp.inf), axis=-1)

        a = probs(qb1, k1) - lam * probs(qb2, k2)
        return jnp.einsum('bhqk,bkhd->bqhd', a.astype(v.dtype), v)

    o = lax.map(block, (to_query_blocks(q1, nb), to_query_blocks(q2, nb), q_chunk_blocks))
    return from_query_blocks(o, L)

def mla_attention(q_nope, q_rope, k_nope, k_rope, v, q_chunk_blocks, k_chunk):
    L = k_nope.shape[1]
    nb = q_chunk_blocks.shape[0]
    scale = (MLA_NOPE + MLA_ROPE) ** -0.5

    def block(args):
        qn, qr, qc = args
        mask = k_chunk[None, :] <= qc[:, None]
        s = (jnp.einsum('bqhd,bkhd->bhqk', qn, k_nope)
             + jnp.einsum('bqhr,bkr->bhqk', qr, k_rope)).astype(jnp.float32) * scale
        p = jax.nn.softmax(jnp.where(mask, s, -jnp.inf), axis=-1)
        return jnp.einsum('bhqk,bkhd->bqhd', p.astype(v.dtype), v)

    o = lax.map(block, (to_query_blocks(q_nope, nb), to_query_blocks(q_rope, nb), q_chunk_blocks))
    return from_query_blocks(o, L)

def diff_attn_layer(h, g_norm, w_qkv, lq1, lk1, lq2, lk2, g_sub, w_o, layer_idx, pos, qcb, kc):
    B, L, _ = h.shape
    H, d = DIFF_HEADS, DIFF_HEAD_DIM
    xn = rms_norm_2(h, g_norm)
    qkv = xn @ w_qkv
    q, k, v = jnp.split(qkv, [2 * H * d, 4 * H * d], axis=-1)
    q = rotary(q.reshape(B, L, 2 * H, d), pos, ROPE_THETA, ROT_DIM).reshape(B, L, H, 2, d)
    k = rotary(k.reshape(B, L, 2 * H, d), pos, ROPE_THETA, ROT_DIM).reshape(B, L, H, 2, d)
    v = v.reshape(B, L, H, DIFF_V_DIM)
    lam_init = 0.8 - 0.6 * math.exp(-0.3 * layer_idx)
    lam = (jnp.exp(jnp.sum(lq1.astype(jnp.float32) * lk1.astype(jnp.float32)))
           - jnp.exp(jnp.sum(lq2.astype(jnp.float32) * lk2.astype(jnp.float32))) + lam_init)
    o = diff_attention(q[..., 0, :], q[..., 1, :], k[..., 0, :], k[..., 1, :], v, lam, qcb, kc)
    o = rms_norm_2(o, g_sub) * (1.0 - lam_init)
    return h + o.reshape(B, L, H * DIFF_V_DIM) @ w_o

def shared_latent_kv(h, g_norm, w_dkv, g_kv, w_ukv, pos):
    B, L, _ = h.shape
    xn = rms_norm_2(h, g_norm)
    ckv = xn @ w_dkv
    c_kv = rms_norm_2(ckv[..., :KV_LORA], g_kv)
    k_rope = rotary(ckv[..., None, KV_LORA:], pos, MLA_ROPE_THETA, MLA_ROPE)[:, :, 0]
    kv = (c_kv @ w_ukv).reshape(B, L, MLA_HEADS, MLA_NOPE + MLA_V)
    return kv[..., :MLA_NOPE], k_rope, kv[..., MLA_NOPE:]

def mla_layer(h, g_norm, w_dq, g_q, w_uq, w_o, k_nope, k_rope, v, pos, qcb, kc):
    B, L, _ = h.shape
    xn = rms_norm_2(h, g_norm)
    c_q = rms_norm_2(xn @ w_dq, g_q)
    q = (c_q @ w_uq).reshape(B, L, MLA_HEADS, MLA_NOPE + MLA_ROPE)
    q_nope = q[..., :MLA_NOPE]
    q_rope = rotary(q[..., MLA_NOPE:], pos, MLA_ROPE_THETA, MLA_ROPE)
    o = mla_attention(q_nope, q_rope, k_nope, k_rope, v, qcb, kc)
    return h + o.reshape(B, L, MLA_HEADS * MLA_V) @ w_o

def conv_ffn(h, g_norm, w_in, conv_w, conv_b, w_out):
    L = h.shape[1]
    xn = rms_norm_2(h, g_norm)
    a, b = jnp.split(xn @ w_in, 2, axis=-1)
    ap = jnp.pad(a, ((0, 0), (CONV_W - 1, 0), (0, 0)))
    a_conv = conv_b
    for j in range(CONV_W):
        a_conv = a_conv + ap[:, j:j + L] * conv_w[j]
    return h + (jax.nn.silu(a_conv) * b) @ w_out

def second_inputs(seed: int = 0) -> dict:
    key = jax.random.key(seed)
    ks = iter(jax.random.split(key, 32))
    f32 = jnp.float32

    def nrm(shape, scale):
        return jax.random.normal(next(ks), shape, f32) * scale

    def gain(shape):
        return 1.0 + 0.02 * jax.random.normal(next(ks), shape, f32)

    nA, nB = N_A_LAYERS, N_B_LAYERS
    qkv_out = 4 * DIFF_HEADS * DIFF_HEAD_DIM + DIFF_HEADS * DIFF_V_DIM
    return {
        "x": nrm((BATCH, SEQ, D_MODEL), 1.0),
        "meta_tokens": nrm((N_META, D_MODEL), 1.0),
        "a_attn_norm": gain((nA, D_MODEL)),
        "a_w_qkv": nrm((nA, D_MODEL, qkv_out), D_MODEL ** -0.5),
        "a_lambda_q1": nrm((nA, DIFF_HEAD_DIM), 0.1),
        "a_lambda_k1": nrm((nA, DIFF_HEAD_DIM), 0.1),
        "a_lambda_q2": nrm((nA, DIFF_HEAD_DIM), 0.1),
        "a_lambda_k2": nrm((nA, DIFF_HEAD_DIM), 0.1),
        "a_sub_norm": gain((nA, DIFF_V_DIM)),
        "a_w_o": nrm((nA, DIFF_HEADS * DIFF_V_DIM, D_MODEL), (DIFF_HEADS * DIFF_V_DIM) ** -0.5),
        "kv_norm": gain((D_MODEL,)),
        "kv_w_dkv": nrm((D_MODEL, KV_LORA + MLA_ROPE), D_MODEL ** -0.5),
        "kv_a_norm": gain((KV_LORA,)),
        "kv_w_ukv": nrm((KV_LORA, MLA_HEADS * (MLA_NOPE + MLA_V)), KV_LORA ** -0.5),
        "b_attn_norm": gain((nB, D_MODEL)),
        "b_w_dq": nrm((nB, D_MODEL, Q_LORA), D_MODEL ** -0.5),
        "b_q_a_norm": gain((nB, Q_LORA)),
        "b_w_uq": nrm((nB, Q_LORA, MLA_HEADS * (MLA_NOPE + MLA_ROPE)), Q_LORA ** -0.5),
        "b_w_o": nrm((nB, MLA_HEADS * MLA_V, D_MODEL), (MLA_HEADS * MLA_V) ** -0.5),
        "ffn_norm": gain((DEPTH_2, D_MODEL)),
        "ffn_w_in": nrm((DEPTH_2, D_MODEL, 2 * D_FF), D_MODEL ** -0.5),
        "ffn_conv_w": nrm((DEPTH_2, CONV_W, D_FF), CONV_W ** -0.5),
        "ffn_conv_b": nrm((DEPTH_2, D_FF), 0.01),
        "ffn_w_out": nrm((DEPTH_2, D_FF, D_MODEL), D_FF ** -0.5),
        "final_norm": gain((D_MODEL,)),
    }

def second_block(x, meta_tokens, a_attn_norm, a_w_qkv, a_lambda_q1, a_lambda_k1, a_lambda_q2,
              a_lambda_k2, a_sub_norm, a_w_o, kv_norm, kv_w_dkv, kv_a_norm, kv_w_ukv,
              b_attn_norm, b_w_dq, b_q_a_norm, b_w_uq, b_w_o, ffn_norm, ffn_w_in,
              ffn_conv_w, ffn_conv_b, ffn_w_out, final_norm):
    B = x.shape[0]
    meta = jnp.broadcast_to(meta_tokens[None].astype(x.dtype), (B, N_META, D_MODEL))
    h = jnp.concatenate([meta, x], axis=1)
    L = h.shape[1]
    pos = jnp.arange(L, dtype=jnp.int32)
    n_blocks = -(-L // Q_BLOCK)
    kc = chunk_ids(pos)
    qcb = chunk_ids(jnp.arange(n_blocks * Q_BLOCK, dtype=jnp.int32)).reshape(n_blocks, Q_BLOCK)

    k_nope = k_rope = v_shared = None
    for layer in range(DEPTH_2):
        if layer < N_A_LAYERS:
            h = diff_attn_layer(h, a_attn_norm[layer], a_w_qkv[layer], a_lambda_q1[layer],
                                a_lambda_k1[layer], a_lambda_q2[layer], a_lambda_k2[layer],
                                a_sub_norm[layer], a_w_o[layer], layer, pos, qcb, kc)
        else:
            if layer == N_A_LAYERS:
                k_nope, k_rope, v_shared = shared_latent_kv(h, kv_norm, kv_w_dkv, kv_a_norm,
                                                            kv_w_ukv, pos)
            i = layer - N_A_LAYERS
            h = mla_layer(h, b_attn_norm[i], b_w_dq[i], b_q_a_norm[i], b_w_uq[i], b_w_o[i],
                          k_nope, k_rope, v_shared, pos, qcb, kc)
        h = conv_ffn(h, ffn_norm[layer], ffn_w_in[layer], ffn_conv_w[layer],
                     ffn_conv_b[layer], ffn_w_out[layer])
    return rms_norm_2(h, final_norm)[:, N_META:]


def setup_inputs(seed=0):
    out = dict(first_inputs(seed))
    for name, value in second_inputs(seed + 1).items():
        if name != "x":
            out[name + "_2"] = value
    return out


def reference(
    x, c, w_ada, b_ada, g_norm1, w_in, b_igate, b_fgate, conv_w, g_q_sb, g_k_sb, g_out_sb,
    g_out_ml, w_out, g_norm2, w_q_peer, sub_keys, expert_u, expert_v, meta_tokens_2,
    a_attn_norm_2, a_w_qkv_2, a_lambda_q1_2, a_lambda_k1_2, a_lambda_q2_2, a_lambda_k2_2,
    a_sub_norm_2, a_w_o_2, kv_norm_2, kv_w_dkv_2, kv_a_norm_2, kv_w_ukv_2, b_attn_norm_2,
    b_w_dq_2, b_q_a_norm_2, b_w_uq_2, b_w_o_2, ffn_norm_2, ffn_w_in_2, ffn_conv_w_2,
    ffn_conv_b_2, ffn_w_out_2, final_norm_2,
):
    x = first_block(
        x, c, w_ada, b_ada, g_norm1, w_in, b_igate, b_fgate, conv_w, g_q_sb, g_k_sb, g_out_sb,
        g_out_ml, w_out, g_norm2, w_q_peer, sub_keys, expert_u, expert_v,
    )
    return second_block(
        x, meta_tokens_2, a_attn_norm_2, a_w_qkv_2, a_lambda_q1_2, a_lambda_k1_2, a_lambda_q2_2,
        a_lambda_k2_2, a_sub_norm_2, a_w_o_2, kv_norm_2, kv_w_dkv_2, kv_a_norm_2, kv_w_ukv_2,
        b_attn_norm_2, b_w_dq_2, b_q_a_norm_2, b_w_uq_2, b_w_o_2, ffn_norm_2, ffn_w_in_2,
        ffn_conv_w_2, ffn_conv_b_2, ffn_w_out_2, final_norm_2,
    )


_drawn_inputs = setup_inputs


def setup_inputs(seed=0):
    import zlib

    import numpy as np

    out = dict(_drawn_inputs(seed))
    spreads = {}
    factors = {'g_norm1': 3.521,
     'b_igate': 64.0,
     'g_q_sb': 5.896,
     'g_k_sb': 5.667,
     'g_out_sb': 3.327,
     'g_out_ml': 4.29,
     'a_lambda_q1_2': 8.0,
     'a_sub_norm_2': 3.963,
     'kv_norm_2': 8.0,
     'kv_a_norm_2': 8.0,
     'b_attn_norm_2': 8.0,
     'b_q_a_norm_2': 8.0,
     'ffn_norm_2': 3.373,
     'ffn_conv_b_2': 8.0,
     'final_norm_2': 8.071}
    for name, (base, spread) in spreads.items():
        noise = np.random.default_rng([zlib.crc32(name.encode()), seed]).standard_normal(out[name].shape)
        drawn = base * np.exp(spread * noise) if base else spread * noise
        out[name] = __import__('jax').numpy.asarray(drawn.astype(out[name].dtype))
    for name, factor in factors.items():
        out[name] = (out[name] * factor).astype(out[name].dtype)
    return out
```

```python
from contextlib import ExitStack
import math

import numpy as np

import concourse.bass as bass
from concourse import mybir

F32 = mybir.dt.float32
BF16 = mybir.dt.bfloat16
U32 = mybir.dt.uint32
ALU = mybir.AluOpType
ACT = mybir.ActivationFunctionType
AX = mybir.AxisListType.X

P = 128
D = 1024
DC = D // P
SEQ = 512
META = 16
L = META + SEQ
HALF = L // 2
TB = SEQ // P
BANK = 512
SB_HEADS, SB_DIM = 8, 64
ML_HEADS, ML_DIM = 4, 128
CONV1 = 4
PEER_HEADS, NKEYS, TOPK = 8, 128, 16
QH = 2 * PEER_HEADS
NSEL = PEER_HEADS * TOPK
DIFF_HEADS, DIFF_DIM, DIFF_V = 8, 64, 128
MLA_HEADS, NOPE, ROPE, MLA_V = 16, 64, 32, 64
QK_MLA = NOPE + ROPE
Q_LORA, KV_LORA = 384, 256
QC, KVC = Q_LORA // P, KV_LORA // P
D_FF = 2816
FC = D_FF // P
CONV2 = 3
CHUNK = 64
EPS1, EPS2 = 1e-6, 1e-5
LAM_INIT = 0.8 - 0.6 * math.exp(-0.3 * 0)
BIG = 1e30
LOWEST = -3.0e38

SLOT = 1024
RING = 4
STAGES = [("ada_shift1", 2), ("ada_scale1", 2), ("qk_sb", 2), ("v_sb", 1), ("qk_ml", 2), ("v_ml", 1),
          ("o_ml", 1), ("ada_gate1", 2), ("ada_shift2", 2), ("ada_scale2", 2), ("ada_gate2", 2),
          ("w_out", 2), ("peer_q", 4), ("experts", 64), ("qk_diff", 4), ("v_diff", 2), ("o_diff", 2),
          ("ffn_in0", 11), ("ffn_out0", 6), ("mla", 4), ("o_mla", 2), ("ffn_in1", 11), ("ffn_out1", 6)]
TURN = {}
_t = 0
for _n, _k in STAGES:
    TURN[_n] = _t
    _t += _k
TURNS = _t

VEC = {}
VECS = [("c", DC), ("b_ada", 6 * DC), ("g_norm1", DC), ("conv_w", DC * CONV1), ("g_q_sb", 1), ("g_k_sb", 1),
        ("g_out_sb", 4), ("g_out_ml", 4), ("g_norm2", DC), ("b_igate", 1), ("b_fgate", 1),
        ("w_gates", DC * 8), ("a_attn_norm", DC), ("lambdas", 4), ("a_sub_norm", 1), ("kv_norm", DC),
        ("kv_a_norm", KVC), ("b_attn_norm", DC), ("b_q_a_norm", QC), ("ffn_norm", 2 * DC),
        ("ffn_conv_w", 2 * FC * CONV2), ("ffn_conv_b", 2 * FC), ("final_norm", DC), ("eps", 2)]
NVEC = 0
for _n, _k in VECS:
    VEC[_n] = NVEC
    NVEC += _k

CONST = {}
NCONST = 0
for _n, _k in [("ident", P), ("ones", P), ("ones64", P), ("tri", P), ("neg_ones", P), ("iota", P),
               ("late", P), ("pick_head", ML_HEADS * P), ("first_half", P), ("lowest", CHUNK)]:
    CONST[_n] = NCONST
    NCONST += _k
TABLE = {}
NTABLE = 0
for _n, _k in [("cos_d", L), ("sin_d", L), ("cos_m", L), ("sin_m", L), ("swap_d", P), ("swap_m", QK_MLA)]:
    TABLE[_n] = NTABLE
    NTABLE += _k

ARENA = 37888
LOG_SEQ = 9
ROW_STEPS = LOG_SEQ + 3
MAX_STEPS = LOG_SEQ + 2
ROUTE = 26


class Norm:
    squares = 0
    groups = 0

    def __init__(self, groups, tokens):
        self.chunks = groups
        self.T = tokens
        self.q0, self.g0 = Norm.squares, Norm.groups
        Norm.squares += sum(len(g) for g in groups)
        Norm.groups += len(groups)
        self.done = Norm.groups


def build(nc, stream, consts_d, vecs_d, tables_d, x_d, meta_d, keys_d, out_d):
    with ExitStack() as ctx:
        def sbuf(name, shape, dt=F32):
            return ctx.enter_context(nc.sbuf_tensor(name, shape, dt))

        def sem(name):
            return ctx.enter_context(nc.semaphore(name))

        ring = sbuf("ring", [P, RING, SLOT])
        x = sbuf("x", [P, DC, L])
        hT = sbuf("hT", [P, DC, L])
        const = sbuf("const", [P, NCONST])
        vec = sbuf("vec", [P, NVEC])
        mod = sbuf("mod", [P, 6 * DC])
        gains = sbuf("gains", [P, 2, DC])
        silu_c = sbuf("silu_c", [P, DC])
        arena = sbuf("arena", [P, ARENA])
        ps = ctx.enter_context(nc.psum_tensor("ps", [P, 8, BANK], F32))

        def view(at, *dims, dt=F32, rows=P):
            n = int(np.prod(dims)) // (2 if dt == BF16 else 1)
            assert at + n <= ARENA, (at, dims)
            a = arena[0:rows, at:at + n]
            if dt != F32:
                a = a.bitcast(dt)
            if len(dims) == 2:
                a = a.rearrange("p (a b) -> p a b", b=dims[1])
            if len(dims) == 3:
                a = a.rearrange("p (a b c) -> p a b c", b=dims[1], c=dims[2])
            if len(dims) == 4:
                a = a.rearrange("p (a b c d) -> p a b c d", b=dims[1], c=dims[2], d=dims[3])
            return a

        def cst(name, n=P, rows=P):
            return const[0:rows, CONST[name]:CONST[name] + n]

        def col(name, i=0, rows=P):
            return vec[0:rows, VEC[name] + i:VEC[name] + i + 1]

        ident, ones, ones64 = cst("ident"), cst("ones"), cst("ones64")
        xf = x[:, :, META:L]
        hf = hT[:, :, META:L]

        qk = view(0, 8, SEQ)
        conv_in = view(4096, 8, SEQ + CONV1 - 1)
        v_sb = view(8216, TB, SEQ)
        v_ml = view(10264, TB, SEQ)
        sig_o = view(12312, 4, SEQ)
        mixed = view(14360, 8, SEQ)
        z_buf = view(18456, 2, 1280)
        sp_buf = view(21016, 2, 1280)
        w_buf = view(23576, 2, 1280)
        f_pad = [view(26136, 1024, rows=4), view(27160, 1024, rows=4)]
        m_pad = [view(28184, 1024, rows=4), view(29208, 1024, rows=4)]
        i_row = view(30232, SEQ, rows=4)
        f_row = view(30744, SEQ, rows=4)
        e_row = view(31256, SEQ, rows=4)
        n_row = view(31768, SEQ, rows=4)
        u_col = view(32280, TB, ML_HEADS)
        conv = view(32296, 8, SEQ)
        den = view(0, 2, SEQ)
        den_floor = view(1024, 2, SEQ)
        sq1 = view(21016, 2, SEQ)
        rstd1 = view(22040, 2, SEQ)

        q_peer = view(0, QH, SEQ)
        score = view(8216, QH, NKEYS)
        cand = view(10264, PEER_HEADS, TOPK * TOPK)
        onehot = view(12312, PEER_HEADS, TOPK, TOPK)
        top_v = view(18456, QH, TOPK)
        top_i = view(18712, QH, TOPK, dt=U32)
        top_if = view(18968, QH, TOPK)
        best = view(19224, PEER_HEADS, TOPK)
        pos = view(19352, PEER_HEADS, TOPK, dt=U32)
        pos_ab = view(19480, 2, NSEL, dt=U32)
        pos_abf = view(19736, 2, NSEL)
        routed = view(19992, 3, NSEL)
        gate_sum = view(20376, 2, PEER_HEADS)
        keys = view(26136, QH, NKEYS)
        G = [view(0, 32, SEQ), view(16384, 32, SEQ)]
        idx1 = view(32768, SEQ)
        idx2 = view(33280, SEQ)
        gate_t = view(20400, SEQ)
        gate_r = view(20912, SEQ)
        gate_p = view(33792, SEQ, 3, dt=BF16)
        hot2 = view(34560, 2, 8, NKEYS, dt=BF16)
        hot1g = view(35584, 2, 8, 3 * 32, dt=BF16)
        hot1 = view(36352, 2, 8, 32)
        act_e = view(36864, 2, SEQ)

        sq2 = view(0, 2, L)
        rstd2 = view(1056, 2, L)
        table = view(2112, NTABLE)

        def tab(name, n=L, rows=P):
            return table[0:rows, TABLE[name]:TABLE[name] + n]

        v_d = view(4448, 5, D)
        qk_d = view(9568, 16, L)
        raw_d = view(18016, 2, L)
        tmp_d = view(19072, 2, L)
        prob = view(20128, 2, 2, L)
        aT = view(22240, 2, 5, P)
        o_d = view(23520, 8, L)
        st_max = view(27744, 2, 2)
        st_nmax = view(27748, 2, 2)
        st_sum = view(27752, 2, 2)
        st_rec = view(27756, 2, 2)
        lam_p = view(27760, 2)
        lam_e = view(27762, 2)
        neg_lam = view(27764, 1)
        pm = view(27776, 16, META)
        pm_max = view(28032, 16)
        pm_sum = view(28048, 16)
        pm_rec = view(28064, 16)
        amT = view(28080, 16, META)
        gated = view(4448, FC, L)
        a_pad = view(16064, 2, L + CONV2 - 1)
        u_ffn = view(17124, 2, L)
        k_m = view(4448, MLA_HEADS, L)
        q_m = view(12896, MLA_HEADS, L)
        v_m = view(21344, 5, D)
        h_kv = view(21344, DC, L)
        o_m = view(26464, 8, L)
        ckv_raw = view(26464, KVC, L)
        ckv = view(27520, KVC, L)
        cq_raw = view(28576, QC, L)
        kr_raw = view(30688, L)
        raw_m = view(31216, 2, L)
        tmp_m = view(32272, 2, L)
        kr = view(33328, L)
        probm = view(33856, 2, L)
        aTm = view(34912, 2, 5, P)
        cqn = view(36192, QC, L)
        STM = 37776
        sm_max, sm_nmax, sm_sum, sm_rec = (view(STM + 2 * k, 2) for k in range(4))
        pmm = view(35000, 16, META)
        pmm_max, pmm_sum, pmm_rec = (view(35256 + 16 * k, 16) for k in range(3))
        amTm = view(35304, 16, META)

        inputs_in = sem("inputs_in")
        keys_in = sem("keys_in")
        tables_in = sem("tables_in")
        slot_loaded = [sem(f"slot_loaded{s}") for s in range(RING)]
        slot_used = sem("slot_used")
        sq_ready = sem("sq_ready")
        sq_summed = sem("sq_summed")
        ln_done = sem("ln_done")
        rstd_ready = sem("rstd_ready")
        normed = sem("normed")
        silu_c_ready = sem("silu_c_ready")
        mod_ready = sem("mod_ready")
        gains_ready = sem("gains_ready")
        shifted = sem("shifted")
        gates_ready = sem("gates_ready")
        gates_taken = sem("gates_taken")
        win_taken = sem("win_taken")
        pads_zeroed = sem("pads_zeroed")
        row_step = sem("row_step")
        row_act = sem("row_act")
        max_step = sem("max_step")
        row_min = sem("row_min")
        z_ready = sem("z_ready")
        z_copied = sem("z_copied")
        z_masked = sem("z_masked")
        nabs_ready = sem("nabs_ready")
        e_ready = sem("e_ready")
        log_ready = sem("log_ready")
        sp_ready = sem("sp_ready")
        between_ready = sem("between_ready")
        logw_ready = sem("logw_ready")
        w_ready = sem("w_ready")
        y_ready = sem("y_ready")
        y_taken = sem("y_taken")
        conv_step = sem("conv_step")
        conv_silu = sem("conv_silu")
        u_turned = sem("u_turned")
        u_col_ready = sem("u_col_ready")
        mqk_ready = sem("mqk_ready")
        mb_ready = sem("mb_ready")
        dec_ready = sem("dec_ready")
        wqk_ready = sem("wqk_ready")
        num_ready = sem("num_ready")
        den_step = sem("den_step")
        floor_ready = sem("floor_ready")
        ml_out = sem("ml_out")
        mix_gated = sem("mix_gated")
        out_added = sem("out_added")
        q_peer_taken = sem("q_peer_taken")
        score_made = sem("score_made")
        score_ready = sem("score_ready")
        route = sem("route")
        gate_exp = sem("gate_exp")
        routed_t = sem("routed_t")
        routed_kept = sem("routed_kept")
        parts_ready = sem("parts_ready")
        hot2_ready = sem("hot2_ready")
        hot1_ready = sem("hot1_ready")
        hot1g_ready = sem("hot1g_ready")
        g_made = sem("g_made")
        g_kept = sem("g_kept")
        gelu_done = sem("gelu_done")
        act_gated = sem("act_gated")
        y_part = sem("y_part")
        y_added = sem("y_added")
        raw_taken = sem("raw_taken")
        rot_ready = sem("rot_ready")
        rope_step = sem("rope_step")
        v_taken = sem("v_taken")
        lam_step = sem("lam_step")
        lam_sum = sem("lam_sum")
        lam_exp = sem("lam_exp")
        meta_step = sem("meta_step")
        meta_pe = sem("meta_pe")
        meta_act = sem("meta_act")
        s_made = sem("s_made")
        max_ready = sem("max_ready")
        nmax_ready = sem("nmax_ready")
        p_ready = sem("p_ready")
        rec_step = sem("rec_step")
        a_ready = sem("a_ready")
        a_turned = sem("a_turned")
        aT_kept = sem("aT_kept")
        av_done = sem("av_done")
        o_taken = sem("o_taken")
        ffn_zero = sem("ffn_zero")
        a_taken = [sem(f"a_taken{k}") for k in range(2)]
        fconv_step = [sem(f"fconv_step{k}") for k in range(2)]
        fsilu_done = [sem(f"fsilu_done{k}") for k in range(2)]
        ffn_gated = [sem(f"ffn_gated{k}") for k in range(2)]
        ffn_added = [sem(f"ffn_added{k}") for k in range(2)]
        o_added = [sem(f"o_added{k}") for k in range(2)]
        lat_taken = sem("lat_taken")
        kr_step = sem("kr_step")
        kr_rot = sem("kr_rot")
        kr_copied = sem("kr_copied")
        kn_taken = sem("kn_taken")
        vm_taken = sem("vm_taken")
        qraw_taken = sem("qraw_taken")
        qrot_ready = sem("qrot_ready")
        qrope_step = sem("qrope_step")
        mm_step, mm_act = sem("mm_step"), sem("mm_act")
        head_made = sem("head_made")
        m_made, m_max, m_nmax, m_prob = sem("m_made"), sem("m_max"), sem("m_nmax"), sem("m_prob")
        m_rec, m_scaled, m_turned = sem("m_rec"), sem("m_scaled"), sem("m_turned")
        m_kept, m_av, m_taken = sem("m_kept"), sem("m_av"), sem("m_taken")
        stored = sem("stored")

        every = list(range(DC))
        Norm.squares = Norm.groups = 0
        n_in1 = Norm([every], SEQ)
        n_qk = Norm([[c] for c in range(8)], SEQ)
        n_ysb = Norm([[c] for c in range(4)], SEQ)
        n_yml = Norm([[c] for c in range(4)], SEQ)
        n_in2 = Norm([every], SEQ)
        n_diff = Norm([every], L)
        n_sub = Norm([[c] for c in range(8)], L)
        n_ffn0 = Norm([every], L)
        n_lat = Norm([every], L)
        n_ckv = Norm([[0, 1]], L)
        n_cq = Norm([[0, 1, 2]], L)
        n_ffn1 = Norm([every], L)
        n_fin = Norm([every], L)

        def pieces(T):
            return [(0, T)] if T <= BANK else [(0, HALF), (HALF, T)]

        def ms_psum(gi, T):
            return ps[:, 4 + gi % 2, 0:T] if T <= BANK else ps[:, 4 + 2 * (gi % 2):6 + 2 * (gi % 2), 0:HALF]

        def split(ap):
            return ap.rearrange("p (a b) -> p a b", b=HALF)

        def wait(eng, s, value):
            if not isinstance(value, int) or value > 0:
                eng.wait_ge(s, value)

        def turns(eng, n, body):
            body(0)
            if n == 2:
                body(1)
            elif n > 2:
                with eng.Fori(1, n) as i:
                    body(i)

        def at(t, k):
            return t[:, k, :] if isinstance(k, int) else t[:, bass.ds(k, 1), :].rearrange("p o n -> p (o n)")

        def norm_sums(pe, n, lhsT):
            k = n.q0
            for g, group in enumerate(n.chunks):
                gi = n.g0 + g
                wait(pe, ln_done, gi - 1)
                dst = ms_psum(gi, n.T)
                for j, _ in enumerate(group):
                    pe.wait_ge(sq_ready, k + 1)
                    src = (sq1 if n.T == SEQ else sq2)[:, k % 2, :]
                    for b, (lo, hi) in enumerate(pieces(n.T)):
                        last = pe.matmul(dst if n.T == SEQ else dst[:, b, :], lhsT, src[:, lo:hi],
                                         start=j == 0, stop=j == len(group) - 1)
                    last.then_inc(sq_summed, 1)
                    k += 1

        def norm_rstd(act, n, src, scale, eps, ready=None):
            at_q = [n.q0]

            def squares(g):
                for c in n.chunks[g]:
                    k = at_q[0]
                    wait(act, sq_summed, k - 1)
                    if ready is not None:
                        ready(c)
                    act.activation((sq1 if n.T == SEQ else sq2)[:, k % 2, :], src(c), ACT.Square).then_inc(sq_ready, 1)
                    at_q[0] += 1

            squares(0)
            summed = n.q0
            for g, group in enumerate(n.chunks):
                gi = n.g0 + g
                if g + 1 < len(n.chunks):
                    squares(g + 1)
                summed += len(group)
                act.wait_ge(sq_summed, summed)
                wait(act, normed, gi - 1)
                r = (rstd1 if n.T == SEQ else rstd2)[:, gi % 2, :]
                act.activation(r if n.T == SEQ else split(r), ms_psum(gi, n.T), ACT.Ln,
                               bias=col("eps", eps), scale=scale).then_inc(ln_done, 1)
                act.wait_ge(ln_done, gi + 1)
                act.activation(r, r, ACT.Exp, scale=-0.5).then_inc(rstd_ready, 1)

        def norm_apply(dve, n, src, gain, dst):
            for g, group in enumerate(n.chunks):
                gi = n.g0 + g
                dve.wait_ge(rstd_ready, gi + 1)
                r = (rstd1 if n.T == SEQ else rstd2)[:, gi % 2, :]
                for c in group:
                    last = dve.scalar_tensor_tensor(dst(c), src(c), gain(c), r, ALU.mult, ALU.mult)
                last.then_inc(normed, 1)

        def slot_wait(pe, turn, s):
            pe.wait_ge(slot_loaded[s], turn * 16 + 16)

        def slot(s):
            return ring[:, s, :]

        def used(turn, s):
            return turn * RING + (s + 1)

        block = ctx.enter_context(nc.Block())

        @block.sync
        def _(sp):
            for s in range(RING):
                sp.dma_start(ring[:, s, :], stream[s]).then_inc(slot_loaded[s], 16)
            with sp.Fori(1, TURNS) as i:
                for s in range(RING):
                    sp.wait_ge(slot_used, i * RING + (s + 1 - RING))
                    sp.dma_start(ring[:, s, :], stream[bass.ds(i * RING + s, 1), :, :]
                                 .rearrange("o p n -> (o p) n")).then_inc(slot_loaded[s], 16)

        @block.tensor
        def _(pe):
            def ada(name, m):
                t0 = TURN[name]
                for i in range(2):
                    for s in range(RING):
                        slot_wait(pe, t0 + i, s)
                        j = m * DC + RING * i + s
                        for c in range(DC):
                            last = pe.matmul(ps[:, 7, j:j + 1], slot(s)[:, c * P:(c + 1) * P], silu_c[:, c:c + 1],
                                             start=c == 0, stop=c == DC - 1)
                        last.then_inc(slot_used, 1)

            def tile1(turn, s, src, bank):
                slot_wait(pe, turn, s)
                for c in range(DC):
                    last = pe.matmul(ps[:, bank, :], slot(s)[:, c * P:(c + 1) * P], src[:, c, :],
                                     start=c == 0, stop=c == DC - 1)
                last.then_inc(slot_used, 1)

            pe.wait_ge(inputs_in, 5 * 16)
            norm_sums(pe, n_in1, ones)
            pe.wait_ge(silu_c_ready, 1)
            ada("ada_shift1", 0)
            ada("ada_scale1", 1)

            pe.wait_ge(shifted, DC)
            for k, rows in enumerate((0, 4)):
                for c in range(DC):
                    o = VEC["w_gates"] + 8 * c + rows
                    last = pe.matmul(ps[0:4, 4 + k, :], vec[:, o:o + 4], hf[:, c, :], start=c == 0, stop=c == DC - 1)
                last.then_inc(gates_ready, 1)
            tile = 0
            for name, n in (("qk_sb", 2), ("v_sb", 1), ("qk_ml", 2), ("v_ml", 1), ("o_ml", 1)):
                if name.startswith("v"):
                    pe.wait_ge(win_taken, tile)
                    for s in range(RING):
                        slot_wait(pe, TURN[name], s)
                        for b in range(TB):
                            for j in range(2):
                                c = 2 * s + j
                                last = pe.matmul(ps[:, b, :], hf[:, c, b * P:(b + 1) * P],
                                                 slot(s)[:, j * BANK:(j + 1) * BANK], start=c == 0, stop=c == DC - 1)
                        last.then_inc(slot_used, 1)
                    tile += TB
                else:
                    for i in range(n):
                        for s in range(RING):
                            wait(pe, win_taken, tile - 3)
                            tile1(TURN[name] + i, s, hf, s)
                            tile += 1

            pe.wait_ge(gates_taken, 2)
            norm_sums(pe, n_qk, ones64)

            pe.wait_ge(normed, n_qk.done)
            pe.wait_ge(win_taken, 28)

            def causal(bank0, s):
                o = (0, 512, 1024, 896)[s]
                return ps[:, bank0 + o // BANK, o % BANK:o % BANK + SEQ - s * P]

            def sb_scores(h):
                rows = slice(64 * (h % 2), 64 * (h % 2) + 64)
                wait(pe, z_copied, h)
                for s in range(TB):
                    last = pe.matmul(causal(0, s), qk[rows, 4 + h // 2, s * P:(s + 1) * P],
                                     qk[rows, h // 2, s * P:SEQ], start=True, stop=True)
                last.then_inc(z_ready, 1)

            def sb_between(h):
                pe.wait_ge(sp_ready, h + 1)
                wait(pe, logw_ready, h)
                for s in range(TB):
                    out = causal(3, s)
                    for j in range(s, TB):
                        o = (0, 512, 1024, 896)[j]
                        last = pe.matmul(out[:, (j - s) * P:], cst("tri") if j == s else cst("neg_ones"),
                                         sp_buf[:, h % 2, o:o + SEQ - j * P], start=j == s, stop=j == TB - 1)
                last.then_inc(between_ready, 1)

            def sb_out(h):
                rows = slice(64 * (h % 2), 64 * (h % 2) + 64)
                pe.wait_ge(w_ready, h + 1)
                if h % 2 == 0:
                    wait(pe, y_taken, h // 2)
                for s in range(TB):
                    o = (0, 512, 1024, 896)[s]
                    last = pe.matmul(ps[rows, 6, s * P:SEQ], v_sb[:, s, h * SB_DIM:(h + 1) * SB_DIM],
                                     w_buf[:, h % 2, o:o + SEQ - s * P], start=s == 0, stop=s == TB - 1)
                last.then_inc(y_ready, 1)

            sb_scores(0)
            sb_scores(1)
            for h in range(SB_HEADS):
                sb_between(h)
                if h:
                    sb_out(h - 1)
                if h + 2 < SB_HEADS:
                    sb_scores(h + 2)
                if h % 2 == 0:
                    ada(("ada_gate1", "ada_shift2", "ada_scale2", "ada_gate2")[h // 2], 2 + h // 2)
            sb_out(SB_HEADS - 1)
            norm_sums(pe, n_ysb, ones64)
            pe.wait_ge(ln_done, n_ysb.done)

            pe.wait_ge(max_step, MAX_STEPS)
            for b in range(TB):
                last = pe.transpose(ps[:, 6, 4 * b:4 * b + 4], n_row[:, b * P:(b + 1) * P], ident[0:4, 0:4])
            last.then_inc(u_turned, 1)
            pe.wait_ge(conv_silu, 8)
            for h in range(ML_HEADS):
                wait(pe, wqk_ready, h)
                for s in range(TB):
                    last = pe.matmul(causal(0, s), conv[:, 4 + h, s * P:(s + 1) * P], conv[:, h, s * P:SEQ],
                                     start=True, stop=True)
                last.then_inc(mqk_ready, 1)
                wait(pe, floor_ready, h)
                wait(pe, dec_ready, 4 * h)
                for s in range(TB):
                    out = causal(3, s)
                    pe.matmul(out, cst("pick_head", ML_HEADS * P, 4)[:, h * P:(h + 1) * P],
                              m_pad[1][:, SEQ + s * P:2 * SEQ], start=True, stop=False)
                    last = pe.matmul(out[:, 0:P], ident, cst("late"), start=False, stop=True)
                last.then_inc(mb_ready, 1)
                pe.wait_ge(wqk_ready, h + 1)
                if h == 0:
                    pe.wait_ge(row_act, 3)
                    pe.wait_ge(u_col_ready, 1)
                    pe.wait_ge(mod_ready, 5)
                wait(pe, ml_out, h)
                for bank, lhs in ((6, None), (7, ones)):
                    for s in range(TB):
                        o = (0, 512, 1024, 896)[s]
                        lhsT = v_ml[:, s, h * P:(h + 1) * P] if lhs is None else lhs
                        last = pe.matmul(ps[:, bank, s * P:SEQ], lhsT, w_buf[:, h % 2, o:o + SEQ - s * P],
                                         start=s == 0, stop=s == TB - 1)
                last.then_inc(num_ready, 1)
                pe.wait_ge(dec_ready, 4 * (h + 1))
                pe.matmul(ps[:, 3, :], cst("pick_head", ML_HEADS * P, 4)[:, h * P:(h + 1) * P], e_row,
                          start=True, stop=True).then_inc(num_ready, 1)
            norm_sums(pe, n_yml, ones)

            pe.wait_ge(mix_gated, 4)
            pe.wait_ge(normed, n_ysb.done)
            pe.wait_ge(wqk_ready, ML_HEADS)
            pe.wait_ge(floor_ready, ML_HEADS)
            for t in range(DC):
                wait(pe, out_added, t - 3)
                tile1(TURN["w_out"] + t // 4, t % 4, mixed, t % 4)

            norm_sums(pe, n_in2, ones)
            pe.wait_ge(shifted, 2 * DC)
            pe.wait_ge(out_added, DC)

            def q_tiles(i):
                for s in range(RING):
                    t = RING * i + s
                    wait(pe, q_peer_taken, t - 3)
                    tile1(TURN["peer_q"] + i, s, hf, s)
            turns(pe, 4, q_tiles)
            pe.wait_ge(q_peer_taken, QH)
            pe.wait_ge(keys_in, 16)

            def peer_scores(b):
                wait(pe, score_ready, b)
                for j in range(QH):
                    last = pe.matmul(ps[:, j // 4, (j % 4) * P:(j % 4 + 1) * P], q_peer[:, j, b * P:(b + 1) * P],
                                     keys[:, j, :], start=True, stop=True)
                last.then_inc(score_made, 1)

            peer_scores(0)
            for b in range(TB):
                if b + 1 < TB:
                    peer_scores(b + 1)
                pe.wait_ge(route, ROUTE * (b + 1))
                wait(pe, routed_kept, 3 * b)
                for k in range(3):
                    last = pe.transpose(ps[:, 6, k * P:(k + 1) * P], routed[:, k, :], ident)
                last.then_inc(routed_t, 1)
            pe.wait_ge(routed_kept, 3 * TB)
            pe.wait_ge(score_ready, TB)

            def g_batch(n, k):
                pe.wait_ge(hot2_ready, n + 1)
                pe.wait_ge(hot1g_ready, n + 1)
                wait(pe, g_kept, n + -1)
                for t in range(8):
                    for part in range(3):
                        last = pe.matmul(ps[:, 6 + k, t * 32:(t + 1) * 32], hot2[:, k, t, :],
                                         hot1g[:, k, t, part * 32:(part + 1) * 32], start=part == 0, stop=part == 2)
                last.then_inc(g_made, 1)

            def g_two(i):
                for k in range(2):
                    g_batch(i * 2 + k, k)
            turns(pe, 32, g_two)
            for quarter in range(4):
                def experts(i, quarter=quarter):
                    group = i + 16 * quarter
                    turn = group + TURN["experts"]
                    for e in range(2):
                        wait(pe, gelu_done, group * 2 + (e - 1))
                        slot_wait(pe, turn, e)
                        for c in range(DC):
                            last = pe.matmul(ps[:, e, :], slot(e)[:, c * P:(c + 1) * P], hf[:, c, :],
                                             start=c == 0, stop=c == DC - 1)
                        last.then_inc(slot_used, 1)
                    if quarter < 3:
                        for k in range(4):
                            g_batch(i * 4 + (64 * (quarter + 1) + k), k % 2)
                    pe.wait_ge(act_gated, group * 2 + 2)
                    slot_wait(pe, turn, 2)
                    slot_wait(pe, turn, 3)
                    for d in range(DC):
                        wait(pe, y_added, group * DC + (d - 3))
                        a = pe.matmul(ps[:, 2 + d % 4, :], slot(2)[:, d * P:(d + 1) * P], act_e[:, 0, :],
                                      start=True, stop=False)
                        b = pe.matmul(ps[:, 2 + d % 4, :], slot(3)[:, d * P:(d + 1) * P], act_e[:, 1, :],
                                      start=False, stop=True)
                        if d < DC - 1:
                            b.then_inc(y_part, 1)
                        else:
                            a.then_inc(slot_used, 1)
                            b.then_inc(slot_used, 1)
                if quarter == 0:
                    turns(pe, 16, experts)
                else:
                    with pe.Fori(0, 16) as i:
                        experts(i)

            def tile2(turn, s, src, pair, chunks=DC, at0=0, step=P, M=P):
                for c in range(chunks):
                    for b, (lo, hi) in enumerate(pieces(L)):
                        dst = ps[0:M, 2 * pair + b, 0:HALF]
                        o = at0 + c * step
                        last = pe.matmul(dst, slot(s)[:, o:o + M], src[:, c, lo:hi], start=c == 0, stop=c == chunks - 1)
                return last

            def rot(src, pair, rows=P, name="swap_d"):
                for b, (lo, hi) in enumerate(pieces(L)):
                    last = pe.matmul(ps[0:rows, 2 * pair + b, 0:HALF], tab(name, rows, rows), src[0:rows, lo:hi],
                                     start=True, stop=True)
                return last

            pe.wait_ge(y_added, 64 * DC)
            norm_sums(pe, n_diff, ones)
            pe.wait_ge(normed, n_diff.done)
            pe.wait_ge(tables_in, 16)

            def qk_tiles(i):
                for s in range(RING):
                    t = RING * i + s
                    wait(pe, raw_taken, t + -1)
                    slot_wait(pe, TURN["qk_diff"] + i, s)
                    tile2(TURN["qk_diff"] + i, s, hT, s % 2).then_inc(slot_used, 1)
                    if s or not isinstance(i, int) or i:
                        pe.wait_ge(raw_taken, t)
                        wait(pe, rope_step, t * 3 + -6)
                        rot(raw_d[:, (s + 1) % 2, :], 2 + (s + 1) % 2).then_inc(rot_ready, 1)
            turns(pe, 4, qk_tiles)
            pe.wait_ge(raw_taken, 16)
            pe.wait_ge(rope_step, 3 * 14)
            rot(raw_d[:, 1, :], 3).then_inc(rot_ready, 1)

            def token_major(turn, src, per_slot, taken, base, first_slot, chunks):
                wait(pe, taken, base)
                n = chunks // per_slot
                for k in range(n):
                    s = (first_slot + k) % RING
                    slot_wait(pe, turn + (first_slot + k) // RING, s)
                    for b in range(5):
                        lo, hi = (0, META) if b == 0 else (META + (b - 1) * P, META + b * P)
                        for j in range(per_slot):
                            c = per_slot * k + j
                            last = pe.matmul(ps[0:hi - lo, b, :], src[:, c, lo:hi], slot(s)[:, j * BANK:(j + 1) * BANK],
                                             start=c == 0, stop=c == chunks - 1)
                    last.then_inc(slot_used, 1)

            pe.wait_ge(rope_step, 48)
            for half in range(2):
                token_major(TURN["v_diff"] + half, hT, 2, v_taken, 5 * half, 0, DC)

            pe.wait_ge(lam_step, 1)
            pe.matmul(ps[:, 5, 0:2], ones, lam_p, start=True, stop=True).then_inc(lam_sum, 1)
            pe.wait_ge(v_taken, 10)
            for m in range(16):
                r = slice(64 * (m % 2), 64 * (m % 2) + 64)
                last = pe.matmul(ps[0:META, 6 + m % 2, 16 * (m // 2):16 * (m // 2) + META], qk_d[r, m // 2, 0:META],
                                 qk_d[r, 8 + m // 2, 0:META], start=True, stop=True)
            last.then_inc(meta_pe, 1)
            pe.wait_ge(meta_step, 7)
            pe.wait_ge(lam_exp, 1)
            for h in range(8):
                last = pe.transpose(ps[0:META, 5, 16 * h:16 * h + 16], pm[0:META, h, :], ident[0:META, 0:META])
            last.then_inc(meta_pe, 1)
            pe.wait_ge(meta_act, 2)
            for h in range(8):
                last = pe.matmul(ps[:, 7, 16 * h:16 * h + 16], v_d[0:META, 0, h * P:(h + 1) * P], amT[0:META, h, :],
                                 start=True, stop=True)
            last.then_inc(meta_pe, 1)

            def scores(out0, lhsT, rhs, b):
                W = META + (b + 1) * P
                if W <= BANK:
                    pe.matmul(ps[:, out0, 0:W], lhsT, rhs[:, 0:W], start=True, stop=False)
                    m = ps[:, out0, W - CHUNK:W]
                else:
                    pe.matmul(ps[:, out0, 0:HALF], lhsT, rhs[:, 0:HALF], start=True, stop=True)
                    pe.matmul(ps[:, out0 + 1, 0:HALF], lhsT, rhs[:, HALF:L], start=True, stop=False)
                    m = ps[:, out0 + 1, HALF - CHUNK:HALF]
                return pe.matmul(m, cst("first_half", P, 1), cst("lowest", CHUNK, 1), start=False, stop=True)

            def turn_probs(a, b):
                for k in range(b + 1):
                    pe.transpose(ps[:, 4, k * P:(k + 1) * P], a[:, META + k * P:META + (k + 1) * P], ident)
                return pe.transpose(ps[0:META, 5, 0:P], a[:, 0:META], ident)

            units = [(h, b) for h in range(DIFF_HEADS) for b in range(TB)]

            def d_scores(u):
                h, b = units[u]
                for m in range(2):
                    wait(pe, p_ready, 2 * (u - 1) + m + 1)
                    r = slice(64 * m, 64 * m + 64)
                    scores(2 * m, qk_d[r, h, META + b * P:META + (b + 1) * P], qk_d[r, 8 + h, :], b).then_inc(s_made, 1)

            def d_turn(u):
                pe.wait_ge(a_ready, u + 1)
                wait(pe, aT_kept, 2 * u)
                turn_probs(prob[:, u % 2, 0, :], units[u][1]).then_inc(a_turned, 1)

            def d_out(u):
                h, b = units[u]
                pe.wait_ge(aT_kept, 2 * u + 2)
                if b == 0:
                    wait(pe, o_taken, h)
                out = ps[:, 6, b * P:(b + 1) * P]
                pe.matmul(out, v_d[0:META, 0, h * P:(h + 1) * P], aT[0:META, u % 2, 0, :], start=True, stop=False)
                for k in range(1, b + 2):
                    last = pe.matmul(out, v_d[:, k, h * P:(h + 1) * P], aT[:, u % 2, k, :], start=False, stop=k == b + 1)
                last.then_inc(av_done, 1)

            pe.wait_ge(meta_act, 3)
            n = len(units)
            d_scores(0)
            for u in range(n + 2):
                if 1 <= u <= n:
                    d_turn(u - 1)
                if u >= 2:
                    d_out(u - 2)
                if u + 1 < n:
                    d_scores(u + 1)
            norm_sums(pe, n_sub, ones)

            def out_tiles(name, src, k):
                for t in range(DC):
                    wait(pe, o_added[k], t - 1)
                    slot_wait(pe, TURN[name] + t // 4, t % 4)
                    tile2(TURN[name] + t // 4, t % 4, src, t % 2).then_inc(slot_used, 1)

            pe.wait_ge(normed, n_sub.done)
            out_tiles("o_diff", o_d, 0)

            def ffn(k, n):
                norm_sums(pe, n, ones)
                pe.wait_ge(normed, n.done)

                def up(i):
                    turn = i + TURN[f"ffn_in{k}"]
                    for e in range(2):
                        wait(pe, a_taken[k], i * 2 + (e - 1))
                        slot_wait(pe, turn, 2 * e)
                        tile2(turn, 2 * e, hT, 2 * e).then_inc(slot_used, 1)
                        wait(pe, ffn_gated[k], i * 2 + (e - 1))
                        slot_wait(pe, turn, 2 * e + 1)
                        tile2(turn, 2 * e + 1, hT, 2 * e + 1).then_inc(slot_used, 1)
                turns(pe, FC // 2, up)
                pe.wait_ge(ffn_gated[k], FC)

                def down(i):
                    for t in range(4):
                        wait(pe, ffn_added[k], i * 4 + (t - 3))
                        for q in range(3):
                            s = 3 * t + q
                            slot_wait(pe, i * 3 + (TURN[f"ffn_out{k}"] + s // RING), s % RING)
                            for c in range(8):
                                f = 8 * q + c
                                if f >= FC:
                                    continue
                                for b, (lo, hi) in enumerate(pieces(L)):
                                    last = pe.matmul(ps[:, 2 * t + b, 0:HALF], slot(s % RING)[:, c * P:(c + 1) * P],
                                                     gated[:, f, lo:hi], start=f == 0, stop=f == FC - 1)
                            last.then_inc(slot_used, 1)
                turns(pe, 2, down)

            pe.wait_ge(o_added[0], DC)
            ffn(0, n_ffn0)

            pe.wait_ge(ffn_added[0], DC)
            norm_sums(pe, n_lat, ones)
            pe.wait_ge(normed, n_lat.done)
            turn = TURN["mla"]

            def mla_slot(k):
                slot_wait(pe, turn + k // RING, k % RING)
                return k % RING

            for k in range(3):
                s = mla_slot(k)
                tile2(turn, s, h_kv, k, M=P if k < 2 else QK_MLA).then_inc(slot_used, 1)
            for k in range(QC):
                s = mla_slot(3 + k)
                wait(pe, lat_taken, k)
                tile2(turn, s, hT, (3 + k) % 4).then_inc(slot_used, 1)
            pe.wait_ge(lat_taken, 6)
            rot(kr_raw, 0, QK_MLA, "swap_m").then_inc(kr_rot, 1)
            norm_sums(pe, n_ckv, ones)
            norm_sums(pe, n_cq, ones)
            pe.wait_ge(normed, n_ckv.done)
            pe.wait_ge(kr_step, 3)
            for h in range(MLA_HEADS):
                if h % 8 == 0:
                    s = mla_slot(6 + h // 8)
                wait(pe, kn_taken, h - 1)
                last = tile2(turn, s, ckv, h % 2, KVC, (h % 8) * P, NOPE, NOPE)
                last.then_inc(slot_used if h % 8 == 7 else head_made, 1)
            pe.wait_ge(kn_taken, MLA_HEADS)
            pe.wait_ge(normed, n_cq.done)
            for half in range(2):
                token_major(turn, ckv, 2, vm_taken, 5 * half, 8 + half, KVC)
            pe.wait_ge(vm_taken, 10)
            for h in range(MLA_HEADS + 1):
                if h < MLA_HEADS:
                    if h % 3 == 0:
                        s = mla_slot(10 + h // 3)
                    wait(pe, qraw_taken, h - 1)
                    last = tile2(turn, s, cqn, h % 2, QC, (h % 3) * 3 * QK_MLA, QK_MLA, QK_MLA)
                    last.then_inc(slot_used if h % 3 == 2 or h == MLA_HEADS - 1 else head_made, 1)
                if h:
                    pe.wait_ge(qraw_taken, h)
                    wait(pe, qrope_step, 3 * (h - 2))
                    rot(raw_m[:, (h - 1) % 2, :], 2 + (h - 1) % 2, QK_MLA, "swap_m").then_inc(qrot_ready, 1)

            pe.wait_ge(qrope_step, 3 * MLA_HEADS)
            pe.wait_ge(kr_copied, MLA_HEADS)
            for h in range(MLA_HEADS):
                last = pe.matmul(ps[0:META, 7, 16 * h:16 * h + 16], q_m[0:QK_MLA, h, 0:META], k_m[0:QK_MLA, h, 0:META],
                                 start=True, stop=True)
            last.then_inc(m_made, 1)
            pe.wait_ge(mm_step, 5)
            for h in range(MLA_HEADS):
                last = pe.transpose(ps[0:META, 5, 16 * h:16 * h + 16], pmm[0:META, h, :], ident[0:META, 0:META])
            last.then_inc(m_turned, 1)
            pe.wait_ge(mm_act, 2)
            for h in range(MLA_HEADS):
                last = pe.matmul(ps[64 * (h % 2):64 * (h % 2) + 64, 6, 16 * (h // 2):16 * (h // 2) + 16],
                                 v_m[0:META, 0, h * MLA_V:(h + 1) * MLA_V], amTm[0:META, h, :], start=True, stop=True)
            last.then_inc(m_av, 1)

            units = [(h, b) for h in range(MLA_HEADS) for b in range(TB)]
            n = len(units)

            def m_scores(u):
                h, b = units[u]
                wait(pe, m_prob, u - 1)
                scores(2 * (u % 2), q_m[0:QK_MLA, h, META + b * P:META + (b + 1) * P], k_m[0:QK_MLA, h, :], b)\
                    .then_inc(m_made, 1)

            def m_turn(u):
                pe.wait_ge(m_scaled, u + 1)
                wait(pe, m_kept, 2 * u)
                turn_probs(probm[:, u % 2, :], units[u][1]).then_inc(m_turned, 1)

            def m_out(u):
                h, b = units[u]
                pe.wait_ge(m_kept, 2 * u + 2)
                if b == 0 and h % 2 == 0:
                    wait(pe, m_taken, h // 2 - 1)
                r = slice(64 * (h % 2), 64 * (h % 2) + 64)
                out = ps[r, 6 + (h // 2) % 2, b * P:(b + 1) * P]
                v = slice(h * MLA_V, (h + 1) * MLA_V)
                pe.matmul(out, v_m[0:META, 0, v], aTm[0:META, u % 2, 0, :], start=True, stop=False)
                for k in range(1, b + 2):
                    last = pe.matmul(out, v_m[:, k, v], aTm[:, u % 2, k, :], start=False, stop=k == b + 1)
                last.then_inc(m_av, 1)

            pe.wait_ge(mm_act, 3)
            m_scores(0)
            for u in range(n + 2):
                if 1 <= u <= n:
                    m_turn(u - 1)
                if u >= 2:
                    m_out(u - 2)
                if u + 1 < n:
                    m_scores(u + 1)
            pe.wait_ge(m_taken, 8)
            out_tiles("o_mla", o_m, 1)
            pe.wait_ge(o_added[1], DC)
            ffn(1, n_ffn1)
            pe.wait_ge(ffn_added[1], DC)
            norm_sums(pe, n_fin, ones)

        @block.scalar
        def _(act):
            act.dma_start(vec[:, :], vecs_d).then_inc(inputs_in, 16)
            act.dma_start(const[:, :], consts_d).then_inc(inputs_in, 16)
            act.dma_start(x[:, 0:4, META:L], x_d[:, 0:4, :]).then_inc(inputs_in, 16)
            act.dma_start(x[:, 4:8, META:L], x_d[:, 4:8, :]).then_inc(inputs_in, 16)
            act.dma_start(x[:, :, 0:META], meta_d).then_inc(inputs_in, 16)
            act.wait_ge(inputs_in, 5 * 16)
            act.activation(silu_c[:, :], vec[:, VEC["c"]:VEC["c"] + DC], ACT.Silu).then_inc(silu_c_ready, 1)
            norm_rstd(act, n_in1, lambda c: xf[:, c, :], 1.0 / D, 0)
            act.wait_ge(normed, n_in1.done)
            act.wait_ge(mod_ready, 1)
            for c in range(DC):
                act.activation(hf[:, c, :], hf[:, c, :], ACT.Identity, bias=mod[:, c:c + 1]).then_inc(shifted, 1)

            act.wait_ge(gates_ready, 1)
            act.activation(i_row, ps[0:4, 4, :], ACT.Identity, bias=col("b_igate", 0, 4)).then_inc(gates_taken, 1)
            act.wait_ge(gates_ready, 2)
            act.activation(f_row, ps[0:4, 5, :], ACT.Identity, bias=col("b_fgate", 0, 4)).then_inc(gates_taken, 1)
            for name, n in (("qk_sb", 8), ("v_sb", 4), ("qk_ml", 8), ("v_ml", 4), ("o_ml", 4)):
                if name == "qk_ml":
                    act.wait_ge(pads_zeroed, 5)
                    act.wait_ge(row_min, 2)
                    act.activation(e_row, e_row, ACT.Exp).then_inc(row_act, 1)
                    act.wait_ge(row_act, 1)
                    act.activation(e_row, e_row, ACT.Ln, bias=1.0).then_inc(row_act, 1)
                for t in range(n):
                    done = used(TURN[name], 3 if name.startswith("v") else t)
                    act.wait_ge(slot_used, done)
                    src = ps[:, t % 4, :]
                    if name == "o_ml":
                        act.activation(sig_o[:, t, :], src, ACT.Sigmoid).then_inc(win_taken, 1)
                    else:
                        dst = {"qk_sb": qk, "v_sb": v_sb, "v_ml": v_ml}.get(name)
                        dst = conv_in[:, t, CONV1 - 1:] if dst is None else dst[:, t, :]
                        act.activation(dst, src, ACT.Copy).then_inc(win_taken, 1)
            act.wait_ge(win_taken, 8)
            norm_rstd(act, n_qk, lambda c: qk[:, c, :], 1.0 / SB_DIM, 0)

            def sb_copy(h):
                act.wait_ge(z_ready, h + 1)
                wait(act, logw_ready, h - 1)
                act.activation(z_buf[:, h % 2, :], ps[:, 0:3, :].rearrange("p a b -> p (a b)")[:, 0:1280], ACT.Copy,
                               scale=SB_DIM ** -0.5).then_inc(z_copied, 1)

            def sb_weights(h):
                act.wait_ge(logw_ready, h + 1)
                act.activation(w_buf[:, h % 2, :], w_buf[:, h % 2, :], ACT.Exp).then_inc(w_ready, 1)

            sb_copy(0)
            for h in range(SB_HEADS):
                act.wait_ge(nabs_ready, h + 1)
                act.activation(sp_buf[:, h % 2, :], sp_buf[:, h % 2, :], ACT.Exp).then_inc(e_ready, 1)
                act.wait_ge(e_ready, h + 1)
                act.activation(sp_buf[:, h % 2, :], sp_buf[:, h % 2, :], ACT.Ln, bias=1.0).then_inc(log_ready, 1)
                if h + 1 < SB_HEADS:
                    sb_copy(h + 1)
                if h:
                    sb_weights(h - 1)
            sb_weights(SB_HEADS - 1)
            for c in range(8):
                act.wait_ge(conv_step, 4 * (c + 1))
                act.activation(conv[:, c, :], conv[:, c, :], ACT.Silu).then_inc(conv_silu, 1)
            norm_rstd(act, n_ysb, lambda c: mixed[:, c, :], 1.0 / SB_DIM, 0, lambda c: act.wait_ge(y_taken, c + 1))

            act.wait_ge(max_step, MAX_STEPS)
            act.activation(e_row, e_row, ACT.Exp, scale=-1.0).then_inc(row_act, 1)
            act.wait_ge(u_col_ready, 1)
            for h in range(ML_HEADS):
                act.wait_ge(mb_ready, h + 1)
                wait(act, wqk_ready, h - 1)
                for s in range(TB):
                    o = (0, 512, 1024, 896)[s]
                    act.activation(z_buf[:, h % 2, o:o + SEQ - s * P],
                                   ps[:, 3 + o // BANK, o % BANK:o % BANK + SEQ - s * P], ACT.Exp,
                                   bias=u_col[:, s, h:h + 1], scale=-1.0).then_inc(dec_ready, 1)
                act.wait_ge(num_ready, 2 * h + 2)
                wait(act, ml_out, h - 1)
                act.activation(den_floor[:, h % 2, :], ps[:, 3, :], ACT.Copy).then_inc(floor_ready, 1)
            norm_rstd(act, n_yml, lambda c: mixed[:, 4 + c, :], 1.0 / ML_DIM, 0, lambda c: act.wait_ge(ml_out, c + 1))

            act.wait_ge(num_ready, 2 * ML_HEADS)
            act.wait_ge(row_act, 3)
            act.dma_start(keys, keys_d).then_inc(keys_in, 16)
            norm_rstd(act, n_in2, lambda c: xf[:, c, :], 1.0 / D, 0, lambda c: act.wait_ge(out_added, c + 1))
            act.wait_ge(normed, n_in2.done)
            act.wait_ge(mod_ready, 5)
            for c in range(DC):
                act.activation(hf[:, c, :], hf[:, c, :], ACT.Identity, bias=mod[:, 3 * DC + c:3 * DC + c + 1])\
                    .then_inc(shifted, 1)

            def q_copy(i):
                for s in range(RING):
                    act.wait_ge(slot_used, used(TURN["peer_q"] + i, s))
                    act.activation(at(q_peer, RING * i + s), ps[:, s, :], ACT.Copy).then_inc(q_peer_taken, 1)
            turns(act, 4, q_copy)
            for b in range(TB):
                act.wait_ge(score_made, b + 1)
                wait(act, route, ROUTE * (b - 1) + 5)
                act.activation(score.rearrange("p a b -> p (a b)"), ps[:, 0:4, :].rearrange("p a b -> p (a b)"),
                               ACT.Copy).then_inc(score_ready, 1)
                act.wait_ge(route, ROUTE * b + 14)
                act.activation(best, best, ACT.Exp).then_inc(gate_exp, 1)

            def g_copy(n, k, quarter, t0):
                act.wait_ge(g_made, n + 1)
                dst = G[quarter % 2][:, :, t0] if isinstance(t0, slice) else G[quarter % 2][:, :, bass.ds(t0, 8)]
                act.activation(dst, ps[:, 6 + k, 0:256].rearrange("p (t i) -> p i t", i=32), ACT.Copy).then_inc(g_kept, 1)

            def g_two(i):
                for k in range(2):
                    t0 = slice(8 * k, 8 * k + 8) if isinstance(i, int) and i == 0 else i * 16 + 8 * k
                    g_copy(i * 2 + k, k, 0, t0)
            turns(act, 32, g_two)
            for quarter in range(4):
                def experts(i, quarter=quarter):
                    group = i + 16 * quarter
                    for e in range(2):
                        act.wait_ge(slot_used, used(group + TURN["experts"], e))
                        act.activation(act_e[:, e, :], ps[:, e, :], ACT.Gelu).then_inc(gelu_done, 1)
                    if quarter < 3:
                        for k in range(4):
                            t0 = slice(8 * k, 8 * k + 8) if isinstance(i, int) else i * 32 + 8 * k
                            g_copy(i * 4 + (64 * (quarter + 1) + k), k % 2, quarter + 1, t0)
                wait(act, act_gated, 32 * quarter)
                if quarter == 0:
                    turns(act, 16, experts)
                else:
                    with act.Fori(0, 16) as i:
                        experts(i)

            act.wait_ge(y_added, 64 * DC)
            act.dma_start(table, tables_d).then_inc(tables_in, 16)
            norm_rstd(act, n_diff, lambda c: x[:, c, :], 1.0 / D, 1)

            def pair(k, rows=P):
                return ps[0:rows, 2 * k:2 * k + 2, 0:HALF]

            def qk_copy(i):
                for s in range(RING):
                    t = RING * i + s
                    act.wait_ge(slot_used, used(TURN["qk_diff"] + i, s))
                    wait(act, rope_step, t * 3 + -3)
                    act.activation(split(raw_d[:, s % 2, :]), pair(s % 2), ACT.Copy).then_inc(raw_taken, 1)
            turns(act, 4, qk_copy)

            def v_copy(dst, half, done, taken):
                act.wait_ge(slot_used, done)
                for b in range(5):
                    r = META if b == 0 else P
                    act.activation(dst[0:r, b, half * BANK:(half + 1) * BANK], ps[0:r, b, :], ACT.Copy).then_inc(taken, 1)

            for half in range(2):
                v_copy(v_d, half, used(TURN["v_diff"] + half, 3), v_taken)
            act.wait_ge(lam_sum, 1)
            act.activation(lam_e, ps[:, 5, 0:2], ACT.Exp).then_inc(lam_exp, 1)
            act.wait_ge(meta_step, 2)
            act.activation(pm[0:META, :, :], pm[0:META, :, :], ACT.Exp, scale=DIFF_DIM ** -0.5).then_inc(meta_act, 1)
            act.wait_ge(meta_pe, 2)
            act.activation(amT[0:META, 0:8, :], ps[0:META, 5, 0:P].rearrange("p (a b) -> p a b", b=META), ACT.Copy)\
                .then_inc(meta_act, 1)
            act.wait_ge(meta_pe, 3)
            act.activation(o_d[:, :, 0:META], ps[:, 7, 0:P].rearrange("p (a b) -> p a b", b=META), ACT.Copy)\
                .then_inc(meta_act, 1)

            def seen(k, b):
                W = META + (b + 1) * P
                return ps[:, k, 0:W] if W <= BANK else ps[:, k:k + 2, 0:HALF]

            def keep(dst, u, b, kept):
                act.activation(dst[:, u % 2, 1:b + 2, :], ps[:, 4, 0:(b + 1) * P].rearrange("p (a b) -> p a b", b=P),
                               ACT.Copy).then_inc(kept, 1)
                act.activation(dst[0:META, u % 2, 0, :], ps[0:META, 5, 0:P], ACT.Copy).then_inc(kept, 1)

            units = [(h, b) for h in range(DIFF_HEADS) for b in range(TB)]
            n = len(units)
            for u in range(n + 2):
                if u < n:
                    h, b = units[u]
                    wait(act, a_turned, u - 1)
                    for m in range(2):
                        act.wait_ge(nmax_ready, 2 * u + m + 1)
                        dst = prob[:, u % 2, m, 0:META + (b + 1) * P]
                        act.activation(dst if b < TB - 1 else split(dst), seen(2 * m, b), ACT.Exp,
                                       bias=st_nmax[:, u % 2, m:m + 1], scale=DIFF_DIM ** -0.5,
                                       accum_out=st_sum[:, u % 2, m:m + 1]).then_inc(p_ready, 1)
                if 1 <= u <= n:
                    act.wait_ge(a_turned, u)
                    wait(act, av_done, u - 2)
                    keep(aT, u - 1, units[u - 1][1], aT_kept)
                if u >= 2 and units[u - 2][1] == TB - 1:
                    h = units[u - 2][0]
                    act.wait_ge(av_done, u - 1)
                    act.activation(o_d[:, h, META:L], ps[:, 6, :], ACT.Copy).then_inc(o_taken, 1)
            norm_rstd(act, n_sub, lambda c: o_d[:, c, :], 1.0 / DIFF_V, 1, lambda c: act.wait_ge(o_taken, c + 1))

            def ffn(k, n, ready):
                norm_rstd(act, n, lambda c: x[:, c, :], 1.0 / D, 1, ready)
                act.wait_ge(ffn_zero, k + 1)

                def up(i):
                    for e in range(2):
                        act.wait_ge(slot_used, used(i + TURN[f"ffn_in{k}"], 2 * e))
                        wait(act, fconv_step[k], i * 6 + (3 * e - 3))
                        act.activation(split(a_pad[:, e, CONV2 - 1:]), pair(2 * e), ACT.Copy).then_inc(a_taken[k], 1)
                        act.wait_ge(fconv_step[k], i * 6 + (3 * e + 3))
                        act.activation(u_ffn[:, e, :], u_ffn[:, e, :], ACT.Silu).then_inc(fsilu_done[k], 1)
                turns(act, FC // 2, up)

            ffn(0, n_ffn0, lambda c: act.wait_ge(o_added[0], c + 1))

            norm_rstd(act, n_lat, lambda c: x[:, c, :], 1.0 / D, 1, lambda c: act.wait_ge(ffn_added[0], c + 1))
            t0 = TURN["mla"]
            for k in range(6):
                act.wait_ge(slot_used, used(t0, k))
                dst = ckv_raw[:, k, :] if k < 2 else kr_raw[0:QK_MLA, :] if k == 2 else cq_raw[:, k - 3, :]
                act.activation(split(dst), pair(k % 4, QK_MLA if k == 2 else P), ACT.Copy).then_inc(lat_taken, 1)
            act.wait_ge(lat_taken, 6)
            norm_rstd(act, n_ckv, lambda c: ckv_raw[:, c, :], 1.0 / KV_LORA, 1)
            norm_rstd(act, n_cq, lambda c: cq_raw[:, c, :], 1.0 / Q_LORA, 1)
            made = 0
            for h in range(MLA_HEADS):
                if h % 8 == 7:
                    act.wait_ge(slot_used, used(t0, 6 + h // 8))
                else:
                    made += 1
                    act.wait_ge(head_made, made)
                act.activation(split(k_m[0:NOPE, h, :]), pair(h % 2, NOPE), ACT.Copy).then_inc(kn_taken, 1)
            for half in range(2):
                v_copy(v_m, half, used(t0, 8 + half), vm_taken)
            for h in range(MLA_HEADS):
                if h % 3 == 2 or h == MLA_HEADS - 1:
                    act.wait_ge(slot_used, used(t0, 10 + h // 3))
                else:
                    made += 1
                    act.wait_ge(head_made, made)
                wait(act, qrope_step, 3 * (h - 1))
                act.activation(split(raw_m[0:QK_MLA, h % 2, :]), pair(h % 2, QK_MLA), ACT.Copy).then_inc(qraw_taken, 1)
            scale = QK_MLA ** -0.5
            act.wait_ge(mm_step, 2)
            act.activation(pmm[0:META, :, :], pmm[0:META, :, :], ACT.Exp, scale=scale).then_inc(mm_act, 1)
            act.wait_ge(m_turned, 1)
            act.activation(amTm[0:META, :, :], ps[0:META, 5, 0:256].rearrange("p (a b) -> p a b", b=META), ACT.Copy)\
                .then_inc(mm_act, 1)
            act.wait_ge(m_av, 1)
            act.activation(o_m[:, :, 0:META], ps[:, 6, 0:P].rearrange("p (a b) -> p a b", b=META), ACT.Copy)\
                .then_inc(mm_act, 1)
            units = [(h, b) for h in range(MLA_HEADS) for b in range(TB)]
            n = len(units)
            for u in range(n + 2):
                if u < n:
                    h, b = units[u]
                    wait(act, m_turned, u)
                    act.wait_ge(m_nmax, u + 1)
                    dst = probm[:, u % 2, 0:META + (b + 1) * P]
                    act.activation(dst if b < TB - 1 else split(dst), seen(2 * (u % 2), b), ACT.Exp,
                                   bias=sm_nmax[:, u % 2:u % 2 + 1], scale=scale,
                                   accum_out=sm_sum[:, u % 2:u % 2 + 1]).then_inc(m_prob, 1)
                if 1 <= u <= n:
                    act.wait_ge(m_turned, u + 1)
                    if u >= 3:
                        act.wait_ge(m_av, u - 1)
                    keep(aTm, u - 1, units[u - 1][1], m_kept)
                if u >= 2 and units[u - 2][1] == TB - 1 and units[u - 2][0] % 2:
                    h = units[u - 2][0]
                    act.wait_ge(m_av, u)
                    act.activation(o_m[:, h // 2, META:L], ps[:, 6 + (h // 2) % 2, :], ACT.Copy).then_inc(m_taken, 1)
            ffn(1, n_ffn1, lambda c: act.wait_ge(o_added[1], c + 1))
            norm_rstd(act, n_fin, lambda c: x[:, c, :], 1.0 / D, 1, lambda c: act.wait_ge(ffn_added[1], c + 1))
            act.wait_ge(normed, n_fin.done)
            act.dma_start(out_d, hf).then_inc(stored, 16)
            act.wait_ge(stored, 16)

        @block.gpsimd
        def _(pool):
            for k in range(2):
                pool.memset(f_pad[k][:, 0:SEQ], 0.0).then_inc(pads_zeroed, 1)
                pool.memset(m_pad[k][:, 0:SEQ], 0.0).then_inc(pads_zeroed, 1)
            pool.memset(conv_in[:, :, 0:CONV1 - 1], 0.0).then_inc(pads_zeroed, 1)
            pool.wait_ge(pads_zeroed, 5)
            pool.wait_ge(gates_taken, 2)
            pool.tensor_scalar(n_row, f_row, 0.0, 2.0, ALU.min, ALU.mult).then_inc(row_min, 1)
            pool.wait_ge(row_min, 1)
            pool.tensor_tensor(e_row, n_row, f_row, ALU.subtract).then_inc(row_min, 1)
            pool.wait_ge(row_act, 2)
            pool.tensor_scalar(f_row, f_row, 0.0, None, ALU.min).then_inc(row_step, 1)
            pool.wait_ge(row_step, 1)
            pool.tensor_tensor(f_pad[0][:, SEQ:], f_row, e_row, ALU.subtract).then_inc(row_step, 1)
            for k in range(LOG_SEQ):
                pool.wait_ge(row_step, k + 2)
                src, dst = f_pad[k % 2], f_pad[(k + 1) % 2]
                pool.tensor_tensor(dst[:, SEQ:], src[:, SEQ:], src[:, SEQ - (1 << k):2 * SEQ - (1 << k)], ALU.add)\
                    .then_inc(row_step, 1)
            pool.wait_ge(row_step, LOG_SEQ + 2)
            pool.tensor_tensor(n_row, i_row, f_pad[1][:, SEQ:], ALU.subtract).then_inc(row_step, 1)
            for h in range(SB_HEADS):
                pool.wait_ge(z_copied, h + 1)
                for s in range(TB):
                    o = (0, 512, 1024, 896)[s]
                    m = z_buf[:, h % 2, o:o + P]
                    last = pool.affine_select(out=m, in_=m, compare_op=ALU.is_gt, fill=-BIG, base=0,
                                              pattern=[[1, P]], channel_multiplier=-1)
                last.then_inc(z_masked, 1)

            for k in range(2):
                if k == 0:
                    pool.wait_ge(o_added[0], DC)
                else:
                    pool.wait_ge(kr_step, 3)
                    for h in range(MLA_HEADS):
                        pool.tensor_copy(k_m[NOPE:QK_MLA, h, :], kr[NOPE:QK_MLA, :]).then_inc(kr_copied, 1)
                    pool.wait_ge(o_added[1], DC)
                pool.memset(a_pad[:, :, 0:CONV2 - 1], 0.0).then_inc(ffn_zero, 1)

        @block.vector
        def _(dve):
            def modulation(first, n):
                return dve.tensor_tensor(mod[:, first:first + n], ps[:, 7, first:first + n],
                                         vec[:, VEC["b_ada"] + first:VEC["b_ada"] + first + n], ALU.add)

            def modulated_gain(k, name):
                s = (1 + 3 * k) * DC
                dve.scalar_tensor_tensor(gains[:, k, :], mod[:, s:s + DC], 1.0, vec[:, VEC[name]:VEC[name] + DC],
                                         ALU.add, ALU.mult).then_inc(gains_ready, 1)

            dve.wait_ge(inputs_in, 5 * 16)
            dve.wait_ge(slot_used, used(TURN["ada_scale1"], 7))
            modulation(0, 2 * DC).then_inc(mod_ready, 1)
            dve.wait_ge(mod_ready, 1)
            modulated_gain(0, "g_norm1")
            dve.wait_ge(gains_ready, 1)
            norm_apply(dve, n_in1, lambda c: xf[:, c, :], lambda c: gains[:, 0, c:c + 1], lambda c: hf[:, c, :])
            norm_apply(dve, n_qk, lambda c: qk[:, c, :], lambda c: col("g_q_sb" if c < 4 else "g_k_sb"),
                       lambda c: qk[:, c, :])

            def sb_logw(h):
                dve.wait_ge(between_ready, h + 1)
                wait(dve, y_ready, h - 1)
                dve.tensor_tensor(w_buf[:, h % 2, :], ps[:, 3:6, :].rearrange("p a b -> p (a b)")[:, 0:1280],
                                  z_buf[:, h % 2, :], ALU.add).then_inc(logw_ready, 1)

            def sb_take(pair):
                dve.wait_ge(y_ready, 2 * pair + 2)
                dve.tensor_copy(mixed[:, pair, :], ps[:, 6, :]).then_inc(y_taken, 1)

            dve.wait_ge(normed, n_qk.done)
            for h in range(SB_HEADS):
                z, sp = z_buf[:, h % 2, :], sp_buf[:, h % 2, :]
                dve.wait_ge(z_masked, h + 1)
                wait(dve, between_ready, h - 1)
                dve.scalar_tensor_tensor(sp, z, -1.0, z, ALU.mult, ALU.min).then_inc(nabs_ready, 1)
                if h:
                    sb_logw(h - 1)
                dve.wait_ge(log_ready, h + 1)
                dve.scalar_tensor_tensor(sp, z, 0.0, sp, ALU.max, ALU.add).then_inc(sp_ready, 1)
                if h >= 2 and h % 2 == 0:
                    sb_take(h // 2 - 1)
                if h == 3:
                    dve.wait_ge(row_step, ROW_STEPS)
                    dve.tensor_scalar(m_pad[0][:, SEQ:], n_row, 0.0, None, ALU.max).then_inc(max_step, 1)
                    for k in range(LOG_SEQ):
                        dve.wait_ge(max_step, k + 1)
                        src, dst = m_pad[k % 2], m_pad[(k + 1) % 2]
                        dve.tensor_tensor(dst[:, SEQ:], src[:, SEQ:], src[:, SEQ - (1 << k):2 * SEQ - (1 << k)], ALU.max)\
                            .then_inc(max_step, 1)
                    dve.wait_ge(max_step, LOG_SEQ + 1)
                    dve.tensor_tensor(e_row, m_pad[1][:, SEQ:], f_pad[1][:, SEQ:], ALU.add).then_inc(max_step, 1)
                dve.wait_ge(win_taken, 20)
                for j in range(CONV1):
                    src = conv_in[:, h, j:j + SEQ]
                    w = col("conv_w", CONV1 * h + j)
                    if j == 0:
                        dve.tensor_scalar(conv[:, h, :], src, w, None, ALU.mult).then_inc(conv_step, 1)
                    else:
                        dve.wait_ge(conv_step, CONV1 * h + j)
                        dve.scalar_tensor_tensor(conv[:, h, :], src, w, conv[:, h, :], ALU.mult, ALU.add)\
                            .then_inc(conv_step, 1)
                if h >= 1 and h % 2 == 1:
                    m = 2 + h // 2
                    dve.wait_ge(slot_used, used(TURN["ada_gate1"], 8 * (m - 2) + 7))
                    modulation(m * DC, DC).then_inc(mod_ready, 1)
            sb_logw(SB_HEADS - 1)
            sb_take(3)
            dve.wait_ge(mod_ready, 5)
            modulated_gain(1, "g_norm2")
            norm_apply(dve, n_ysb, lambda c: mixed[:, c, :], lambda c: col("g_out_sb", c), lambda c: mixed[:, c, :])

            dve.wait_ge(u_turned, 1)
            dve.tensor_copy(u_col, ps[:, 6, 0:16].rearrange("p (a b) -> p a b", b=ML_HEADS)).then_inc(u_col_ready, 1)
            for h in range(ML_HEADS):
                dve.wait_ge(mqk_ready, h + 1)
                dve.wait_ge(dec_ready, 4 * h + 4)
                wait(dve, num_ready, 2 * h - 2)
                dve.scalar_tensor_tensor(w_buf[:, h % 2, :], ps[:, 0:3, :].rearrange("p a b -> p (a b)")[:, 0:1280],
                                         ML_DIM ** -0.5, z_buf[:, h % 2, :], ALU.mult, ALU.mult).then_inc(wqk_ready, 1)
                d = den[:, h % 2, :]
                dve.wait_ge(num_ready, 2 * h + 2)
                dve.tensor_scalar(d, ps[:, 7, :], -1.0, None, ALU.mult).then_inc(den_step, 1)
                dve.wait_ge(den_step, 4 * h + 1)
                dve.tensor_tensor(d, ps[:, 7, :], d, ALU.max).then_inc(den_step, 1)
                dve.wait_ge(den_step, 4 * h + 2)
                dve.wait_ge(floor_ready, h + 1)
                dve.tensor_tensor(d, d, den_floor[:, h % 2, :], ALU.max).then_inc(den_step, 1)
                dve.wait_ge(den_step, 4 * h + 3)
                dve.reciprocal(d, d).then_inc(den_step, 1)
                dve.wait_ge(den_step, 4 * h + 4)
                dve.tensor_tensor(mixed[:, 4 + h, :], ps[:, 6, :], d, ALU.mult).then_inc(ml_out, 1)
            for c in range(4):
                gi = n_yml.g0 + c
                dve.wait_ge(rstd_ready, gi + 1)
                y = mixed[:, 4 + c, :]
                dve.scalar_tensor_tensor(y, y, col("g_out_ml", c), rstd1[:, gi % 2, :], ALU.mult, ALU.mult)\
                    .then_inc(normed, 1)
                dve.wait_ge(normed, gi + 1)
                dve.tensor_tensor(y, y, sig_o[:, c, :], ALU.mult).then_inc(mix_gated, 1)

            for t in range(DC):
                dve.wait_ge(slot_used, used(TURN["w_out"], t))
                dve.scalar_tensor_tensor(xf[:, t, :], ps[:, t % 4, :], mod[:, 2 * DC + t:2 * DC + t + 1], xf[:, t, :],
                                         ALU.mult, ALU.add).then_inc(out_added, 1)
            dve.wait_ge(out_added, DC)
            dve.wait_ge(gains_ready, 2)
            norm_apply(dve, n_in2, lambda c: xf[:, c, :], lambda c: gains[:, 1, c:c + 1], lambda c: hf[:, c, :])

            def route_block(b):
                at0 = b * ROUTE
                steps = [0]

                def end(instruction):
                    instruction.then_inc(route, 1)
                    steps[0] += 1

                def after(k):
                    dve.wait_ge(route, at0 + k)

                dve.wait_ge(score_ready, b + 1)
                for j in range(QH):
                    last = dve.max(top_v[:, j, 0:8], score[:, j, :])
                end(last)
                after(1)
                for j in range(QH):
                    last = dve.max_index(top_i[:, j, 0:8], top_v[:, j, 0:8], score[:, j, :])
                end(last)
                after(2)
                for j in range(QH):
                    last = dve.match_replace(score[:, j, :], top_v[:, j, 0:8], score[:, j, :], LOWEST)
                end(last)
                after(3)
                for j in range(QH):
                    last = dve.max(top_v[:, j, 8:16], score[:, j, :])
                end(last)
                after(4)
                for j in range(QH):
                    last = dve.max_index(top_i[:, j, 8:16], top_v[:, j, 8:16], score[:, j, :])
                end(last)
                after(5)
                end(dve.tensor_copy(top_if, top_i))
                pairs = top_v.rearrange("p (h t) k -> p h t k", t=2)
                grid = [P, PEER_HEADS, TOPK, TOPK]
                end(dve.tensor_tensor(cand.rearrange("p h (a b) -> p h a b", b=TOPK),
                                      pairs[:, :, 0, :].unsqueeze(3).broadcast_to(grid),
                                      pairs[:, :, 1, :].unsqueeze(2).broadcast_to(grid), ALU.add))
                after(7)
                for h in range(PEER_HEADS):
                    last = dve.max(best[:, h, 0:8], cand[:, h, :])
                end(last)
                after(8)
                for h in range(PEER_HEADS):
                    last = dve.max_index(pos[:, h, 0:8], best[:, h, 0:8], cand[:, h, :])
                end(last)
                after(9)
                for h in range(PEER_HEADS):
                    last = dve.match_replace(cand[:, h, :], best[:, h, 0:8], cand[:, h, :], LOWEST)
                end(last)
                after(10)
                for h in range(PEER_HEADS):
                    last = dve.max(best[:, h, 8:16], cand[:, h, :])
                end(last)
                after(11)
                for h in range(PEER_HEADS):
                    last = dve.max_index(pos[:, h, 8:16], best[:, h, 8:16], cand[:, h, :])
                end(last)
                after(12)
                end(dve.tensor_copy(gate_sum[:, 0, :], best[:, :, 0]))
                after(13)
                end(dve.tensor_tensor(best, best, gate_sum[:, 0, :].unsqueeze(2)
                                      .broadcast_to([P, PEER_HEADS, TOPK]), ALU.subtract))
                where = pos.rearrange("p h k -> p (h k)")
                end(dve.tensor_scalar(pos_ab[:, 0, :], where, 4, None, ALU.logical_shift_right))
                end(dve.tensor_scalar(pos_ab[:, 1, :], where, TOPK - 1, None, ALU.bitwise_and))
                after(16)
                end(dve.tensor_copy(pos_abf, pos_ab))
                halves = top_if.rearrange("p (h t) k -> p h t k", t=2)
                flat = onehot.rearrange("p h k a -> p (h k) a")
                for t in range(2):
                    after(17 + 3 * t)
                    end(dve.tensor_tensor(flat, pos_abf[:, t, :].unsqueeze(2).broadcast_to([P, NSEL, TOPK]),
                                          cst("iota", TOPK).unsqueeze(1).broadcast_to([P, NSEL, TOPK]),
                                          ALU.is_equal))
                    after(18 + 3 * t)
                    end(dve.tensor_tensor(onehot, onehot, halves[:, :, t, :].unsqueeze(2).broadcast_to(grid),
                                          ALU.mult))
                    after(19 + 3 * t)
                    end(dve.tensor_reduce(routed[:, t, :], flat, AX, ALU.add))
                dve.wait_ge(gate_exp, b + 1)
                end(dve.tensor_reduce(gate_sum[:, 0, :], best, AX, ALU.add))
                after(24)
                end(dve.reciprocal(gate_sum[:, 1, :], gate_sum[:, 0, :]))
                after(25)
                end(dve.tensor_tensor(routed[:, 2, :].rearrange("p (h k) -> p h k", k=TOPK), best,
                                      gate_sum[:, 1, :].unsqueeze(2).broadcast_to([P, PEER_HEADS, TOPK]),
                                      ALU.mult))
                assert steps[0] == ROUTE
                dve.wait_ge(routed_t, b + 1)
                for k, dst in enumerate((idx1, idx2, gate_t)):
                    here = dst[:, b * P:(b + 1) * P] if isinstance(b, int) else dst[:, bass.ds(b * P, P)]
                    dve.tensor_copy(here, ps[:, 6, k * P:(k + 1) * P]).then_inc(routed_kept, 1)

            for b in range(TB):
                route_block(b)
            dve.wait_ge(routed_kept, 3 * TB)
            dve.tensor_copy(gate_p[:, :, 0], gate_t).then_inc(parts_ready, 1)
            dve.wait_ge(parts_ready, 1)
            dve.tensor_tensor(gate_r, gate_t, gate_p[:, :, 0], ALU.subtract).then_inc(parts_ready, 1)
            dve.wait_ge(parts_ready, 2)
            dve.tensor_copy(gate_p[:, :, 1], gate_r).then_inc(parts_ready, 1)
            dve.wait_ge(parts_ready, 3)
            dve.tensor_tensor(gate_t, gate_r, gate_p[:, :, 1], ALU.subtract).then_inc(parts_ready, 1)
            dve.wait_ge(parts_ready, 4)
            dve.tensor_copy(gate_p[:, :, 2], gate_t).then_inc(parts_ready, 1)
            dve.wait_ge(parts_ready, 5)

            def hot_batch(n, k, quarter, t0):
                a = idx1[:, t0] if isinstance(t0, slice) else idx1[:, bass.ds(t0, 8)]
                b = idx2[:, t0] if isinstance(t0, slice) else idx2[:, bass.ds(t0, 8)]
                g = gate_p[:, t0, :] if isinstance(t0, slice) else gate_p[:, bass.ds(t0, 8), :]
                o = CONST["iota"] + 32 * quarter
                dve.tensor_tensor(hot1[:, k, :, :], a.unsqueeze(2).broadcast_to([P, 8, 32]),
                                  const[:, o:o + 32].unsqueeze(1).broadcast_to([P, 8, 32]), ALU.is_equal)\
                    .then_inc(hot1_ready, 1)
                wait(dve, g_made, n + -1)
                dve.tensor_tensor(hot2[:, k, :, :], b.unsqueeze(2).broadcast_to([P, 8, NKEYS]),
                                  cst("iota").unsqueeze(1).broadcast_to([P, 8, NKEYS]), ALU.is_equal)\
                    .then_inc(hot2_ready, 1)
                dve.wait_ge(hot1_ready, n + 1)
                dve.tensor_tensor(hot1g[:, k, :, :].rearrange("p t (q i) -> p t q i", i=32),
                                  hot1[:, k, :, :].unsqueeze(2).broadcast_to([P, 8, 3, 32]),
                                  g.unsqueeze(3).broadcast_to([P, 8, 3, 32]), ALU.mult).then_inc(hot1g_ready, 1)

            def g_two(i):
                for k in range(2):
                    t0 = slice(8 * k, 8 * k + 8) if isinstance(i, int) else i * 16 + 8 * k
                    hot_batch(i * 2 + k, k, 0, t0)
            turns(dve, 32, g_two)
            for quarter in range(4):
                dve.wait_ge(g_kept, 64 * (quarter + 1))

                def experts(i, quarter=quarter):
                    group = i + 16 * quarter

                    def next_gates(k):
                        t0 = slice(8 * k, 8 * k + 8) if isinstance(i, int) else i * 32 + 8 * k
                        hot_batch(i * 4 + (64 * (quarter + 1) + k), k % 2, quarter + 1, t0)

                    if quarter < 3:
                        next_gates(0)
                        next_gates(1)
                    for e in range(2):
                        dve.wait_ge(gelu_done, group * 2 + (e + 1))
                        dve.tensor_tensor(act_e[:, e, :], act_e[:, e, :], at(G[quarter % 2], i * 2 + e), ALU.mult)\
                            .then_inc(act_gated, 1)
                    if quarter < 3:
                        next_gates(2)
                        next_gates(3)
                    for d in range(DC):
                        if d < DC - 1:
                            dve.wait_ge(y_part, group * (DC - 1) + (d + 1))
                        else:
                            dve.wait_ge(slot_used, used(group + TURN["experts"], 3))
                        wait(dve, y_added, group * DC + (d + 1 - DC))
                        dve.scalar_tensor_tensor(xf[:, d, :], ps[:, 2 + d % 4, :], mod[:, 5 * DC + d:5 * DC + d + 1],
                                                 xf[:, d, :], ALU.mult, ALU.add).then_inc(y_added, 1)
                if quarter == 0:
                    turns(dve, 16, experts)
                else:
                    with dve.Fori(0, 16) as i:
                        experts(i)

            dve.wait_ge(y_added, 64 * DC)
            norm_apply(dve, n_diff, lambda c: x[:, c, :], lambda c: col("a_attn_norm", c), lambda c: hT[:, c, :])
            o = VEC["lambdas"]
            dve.tensor_tensor(lam_p, vec[:, o:o + 2], vec[:, o + 2:o + 4], ALU.mult).then_inc(lam_step, 1)

            def pair(k, rows=P):
                return ps[0:rows, 2 * k:2 * k + 2, 0:HALF]

            def rope(dst, raw, rotated, tmp, cos, sin, step, step0):
                dve.tensor_tensor(dst, raw, cos, ALU.mult).then_inc(step, 1)
                dve.tensor_tensor(split(tmp), rotated, split(sin), ALU.mult).then_inc(step, 1)
                dve.wait_ge(step, step0 + 2)
                dve.tensor_tensor(dst, dst, tmp, ALU.add).then_inc(step, 1)

            dve.wait_ge(tables_in, 16)

            def rope_tiles(i):
                for s in range(RING):
                    t = RING * i + s
                    dve.wait_ge(raw_taken, t + 1)
                    dve.wait_ge(rot_ready, t + 1)
                    rope(at(qk_d, t), raw_d[:, s % 2, :], pair(2 + s % 2), tmp_d[:, s % 2, :], tab("cos_d"),
                         tab("sin_d"), rope_step, t * 3)
            turns(dve, 4, rope_tiles)
            dve.wait_ge(lam_exp, 1)
            dve.scalar_tensor_tensor(neg_lam, lam_e[:, 1:2], LAM_INIT, lam_e[:, 0:1], ALU.subtract, ALU.subtract)\
                .then_inc(lam_step, 1)
            pm4 = pm[0:META, :, :].rearrange("p (m h) k -> p m h k", m=2)
            src4 = ps[0:META, 6:8, 0:P].rearrange("p m (h k) -> p m h k", k=META)
            wide = [META, 16, META]
            dve.wait_ge(meta_pe, 1)
            for m in range(2):
                last = dve.tensor_reduce(pm_max[0:META, 8 * m:8 * m + 8], src4[:, m], AX, ALU.max)
            last.then_inc(meta_step, 1)
            dve.wait_ge(meta_step, 1)
            for m in range(2):
                last = dve.tensor_tensor(pm4[:, m], src4[:, m], pm_max[0:META, 8 * m:8 * m + 8].unsqueeze(2)
                                         .broadcast_to([META, 8, META]), ALU.subtract)
            last.then_inc(meta_step, 1)
            dve.wait_ge(meta_act, 1)
            dve.tensor_reduce(pm_sum[0:META, :], pm[0:META, :, :], AX, ALU.add).then_inc(meta_step, 1)
            dve.wait_ge(meta_step, 3)
            dve.reciprocal(pm_rec[0:META, :], pm_sum[0:META, :]).then_inc(meta_step, 1)
            dve.wait_ge(meta_step, 4)
            dve.wait_ge(lam_step, 2)
            dve.tensor_scalar(pm_rec[0:META, 8:16], pm_rec[0:META, 8:16], neg_lam[0:META, :], None, ALU.mult)\
                .then_inc(meta_step, 1)
            dve.wait_ge(meta_step, 5)
            dve.tensor_tensor(pm[0:META, :, :], pm[0:META, :, :], pm_rec[0:META, :].unsqueeze(2).broadcast_to(wide),
                              ALU.mult).then_inc(meta_step, 1)
            dve.wait_ge(meta_step, 6)
            dve.tensor_tensor(pm[0:META, 0:8, :], pm[0:META, 0:8, :], pm[0:META, 8:16, :], ALU.add)\
                .then_inc(meta_step, 1)

            def seen(k, b):
                W = META + (b + 1) * P
                return ps[:, k, 0:W] if W <= BANK else ps[:, k:k + 2, 0:HALF]

            def row_max(dst, src, b):
                return dve.tensor_reduce(dst, src, AX if b < TB - 1 else mybir.AxisListType.XY, ALU.max)

            units = [(h, b) for h in range(DIFF_HEADS) for b in range(TB)]
            n = len(units)
            scale = DIFF_DIM ** -0.5
            for u in range(n + 1):
                if u < n:
                    b = units[u][1]
                    for m in range(2):
                        k = 2 * u + m
                        dve.wait_ge(s_made, k + 1)
                        row_max(st_max[:, u % 2, m:m + 1], seen(2 * m, b), b).then_inc(max_ready, 1)
                        dve.wait_ge(max_ready, k + 1)
                        wait(dve, p_ready, k - 3)
                        dve.tensor_scalar(st_nmax[:, u % 2, m:m + 1], st_max[:, u % 2, m:m + 1], -scale, None, ALU.mult)\
                            .then_inc(nmax_ready, 1)
                if u:
                    v = u - 1
                    W = META + (units[v][1] + 1) * P
                    dve.wait_ge(p_ready, 2 * v + 2)
                    dve.reciprocal(st_rec[:, v % 2, :], st_sum[:, v % 2, :]).then_inc(rec_step, 1)
                    dve.wait_ge(rec_step, 3 * v + 1)
                    dve.tensor_tensor(st_rec[:, v % 2, 1:2], st_rec[:, v % 2, 1:2], neg_lam, ALU.mult).then_inc(rec_step, 1)
                    p0, p1 = prob[:, v % 2, 0, 0:W], prob[:, v % 2, 1, 0:W]
                    dve.tensor_scalar(p0, p0, st_rec[:, v % 2, 0:1], None, ALU.mult).then_inc(rec_step, 1)
                    dve.wait_ge(rec_step, 3 * v + 3)
                    dve.scalar_tensor_tensor(p0, p1, st_rec[:, v % 2, 1:2], p0, ALU.mult, ALU.add).then_inc(a_ready, 1)
            for c in range(8):
                gi = n_sub.g0 + c
                dve.wait_ge(rstd_ready, gi + 1)
                r = rstd2[:, gi % 2, :]
                dve.tensor_scalar(r, r, 1.0 - LAM_INIT, None, ALU.mult).then_inc(lam_step, 1)
                dve.wait_ge(lam_step, 3 + c)
                dve.scalar_tensor_tensor(o_d[:, c, :], o_d[:, c, :], col("a_sub_norm"), r, ALU.mult, ALU.mult)\
                    .then_inc(normed, 1)

            def out_add(name, k):
                for t in range(DC):
                    dve.wait_ge(slot_used, used(TURN[name], t))
                    dve.tensor_tensor(split(x[:, t, :]), split(x[:, t, :]), pair(t % 2), ALU.add).then_inc(o_added[k], 1)
                dve.wait_ge(o_added[k], DC)

            def ffn(k, n):
                norm_apply(dve, n, lambda c: x[:, c, :], lambda c: col("ffn_norm", DC * k + c), lambda c: hT[:, c, :])

                def up(i):
                    for e in range(2):
                        f = i * 2 + e
                        s0 = i * 6 + 3 * e
                        u = u_ffn[:, e, :]

                        def column(name, width, j, f=f):
                            o = VEC[name] + FC * width * k + j
                            if isinstance(f, int):
                                return vec[:, o + width * f:o + width * f + 1]
                            return vec[:, bass.ds(f * width + o, 1)]

                        dve.wait_ge(a_taken[k], f + 1)
                        dve.tensor_scalar(u, a_pad[:, e, 0:L], column("ffn_conv_w", CONV2, 0), column("ffn_conv_b", 1, 0),
                                          ALU.mult, ALU.add).then_inc(fconv_step[k], 1)
                        for j in range(1, CONV2):
                            dve.wait_ge(fconv_step[k], s0 + j)
                            dve.scalar_tensor_tensor(u, a_pad[:, e, j:j + L], column("ffn_conv_w", CONV2, j), u,
                                                     ALU.mult, ALU.add).then_inc(fconv_step[k], 1)
                        dve.wait_ge(fsilu_done[k], f + 1)
                        dve.wait_ge(slot_used, used(i + TURN[f"ffn_in{k}"], 2 * e + 1))
                        dve.tensor_tensor(split(at(gated, f)), split(u), pair(2 * e + 1), ALU.mult)\
                            .then_inc(ffn_gated[k], 1)
                turns(dve, FC // 2, up)

                for t in range(DC):
                    dve.wait_ge(slot_used, used(TURN[f"ffn_out{k}"], 3 * t + 2))
                    dve.tensor_tensor(split(x[:, t, :]), split(x[:, t, :]), pair(t % 4), ALU.add).then_inc(ffn_added[k], 1)
                dve.wait_ge(ffn_added[k], DC)

            out_add("o_diff", 0)
            ffn(0, n_ffn0)

            dve.wait_ge(rstd_ready, n_lat.done)
            r = rstd2[:, n_lat.g0 % 2, :]
            for c in range(DC):
                dve.scalar_tensor_tensor(h_kv[:, c, :], x[:, c, :], col("kv_norm", c), r, ALU.mult, ALU.mult)
            for c in range(DC):
                last = dve.scalar_tensor_tensor(hT[:, c, :], x[:, c, :], col("b_attn_norm", c), r, ALU.mult, ALU.mult)
            last.then_inc(normed, 1)
            R = QK_MLA
            dve.wait_ge(kr_rot, 1)
            rope(kr[0:R, :], kr_raw[0:R, :], pair(0, R), tmp_m[0:R, 0, :], tab("cos_m", L, R), tab("sin_m", L, R),
                 kr_step, 0)
            norm_apply(dve, n_ckv, lambda c: ckv_raw[:, c, :], lambda c: col("kv_a_norm", c), lambda c: ckv[:, c, :])
            norm_apply(dve, n_cq, lambda c: cq_raw[:, c, :], lambda c: col("b_q_a_norm", c), lambda c: cqn[:, c, :])
            for h in range(MLA_HEADS):
                dve.wait_ge(qraw_taken, h + 1)
                dve.wait_ge(qrot_ready, h + 1)
                rope(q_m[0:R, h, :], raw_m[0:R, h % 2, :], pair(2 + h % 2, R), tmp_m[0:R, h % 2, :],
                     tab("cos_m", L, R), tab("sin_m", L, R), qrope_step, 3 * h)
            dve.wait_ge(m_made, 1)
            src = ps[0:META, 7, 0:256].rearrange("p (h k) -> p h k", k=META)
            dve.tensor_reduce(pmm_max[0:META, :], src, AX, ALU.max).then_inc(mm_step, 1)
            dve.wait_ge(mm_step, 1)
            dve.tensor_tensor(pmm[0:META, :, :], src, pmm_max[0:META, :].unsqueeze(2).broadcast_to(wide), ALU.subtract)\
                .then_inc(mm_step, 1)
            dve.wait_ge(mm_act, 1)
            dve.tensor_reduce(pmm_sum[0:META, :], pmm[0:META, :, :], AX, ALU.add).then_inc(mm_step, 1)
            dve.wait_ge(mm_step, 3)
            dve.reciprocal(pmm_rec[0:META, :], pmm_sum[0:META, :]).then_inc(mm_step, 1)
            dve.wait_ge(mm_step, 4)
            dve.tensor_tensor(pmm[0:META, :, :], pmm[0:META, :, :], pmm_rec[0:META, :].unsqueeze(2).broadcast_to(wide),
                              ALU.mult).then_inc(mm_step, 1)
            units = [(h, b) for h in range(MLA_HEADS) for b in range(TB)]
            n = len(units)
            scale = QK_MLA ** -0.5
            for u in range(n + 1):
                if u < n:
                    b = units[u][1]
                    dve.wait_ge(m_made, u + 2)
                    row_max(sm_max[:, u % 2:u % 2 + 1], seen(2 * (u % 2), b), b).then_inc(m_max, 1)
                    dve.wait_ge(m_max, u + 1)
                    wait(dve, m_prob, u - 1)
                    dve.tensor_scalar(sm_nmax[:, u % 2:u % 2 + 1], sm_max[:, u % 2:u % 2 + 1], -scale, None, ALU.mult)\
                        .then_inc(m_nmax, 1)
                if u:
                    v = u - 1
                    p = probm[:, v % 2, 0:META + (units[v][1] + 1) * P]
                    dve.wait_ge(m_prob, v + 1)
                    dve.reciprocal(sm_rec[:, v % 2:v % 2 + 1], sm_sum[:, v % 2:v % 2 + 1]).then_inc(m_rec, 1)
                    dve.wait_ge(m_rec, v + 1)
                    dve.tensor_scalar(p, p, sm_rec[:, v % 2:v % 2 + 1], None, ALU.mult).then_inc(m_scaled, 1)
            out_add("o_mla", 1)
            ffn(1, n_ffn1)
            norm_apply(dve, n_fin, lambda c: x[:, c, :], lambda c: col("final_norm", c), lambda c: hT[:, c, :])


def feature_slots(w):
    K, N = w.shape
    return w.reshape(K // P, P, N // P, P).transpose(2, 1, 0, 3).reshape(N // P, P, (K // P) * P)


def token_slots(w):
    return w.reshape(-1, 2, P, BANK).transpose(0, 2, 1, 3).reshape(-1, P, SLOT)


def pad_slot(a):
    out = np.zeros((a.shape[0], P, SLOT), np.float32)
    out[:, :, :a.shape[2]] = a
    return out


def columns(v):
    return np.ascontiguousarray(v).reshape(-1, P).T


def kernel(**inp):
    import concourse.bacc as bacc
    from concourse.bass_utils import run_bass_kernel_spmd

    a = {k: np.asarray(v) for k, v in inp.items()}
    f32 = np.float32
    ada = feature_slots(a["w_ada"][0])
    w_in = a["w_in"][0]
    eu = a["expert_u"][0].reshape(NKEYS, P, DC, P).transpose(0, 3, 2, 1).reshape(NKEYS, P, SLOT)
    ev = a["expert_v"][0].reshape(NKEYS, P, SLOT)
    experts = np.concatenate([eu.reshape(64, 2, P, SLOT), ev.reshape(64, 2, P, SLOT)], 1).reshape(256, P, SLOT)
    qkv = a["a_w_qkv_2"][0]

    def ffn_slots(k):
        w = feature_slots(a["ffn_w_in_2"][k])
        up = np.stack([w[:FC], w[FC:]], 1).reshape(2 * FC, P, SLOT)
        down = np.zeros((DC, P, 3 * SLOT), f32)
        down[:, :, :FC * P] = feature_slots(a["ffn_w_out_2"][k])
        return [up, down.reshape(DC, P, 3, SLOT).transpose(0, 2, 1, 3).reshape(3 * DC, P, SLOT)]

    dkv, ukv, uq = a["kv_w_dkv_2"], a["kv_w_ukv_2"], a["b_w_uq_2"][0]
    rope_tile = np.zeros((1, P, DC, P), f32)
    rope_tile[0, :, :, :QK_MLA] = dkv[:, KV_LORA - NOPE:].reshape(DC, P, QK_MLA).transpose(1, 0, 2)
    ukv4 = ukv.reshape(KVC, P, MLA_HEADS, NOPE + MLA_V)
    k_part = ukv4[..., :NOPE].transpose(2, 1, 0, 3).reshape(2, 8, P, KVC * NOPE).transpose(0, 2, 1, 3).reshape(2, P, SLOT)
    v_part = ukv4[..., NOPE:].reshape(KVC, P, 2, BANK).transpose(2, 1, 0, 3).reshape(2, P, SLOT)
    uq_h = uq.reshape(QC, P, MLA_HEADS, QK_MLA).transpose(2, 1, 0, 3).reshape(MLA_HEADS, P, QC * QK_MLA)
    uq_pad = np.zeros((18, P, QC * QK_MLA), f32)
    uq_pad[:MLA_HEADS] = uq_h
    uq_part = pad_slot(uq_pad.reshape(6, 3, P, QC * QK_MLA).transpose(0, 2, 1, 3).reshape(6, P, 3 * QC * QK_MLA))
    parts = [ada[0:16], feature_slots(w_in[:, 0:1024]), token_slots(w_in[:, 1024:1536]),
             feature_slots(w_in[:, 1536:2560]), token_slots(w_in[:, 2560:3072]), feature_slots(w_in[:, 3072:3584]),
             ada[16:48], feature_slots(a["w_out"][0]), feature_slots(a["w_q_peer"][0]), experts,
             feature_slots(qkv[:, 0:2048]), token_slots(qkv[:, 2048:2560]), token_slots(qkv[:, 2560:3072]),
             feature_slots(a["a_w_o_2"][0]), *ffn_slots(0),
             feature_slots(dkv[:, :KV_LORA]), rope_tile.reshape(1, P, SLOT), feature_slots(a["b_w_dq_2"][0]),
             k_part, v_part, uq_part, feature_slots(a["b_w_o_2"][0]), *ffn_slots(1)]
    stream = np.concatenate(parts, 0)
    assert stream.shape == (TURNS * RING, P, SLOT), stream.shape

    vec = np.zeros((P, NVEC), f32)

    def put(name, v, rows=P):
        vec[:rows, VEC[name]:VEC[name] + v.shape[1]] = v

    for name, key in (("c", "c"), ("b_ada", "b_ada"), ("g_norm1", "g_norm1"), ("g_out_sb", "g_out_sb"),
                      ("g_out_ml", "g_out_ml"), ("g_norm2", "g_norm2"), ("a_attn_norm", "a_attn_norm_2"),
                      ("a_sub_norm", "a_sub_norm_2"), ("kv_norm", "kv_norm_2"), ("kv_a_norm", "kv_a_norm_2"),
                      ("b_attn_norm", "b_attn_norm_2"), ("b_q_a_norm", "b_q_a_norm_2"), ("ffn_norm", "ffn_norm_2"),
                      ("ffn_conv_b", "ffn_conv_b_2"), ("final_norm", "final_norm_2")):
        put(name, columns(a[key]))
    put("conv_w", a["conv_w"][0].reshape(CONV1, DC, P).transpose(2, 1, 0).reshape(P, DC * CONV1))
    put("ffn_conv_w", a["ffn_conv_w_2"].reshape(2, CONV2, FC, P).transpose(3, 0, 2, 1).reshape(P, 2 * FC * CONV2))
    put("g_q_sb", np.tile(a["g_q_sb"][0], 2)[:, None])
    put("g_k_sb", np.tile(a["g_k_sb"][0], 2)[:, None])
    put("b_igate", a["b_igate"][0][:, None], 4)
    put("b_fgate", a["b_fgate"][0][:, None], 4)
    put("w_gates", w_in[:, 3584:3592].reshape(DC, P, 8).transpose(1, 0, 2).reshape(P, DC * 8))
    for j, key in enumerate(("a_lambda_q1_2", "a_lambda_q2_2", "a_lambda_k1_2", "a_lambda_k2_2")):
        vec[:DIFF_DIM, VEC["lambdas"] + j] = a[key][0]
    vec[:, VEC["eps"]] = EPS1
    vec[:, VEC["eps"] + 1] = EPS2

    const = np.zeros((P, NCONST), f32)

    def constant(name, v):
        const[:v.shape[0], CONST[name]:CONST[name] + v.shape[1]] = v

    i, j = np.meshgrid(np.arange(P), np.arange(P), indexing="ij")
    constant("ident", np.eye(P, dtype=f32))
    constant("ones", np.ones((P, P), f32))
    constant("ones64", (i // 64 == j // 64).astype(f32))
    constant("tri", -(i >= j).astype(f32))
    constant("neg_ones", -np.ones((P, P), f32))
    constant("iota", j.astype(f32))
    constant("late", np.where(j < i, f32(BIG), f32(0)))
    constant("pick_head", np.repeat(np.eye(ML_HEADS, dtype=f32), P, 1))
    constant("first_half", (j[:1] < CHUNK).astype(f32))
    constant("lowest", np.full((1, CHUNK), -BIG, f32))
    table = np.zeros((P, NTABLE), f32)

    def rotary(kind, theta, rot_dim, heads, rows):
        half = rot_dim // 2
        inv = (1.0 / (f32(theta) ** (np.arange(half, dtype=f32) / f32(half)))).astype(f32)
        ang = np.arange(L, dtype=f32)[:, None] * inv[None, :]
        cos, sin, swap = np.ones((rows, L), f32), np.zeros((rows, L), f32), np.zeros((rows, rows), f32)
        for r0 in heads:
            for k in range(half):
                lo, hi = r0 + k, r0 + half + k
                cos[lo] = cos[hi] = np.cos(ang[:, k])
                sin[lo] = sin[hi] = np.sin(ang[:, k])
                swap[hi, lo] = -1.0
                swap[lo, hi] = 1.0
        for name, v in (("cos_", cos), ("sin_", sin), ("swap_", swap)):
            table[:rows, TABLE[name + kind]:TABLE[name + kind] + v.shape[1]] = v

    rotary("d", 500000.0, DIFF_DIM // 4, (0, DIFF_DIM), P)
    rotary("m", 10000.0, ROPE, (NOPE,), QK_MLA)

    arrays = {
        "weight_stream": stream,
        "constants": const,
        "vectors": vec,
        "tables": table,
        "x_t": np.ascontiguousarray(a["x"][0].reshape(SEQ, DC, P).transpose(2, 1, 0)),
        "meta_t": np.ascontiguousarray(a["meta_tokens_2"].reshape(META, DC, P).transpose(2, 1, 0)),
        "keys_t": np.ascontiguousarray(a["sub_keys"][0].reshape(QH, NKEYS, P).transpose(2, 0, 1)),
    }
    nc = bacc.Bacc("TRN2", target_bir_lowering=False, num_devices=1)
    args = [nc.dram_tensor(k, v.shape, F32, kind="ExternalInput").ap() for k, v in arrays.items()]
    out = nc.dram_tensor("out_t", (P, DC, SEQ), F32, kind="ExternalOutput").ap()
    build(nc, *args, out)
    r = run_bass_kernel_spmd(nc, [arrays], core_ids=[0])
    return r.results[0]["out_t"].transpose(2, 1, 0).reshape(1, SEQ, D)
```

```python
from contextlib import ExitStack
import math

import numpy as np

import concourse.bass as bass
from concourse import mybir

F32 = mybir.dt.float32
F32R = mybir.dt.float32r
U32 = mybir.dt.uint32
ALU = mybir.AluOpType
ACT = mybir.ActivationFunctionType
AX = mybir.AxisListType.X

P = 128
D = 1024
DC = D // P
SEQ = 512
META = 16
L = META + SEQ
HALF = L // 2
TB = SEQ // P
BANK = 512
SB_HEADS, SB_DIM = 8, 64
ML_HEADS, ML_DIM = 4, 128
CONV1 = 4
PEER_HEADS, NKEYS, TOPK = 8, 128, 16
QH = 2 * PEER_HEADS
NSEL = PEER_HEADS * TOPK
DIFF_HEADS, DIFF_DIM, DIFF_V = 8, 64, 128
MLA_HEADS, NOPE, ROPE, MLA_V = 16, 64, 32, 64
QK_MLA = NOPE + ROPE
Q_LORA, KV_LORA = 384, 256
QC, KVC = Q_LORA // P, KV_LORA // P
D_FF = 2816
FC = D_FF // P
CONV2 = 3
CHUNK = 64
EPS1, EPS2 = 1e-6, 1e-5
LAM_INIT = 0.8 - 0.6 * math.exp(-0.3 * 0)
BIG = 1e30
LOWEST = -3.0e38

SLOT = 1024
RING = 4
STAGES = [("qk_sb", 2), ("v_sb", 1), ("qk_ml", 2), ("v_ml", 1),
          ("o_ml", 1),
          ("w_out", 2), ("peer_q", 4), ("experts_u", 16), ("experts", 48), ("qk_diff", 4), ("v_diff", 2), ("o_diff", 2),
          ("ffn_in0", 11), ("ffn_out0", 6), ("mla", 4), ("o_mla", 2), ("ffn_in1", 11), ("ffn_out1", 6)]
TURN = {}
_t = 0
for _n, _k in STAGES:
    TURN[_n] = _t
    _t += _k
TURNS = _t
PLAIN = ("mla",)
UNSPLIT = {}
_t = 0
for _n, _k in STAGES:
    UNSPLIT[_n] = _t
    _t += RING * _k if _n in PLAIN else 0
RUNS = []
for _n, _k in STAGES:
    if RUNS and RUNS[-1][3] == (_n in PLAIN):
        RUNS[-1][1] += _k
    else:
        RUNS.append([TURN[_n], TURN[_n] + _k, UNSPLIT[_n], _n in PLAIN])

VEC = {}
VECS = [("b_ada", 6 * DC), ("g_norm1", DC), ("conv_w", DC * CONV1), ("g_q_sb", 1), ("g_k_sb", 1),
        ("g_out_sb", 4), ("g_out_ml", 4), ("g_norm2", DC), ("b_igate", 1), ("b_fgate", 1),
        ("w_gates", DC * 36), ("a_attn_norm", DC), ("lambdas", 4), ("a_sub_norm", 1), ("kv_norm", DC),
        ("kv_a_norm", KVC), ("b_attn_norm", DC), ("b_q_a_norm", QC), ("ffn_norm", 2 * DC),
        ("ffn_conv_w", 2 * FC * CONV2), ("ffn_conv_b", 2 * FC), ("final_norm", DC), ("eps", 2)]
NVEC = 0
for _n, _k in VECS:
    VEC[_n] = NVEC
    NVEC += _k

CONST = {}
NCONST = 0
for _n, _k in [("ident", P), ("ones", P), ("ones64", P), ("tri", P), ("neg_ones", P), ("iota", P),
               ("late", P), ("hidden", P), ("pick_head", ML_HEADS * P), ("first_half", P), ("lowest", CHUNK)]:
    CONST[_n] = NCONST
    NCONST += _k
TABLE = {}
NTABLE = 0
for _n, _k in [("cos_d", L), ("sin_d", L), ("cos_m", L), ("sin_m", L), ("swap_d", P), ("swap_m", QK_MLA)]:
    TABLE[_n] = NTABLE
    NTABLE += _k

TILES = 64
STEP = 64
BATCH = 4
LOG_SEQ = 9
ROW_STEPS = LOG_SEQ + 3
MAX_STEPS = LOG_SEQ + 2
ROUTE = 26


class Norm:
    squares = 0
    groups = 0

    def __init__(self, groups, tokens):
        self.chunks = groups
        self.T = tokens
        self.q0, self.g0 = Norm.squares, Norm.groups
        Norm.squares += sum(len(g) for g in groups)
        Norm.groups += len(groups)
        self.done = Norm.groups


class Split:
    chunks = 0
    raws = 0

    def __init__(self, norm=None):
        self.norm = norm
        self.q0, self.r0 = Split.chunks, Split.raws
        Split.chunks += DC
        Split.raws += DC - 1 if norm else 0


def build(nc, c_d, ada_d, stream, consts_d, vecs_d, tables_d, x_d, meta_d, keys_d, act_d, gates_d, out_d):
    with ExitStack() as ctx:
        def sem(name):
            return ctx.enter_context(nc.semaphore(name))

        base = -(-nc.sbuf_base // 32) * 32
        top = [0]

        def place(name, shape, dt=F32, at=None):
            n = -(-int(np.prod(shape[1:])) // 8) * 8
            if at is None:
                at = top[0]
                top[0] += n
            return nc.alloc_sbuf_tensor_at(name, shape, dt, offset=base + 4 * at)

        ring = place("ring", [P, RING, SLOT])
        at_w = top[0]
        w_hi = place("w_hi", [P, RING, SLOT], F32R)
        w_lo = place("w_lo", [P, RING, SLOT], F32R)
        work_w = place("work_w", [P, 2 * RING * SLOT], at=at_w)
        at_h = top[0]
        h_hi = place("h_hi", [P, DC, L], F32R)
        h_lo = place("h_lo", [P, DC, L], F32R)
        h32 = place("h32", [P, 2 * DC, L], at=at_h)
        x = place("x", [P, DC, L])
        const = place("const", [P, NCONST])
        vec = place("vec", [P, NVEC])
        mod = place("mod", [P, 6 * DC])
        gains = place("gains", [P, 2, DC])
        mod_sum = place("mod_sum", [P, 6 * DC])
        at_arena = top[0]
        ARENA = (nc.sbuf_top - base) // 4 - at_arena
        arena = place("arena", [P, ARENA])
        arena_r = place("arena_r", [P, ARENA], F32R, at=at_arena)
        ps = ctx.enter_context(nc.psum_tensor("ps", [P, 8, BANK], F32))

        def view(at, *dims, dt=F32, rows=P, of=None):
            n = int(np.prod(dims))
            of = of if of is not None else arena_r if dt == F32R else arena
            assert at + n <= of.shape[1], (at, dims, of.shape)
            a = of[0:rows, at:at + n]
            if dt == U32:
                a = a.bitcast(dt)
            if len(dims) == 2:
                a = a.rearrange("p (a b) -> p a b", b=dims[1])
            if len(dims) == 3:
                a = a.rearrange("p (a b c) -> p a b c", b=dims[1], c=dims[2])
            if len(dims) == 4:
                a = a.rearrange("p (a b c d) -> p a b c d", b=dims[1], c=dims[2], d=dims[3])
            return a

        def cst(name, n=P, rows=P):
            return const[0:rows, CONST[name]:CONST[name] + n]

        def col(name, i=0, rows=P):
            return vec[0:rows, VEC[name] + i:VEC[name] + i + 1]

        ident, ones, ones64 = cst("ident"), cst("ones"), cst("ones64")
        xf = x[:, :, META:L]
        h_tmp = view(4448, 2, L)

        sq1 = view(0, 2, SEQ)
        rstd1 = view(1024, 2, SEQ)
        ada_w = view(5504, 2 * DC, D)
        ada_late = view(10328, 2, RING, D)
        silu_c = view(22632, D)
        qk = view(2112, 8, SEQ)
        conv_in = view(6208, 8, SEQ + CONV1 - 1)
        v_sb = view(10328, TB, SEQ)
        v_ml = view(12376, TB, SEQ)
        sig_o = view(14424, 4, SEQ)
        f_pad = [view(16472, 1024, rows=4), view(17496, 1024, rows=4)]
        m_pad = [view(18520, 1024, rows=4), view(19544, 1024, rows=4)]
        i_row = view(20568, SEQ, rows=4)
        f_row = view(21080, SEQ, rows=4)
        e_row = view(21592, SEQ, rows=4)
        n_row = view(22104, SEQ, rows=4)
        u_col = view(22616, TB, ML_HEADS)
        den = view(2112, 2, SEQ)
        den_floor = view(3136, 2, SEQ)
        z_buf = view(0, 2, 1280, of=work_w)
        sp_buf = view(2560, 2, 1280, of=work_w)
        w_buf = view(5120, 2, 1280, of=work_w)
        conv = h32[:, 0:DC, 0:SEQ]
        mixed = h32[:, DC:2 * DC, META:L]

        idx1 = view(2112, SEQ)
        idx2 = view(2624, SEQ)
        gate_t = view(3136, SEQ)
        q_peer = view(4448, QH, SEQ)
        score = view(12640, QH, NKEYS)
        cand = view(14688, PEER_HEADS, TOPK * TOPK)
        onehot = view(16736, PEER_HEADS, TOPK, TOPK)
        top_v = view(18784, QH, TOPK)
        top_i = view(19040, QH, TOPK, dt=U32)
        top_if = view(19296, QH, TOPK)
        best = view(19552, PEER_HEADS, TOPK)
        pos = view(19680, PEER_HEADS, TOPK, dt=U32)
        pos_ab = view(19808, 2, NSEL, dt=U32)
        pos_abf = view(20064, 2, NSEL)
        routed = view(20320, 3, NSEL)
        gate_sum = view(20704, 2, PEER_HEADS)
        act_u = view(20832, 2, SEQ)
        keys = view(23656, QH, NKEYS)
        g_stage = [view(4448, NKEYS, STEP), view(12640, NKEYS, STEP)]
        hot2 = view(22880, 2, BATCH, NKEYS)
        hot1g = view(23904, 2, BATCH, NKEYS)
        early = view(4448, 2, 2, SEQ)
        g_early = view(6496, 2, SEQ // STEP, 2 * STEP)
        g_late = view(8544, 2, SEQ // STEP, 2 * STEP)
        early_hi = view(11616, 2, SEQ, dt=F32R)
        early_lo = view(12640, 2, SEQ, dt=F32R)
        late_hi = view(13664, 2, 2, SEQ, dt=F32R)
        late_lo = view(15712, 2, 2, SEQ, dt=F32R)
        late = view(22880, 2, SEQ)

        sq2 = view(0, 2, L)
        rstd2 = view(1056, 2, L)
        table = view(2112, NTABLE)

        def tab(name, n=L, rows=P):
            return table[0:rows, TABLE[name]:TABLE[name] + n]

        v_d = view(4448, 5, D)
        qk_d = view(9568, 16, L)
        raw_d = view(18016, 2, L)
        tmp_d = view(19072, 2, L)
        prob = view(18016, 3, 2, L)
        aT = view(21184, 2, 5, P)
        o_d = h32[:, DC:2 * DC, :]
        st_max, st_nmax, st_sum, st_rec = (view(22464 + 6 * k, 3, 2) for k in range(4))
        lam_p = view(22488, 2)
        lam_e = view(22490, 2)
        neg_lam = view(22492, 1)
        pm = view(22496, 16, META)
        pm_max, pm_sum, pm_rec = (view(22752 + 16 * k, 16) for k in range(3))
        amT = view(22800, 16, META)
        a_pad = view(0, 2, L + CONV2 - 1)
        u_ffn = view(1060, 2, L)
        gated_hi = view(2208, FC, L, dt=F32R)
        gated_lo = view(2208 + FC * L, FC, L, dt=F32R)
        k_m = view(4448, MLA_HEADS, L)
        q_m = view(12896, MLA_HEADS, L)
        ckv = view(21344, KVC, L)
        cq = view(22400, QC, L)
        kr_raw = view(23984, L)
        kr = view(24512, L)
        v_m = view(0, 5, D, of=work_w)
        raw_m = view(5120, 2, L, of=work_w)
        tmp_m = view(6176, 2, L, of=work_w)
        probm = view(5120, 3, L, of=work_w)
        aTm = view(6704, 2, 5, P, of=work_w)
        h_kv = h32[:, DC:2 * DC, :]
        h_q = h32[:, 0:DC, :]
        o_m = h32[:, DC:2 * DC, :]
        STM = 25040
        sm_max, sm_nmax, sm_sum, sm_rec = (view(STM + 4 * k, 4) for k in range(4))
        pmm = view(STM + 16, 16, META)
        pmm_max, pmm_sum, pmm_rec = (view(STM + 272 + 16 * k, 16) for k in range(3))
        amTm = view(STM + 320, 16, META)
        y_out = h32[:, 0:DC, :]
        D_SCORES = (2, 0, 2, 0)
        M_SCORES = (0, 1, 2, 3)

        def score_at(k, b):
            W = META + (b + 1) * P
            return ps[:, k, 0:W] if W <= BANK else ps[:, k:k + 2, 0:HALF]

        def turned_at(bank, k, b):
            return ps[:, bank, :], ps[0:META, bank if b < TB - 1 else k + 1, BANK - P:BANK]

        vec_in, const_in, x_in = sem("vec_in"), sem("const_in"), sem("x_in")
        later_in = sem("later_in")
        ada_in = [sem(f"ada_in{k}") for k in range(4)]
        ada_late_in = [sem(f"ada_late_in{k}") for k in range(2)]
        ada_done = sem("ada_done")
        tables_in = sem("tables_in")
        slot_loaded = [sem(f"slot_loaded{s}") for s in range(RING)]
        slot_used = sem("slot_used")
        hi_ready = sem("hi_ready")
        lo_ready = sem("lo_ready")
        h_raw = sem("h_raw")
        h_hi_ready = sem("h_hi_ready")
        h_split = sem("h_split")
        sq_ready = sem("sq_ready")
        sq_summed = sem("sq_summed")
        ln_done = sem("ln_done")
        rstd_ready = sem("rstd_ready")
        normed = sem("normed")
        silu_c_ready = sem("silu_c_ready")
        mod_ready = sem("mod_ready")
        gains_ready = sem("gains_ready")
        gates_ready = sem("gates_ready")
        gates_taken = sem("gates_taken")
        win_taken = sem("win_taken")
        pads_zeroed = sem("pads_zeroed")
        row_step = sem("row_step")
        row_act = sem("row_act")
        max_step = sem("max_step")
        row_min = sem("row_min")
        z_ready = sem("z_ready")
        z_copied = sem("z_copied")
        nabs_ready = sem("nabs_ready")
        e_ready = sem("e_ready")
        log_ready = sem("log_ready")
        sp_ready = sem("sp_ready")
        between_ready = sem("between_ready")
        logw_ready = sem("logw_ready")
        w_ready = sem("w_ready")
        y_ready = sem("y_ready")
        y_taken = sem("y_taken")
        conv_step = sem("conv_step")
        conv_silu = sem("conv_silu")
        u_turned = sem("u_turned")
        u_col_ready = sem("u_col_ready")
        mqk_ready = sem("mqk_ready")
        mb_ready = sem("mb_ready")
        dec_ready = sem("dec_ready")
        wqk_ready = sem("wqk_ready")
        num_ready = sem("num_ready")
        den_step = sem("den_step")
        floor_ready = sem("floor_ready")
        ml_out = sem("ml_out")
        mix_gated = sem("mix_gated")
        out_added = sem("out_added")
        q_peer_taken = sem("q_peer_taken")
        score_made = sem("score_made")
        score_ready = sem("score_ready")
        route = sem("route")
        gate_exp = sem("gate_exp")
        routed_t = sem("routed_t")
        routed_kept = sem("routed_kept")
        hot_ready = sem("hot_ready")
        g_made = sem("g_made")
        g_kept = sem("g_kept")
        gelu_done = sem("gelu_done")
        act_saved = [sem(f"act_saved{k}") for k in range(2)]
        g_saved = [sem(f"g_saved{k}") for k in range(2)]
        early_in = [sem(f"early_in{k}") for k in range(2)]
        late_in = [sem(f"late_in{k}") for k in range(2)]
        act_gated = sem("act_gated")
        act_hi = sem("act_hi")
        act_split = sem("act_split")
        y_part = sem("y_part")
        y_added = sem("y_added")
        raw_taken = sem("raw_taken")
        rot_ready = sem("rot_ready")
        rope_step = sem("rope_step")
        v_taken = sem("v_taken")
        lam_step = sem("lam_step")
        lam_sum = sem("lam_sum")
        lam_exp = sem("lam_exp")
        meta_step = sem("meta_step")
        meta_pe = sem("meta_pe")
        meta_act = sem("meta_act")
        s_made = sem("s_made")
        max_ready = sem("max_ready")
        nmax_ready = sem("nmax_ready")
        p_ready = sem("p_ready")
        rec_step = sem("rec_step")
        a_ready = sem("a_ready")
        a_turned = sem("a_turned")
        aT_kept = sem("aT_kept")
        av_done = sem("av_done")
        o_taken = sem("o_taken")
        ffn_zero = sem("ffn_zero")
        a_taken = [sem(f"a_taken{k}") for k in range(2)]
        fconv_step = [sem(f"fconv_step{k}") for k in range(2)]
        fsilu_done = [sem(f"fsilu_done{k}") for k in range(2)]
        gated_hi_done = [sem(f"gated_hi_done{k}") for k in range(2)]
        gated_split = [sem(f"gated_split{k}") for k in range(2)]
        ffn_gated = [sem(f"ffn_gated{k}") for k in range(2)]
        ffn_added = [sem(f"ffn_added{k}") for k in range(2)]
        o_added = [sem(f"o_added{k}") for k in range(2)]
        lat_taken = sem("lat_taken")
        kr_step = sem("kr_step")
        kr_rot = sem("kr_rot")
        kr_copied = sem("kr_copied")
        kn_taken = sem("kn_taken")
        vm_taken = sem("vm_taken")
        qraw_taken = sem("qraw_taken")
        qrot_ready = sem("qrot_ready")
        qrope_step = sem("qrope_step")
        mm_step, mm_act = sem("mm_step"), sem("mm_act")
        head_made = sem("head_made")
        m_made, m_max, m_nmax, m_prob = sem("m_made"), sem("m_max"), sem("m_nmax"), sem("m_prob")
        m_rec, m_scaled, m_turned = sem("m_rec"), sem("m_scaled"), sem("m_turned")
        m_kept, m_av, m_taken = sem("m_kept"), sem("m_av"), sem("m_taken")
        stored = sem("stored")

        every = list(range(DC))
        Norm.squares = Norm.groups = 0
        n_in1 = Norm([every], SEQ)
        n_qk = Norm([[c] for c in range(8)], SEQ)
        n_ysb = Norm([[c] for c in range(4)], SEQ)
        n_yml = Norm([[c] for c in range(4)], SEQ)
        n_in2 = Norm([every], SEQ)
        n_diff = Norm([every], L)
        n_sub = Norm([[c] for c in range(8)], L)
        n_ffn0 = Norm([every], L)
        n_lat = Norm([every], L)
        n_ckv = Norm([[0, 1]], L)
        n_cq = Norm([[0, 1, 2]], L)
        n_ffn1 = Norm([every], L)
        n_fin = Norm([every], L)
        Split.chunks = Split.raws = 0
        s_in1 = Split(n_in1)
        s_mix = Split()
        s_in2 = Split(n_in2)
        s_diff = Split(n_diff)
        s_od = Split()
        s_ffn0 = Split(n_ffn0)
        s_om = Split()
        s_ffn1 = Split(n_ffn1)

        def pieces(T):
            return [(0, T)] if T <= BANK else [(0, HALF), (HALF, T)]

        def ms_psum(gi, T):
            return ps[:, 4 + gi % 2, 0:T] if T <= BANK else ps[:, 4 + 2 * (gi % 2):6 + 2 * (gi % 2), 0:HALF]

        def split(ap):
            return ap.rearrange("p (a b) -> p a b", b=HALF)

        def wait(eng, s, value):
            if not isinstance(value, int) or value > 0:
                eng.wait_ge(s, value)

        def turns(eng, n, body):
            body(0)
            if n == 2:
                body(1)
            elif n > 2:
                with eng.Fori(1, n) as i:
                    body(i)

        def at(t, k):
            return t[:, k, :] if isinstance(k, int) else t[:, bass.ds(k, 1), :].rearrange("p o n -> p (o n)")

        def norm_sums(pe, n, lhsT):
            k = n.q0
            for g, group in enumerate(n.chunks):
                gi = n.g0 + g
                wait(pe, ln_done, gi - 1)
                dst = ms_psum(gi, n.T)
                for j, _ in enumerate(group):
                    pe.wait_ge(sq_ready, k + 1)
                    src = (sq1 if n.T == SEQ else sq2)[:, k % 2, :]
                    for b, (lo, hi) in enumerate(pieces(n.T)):
                        last = pe.matmul(dst if n.T == SEQ else dst[:, b, :], lhsT, src[:, lo:hi],
                                         start=j == 0, stop=j == len(group) - 1)
                    last.then_inc(sq_summed, 1)
                    k += 1

        def norm_rstd(act, n, src, scale, eps, ready=None, behind=None):
            at_q = [n.q0]

            def squares(g):
                for c in n.chunks[g]:
                    k = at_q[0]
                    wait(act, sq_summed, k - 1)
                    if ready is not None:
                        ready(c)
                    act.activation((sq1 if n.T == SEQ else sq2)[:, k % 2, :], src(c), ACT.Square).then_inc(sq_ready, 1)
                    at_q[0] += 1

            squares(0)
            summed = n.q0
            for g, group in enumerate(n.chunks):
                gi = n.g0 + g
                if g + 1 < len(n.chunks):
                    squares(g + 1)
                summed += len(group)
                act.wait_ge(sq_summed, summed)
                wait(act, normed, gi - 1)
                r = (rstd1 if n.T == SEQ else rstd2)[:, gi % 2, :]
                act.activation(r if n.T == SEQ else split(r), ms_psum(gi, n.T), ACT.Ln,
                               bias=col("eps", eps), scale=scale).then_inc(ln_done, 1)
                act.wait_ge(ln_done, gi + 1)
                act.activation(r, r, ACT.Exp, scale=-0.5).then_inc(rstd_ready, 1)
                if behind is not None:
                    behind(g)

        def exp_log(act):
            act.preload_act_table_set("natural_log_exp_and_others")

        def norm_apply(dve, n, src, gain, dst):
            for g, group in enumerate(n.chunks):
                gi = n.g0 + g
                dve.wait_ge(rstd_ready, gi + 1)
                r = (rstd1 if n.T == SEQ else rstd2)[:, gi % 2, :]
                for c in group:
                    last = dve.scalar_tensor_tensor(dst(c), src(c), gain(c), r, ALU.mult, ALU.mult)
                last.then_inc(normed, 1)

        def split_normed(dve, sp, src, gain, shift=None):
            n, first = sp.norm, L - sp.norm.T
            gi = n.g0
            r = (rstd1 if n.T == SEQ else rstd2)[:, gi % 2, :]
            dve.wait_ge(rstd_ready, gi + 1)
            for c in range(DC + 1):
                if c < DC:
                    if c >= 2:
                        dve.wait_ge(h_split, sp.q0 + c - 1)
                    dve.scalar_tensor_tensor(h_tmp[:, c % 2, 0:n.T], src(c), gain(c), r, ALU.mult, ALU.mult)\
                        .then_inc(*((h_raw, 1) if c < DC - 1 else (normed, 1)))
                if c:
                    low_part(dve, sp, c - 1, h_tmp[:, (c - 1) % 2, 0:n.T], first, shift)

        def low_part(dve, sp, c, src, first, shift=None):
            dve.wait_ge(h_hi_ready, sp.q0 + c + 1)
            lo, hi = h_lo[:, c, first:L], h_hi[:, c, first:L]
            if shift is None:
                dve.tensor_tensor(lo, src, hi, ALU.subtract).then_inc(h_split, 1)
            else:
                dve.scalar_tensor_tensor(lo, src, shift(c), hi, ALU.add, ALU.subtract).then_inc(h_split, 1)

        def high_normed(act, sp, c, shift=None):
            n = sp.norm
            if c < DC - 1:
                act.wait_ge(h_raw, sp.r0 + c + 1)
            else:
                act.wait_ge(normed, n.done)
            dst, src = h_hi[:, c, L - n.T:L], h_tmp[:, c % 2, 0:n.T]
            if shift is None:
                act.activation(dst, src, ACT.Copy).then_inc(h_hi_ready, 1)
            else:
                act.activation(dst, src, ACT.Identity, bias=shift(c)).then_inc(h_hi_ready, 1)

        def slot_wait(pe, turn, s):
            pe.wait_ge(slot_loaded[s], turn * 16 + 16)

        def slot(s):
            return ring[:, s, :]

        def split_wait(pe, name, turn, s):
            pe.wait_ge(lo_ready, turn * RING + (s + 1 - UNSPLIT[name]))

        def split_slot(act, turn, s):
            act.wait_ge(slot_loaded[s], turn * 16 + 16)
            wait(act, slot_used, turn * RING + (s + 1 - RING))
            act.activation(w_hi[:, s, :], ring[:, s, :], ACT.Copy).then_inc(hi_ready, 1)

        def split_next(act, name, turn, s):
            split_slot(act, turn + (TURN[name] + 1), s)

        def bodies(eng, body):
            t0 = TURN["experts"]
            body(0, t0, 2, 0, 0)
            with eng.Fori(0, TILES // 4 - 1) as m:
                body(m * 2 + 1, m * 3 + (t0 + 2), 0, 1, m)
                body(m * 2 + 2, m * 3 + (t0 + 3), 2, 0, m + 1)

        def span(eng, lo, hi, body):
            if lo == 0:
                body(0)
                lo = 1
            if hi - lo == 1:
                body(lo)
            elif hi > lo:
                with eng.Fori(lo, hi) as i:
                    body(i)

        def used(turn, s):
            return turn * RING + (s + 1)

        block = ctx.enter_context(nc.Block())

        @block.sync
        def _(sp):
            for s in range(RING):
                sp.dma_start(ring[:, s, :], stream[s]).then_inc(slot_loaded[s], 16)
            for first, end, unsplit, plain in RUNS:
                with sp.Fori(first + 1, min(end + 1, TURNS)) as i:
                    for s in range(RING):
                        if plain:
                            sp.wait_ge(slot_used, i * RING + (s + 1 - RING))
                        else:
                            sp.wait_ge(lo_ready, i * RING + (s + 1 - RING - unsplit))
                        sp.dma_start(ring[:, s, :], stream[bass.ds(i * RING + s, 1), :, :]
                                     .rearrange("o p n -> (o p) n")).then_inc(slot_loaded[s], 16)

        @block.tensor
        def _(pe):
            def three(h, w):
                return (w[0], h[0]), (w[0], h[1]), (w[1], h[0])

            def weights(s, lo, hi):
                return w_hi[:, s, lo:hi], w_lo[:, s, lo:hi]

            def tile1(name, turn, s, bank, sp=None, between=None):
                split_wait(pe, name, turn, s)
                for c in range(DC):
                    if sp is not None:
                        pe.wait_ge(h_split, sp.q0 + c + 1)
                    h = h_hi[:, c, META:L], h_lo[:, c, META:L]
                    for p, (w, v) in enumerate(three(h, weights(s, c * P, (c + 1) * P))):
                        last = pe.matmul(ps[:, bank, :], w, v, start=c == 0 and p == 0, stop=c == DC - 1 and p == 2)
                    if c == DC - 1:
                        last.then_inc(slot_used, 1)
                    if between is not None and c % 2:
                        between(c // 2)

            pe.wait_ge(const_in, 16)
            norm_sums(pe, n_in1, ones)

            pe.wait_ge(h_split, s_in1.q0 + DC)
            for c in range(DC):
                o = VEC["w_gates"] + 36 * c
                for p in range(2):
                    part = (h_hi, h_lo)[p][:, c, META:L].bitcast(F32)
                    last = pe.matmul(ps[0:36, 4, :], vec[:, o:o + 36], part,
                                     start=c == 0 and p == 0, stop=c == DC - 1 and p == 1)
            last.then_inc(gates_ready, 1)
            tile = 0
            for name, n in (("qk_sb", 2), ("v_sb", 1), ("qk_ml", 2), ("v_ml", 1), ("o_ml", 1)):
                if name.startswith("v"):
                    pe.wait_ge(win_taken, tile)
                    for s in range(RING):
                        split_wait(pe, name, TURN[name], s)
                        for b in range(TB):
                            for j in range(2):
                                c = 2 * s + j
                                t = slice(META + b * P, META + (b + 1) * P)
                                h = h_hi[:, c, t], h_lo[:, c, t]
                                for p, (w, v) in enumerate(three(h, weights(s, j * BANK, (j + 1) * BANK))):
                                    last = pe.matmul(ps[:, b, :], v, w, start=c == 0 and p == 0,
                                                     stop=c == DC - 1 and p == 2)
                        last.then_inc(slot_used, 1)
                    tile += TB
                else:
                    for i in range(n):
                        for s in range(RING):
                            wait(pe, win_taken, tile - 3)
                            tile1(name, TURN[name] + i, s, s)
                            tile += 1

            pe.wait_ge(gates_taken, 2)
            norm_sums(pe, n_qk, ones64)

            pe.wait_ge(normed, n_qk.done)
            pe.wait_ge(win_taken, 28)

            def causal(bank0, s):
                o = (0, 512, 1024, 896)[s]
                return ps[:, bank0 + o // BANK, o % BANK:o % BANK + SEQ - s * P]

            def sb_scores(h):
                rows = slice(64 * (h % 2), 64 * (h % 2) + 64)
                wait(pe, z_copied, h)
                for s in range(TB):
                    pe.matmul(causal(0, s), qk[rows, 4 + h // 2, s * P:(s + 1) * P], qk[rows, h // 2, s * P:SEQ],
                              start=True, stop=False)
                    last = pe.matmul(causal(0, s)[:, 0:P], ident, cst("hidden"), start=False, stop=True)
                last.then_inc(z_ready, 1)

            def sb_between(h):
                pe.wait_ge(sp_ready, h + 1)
                wait(pe, logw_ready, h)
                for s in range(TB):
                    out = causal(3, s)
                    for j in range(s, TB):
                        o = (0, 512, 1024, 896)[j]
                        last = pe.matmul(out[:, (j - s) * P:], cst("tri") if j == s else cst("neg_ones"),
                                         sp_buf[:, h % 2, o:o + SEQ - j * P], start=j == s, stop=j == TB - 1)
                last.then_inc(between_ready, 1)

            def sb_out(h):
                rows = slice(64 * (h % 2), 64 * (h % 2) + 64)
                pe.wait_ge(w_ready, h + 1)
                if h % 2 == 0:
                    wait(pe, y_taken, h // 2)
                for s in range(TB):
                    o = (0, 512, 1024, 896)[s]
                    last = pe.matmul(ps[rows, 6, s * P:SEQ], v_sb[:, s, h * SB_DIM:(h + 1) * SB_DIM],
                                     w_buf[:, h % 2, o:o + SEQ - s * P], start=s == 0, stop=s == TB - 1)
                last.then_inc(y_ready, 1)

            sb_scores(0)
            sb_scores(1)
            for h in range(SB_HEADS):
                sb_between(h)
                if h:
                    sb_out(h - 1)
                if h + 2 < SB_HEADS:
                    sb_scores(h + 2)
            sb_out(SB_HEADS - 1)
            norm_sums(pe, n_ysb, ones64)
            pe.wait_ge(ln_done, n_ysb.done)

            pe.wait_ge(max_step, MAX_STEPS)
            for b in range(TB):
                last = pe.transpose(ps[:, 6, 4 * b:4 * b + 4], n_row[:, b * P:(b + 1) * P], ident[0:4, 0:4])
            last.then_inc(u_turned, 1)
            pe.wait_ge(conv_silu, 8)
            for h in range(ML_HEADS):
                wait(pe, wqk_ready, h)
                for s in range(TB):
                    last = pe.matmul(causal(0, s), conv[:, 4 + h, s * P:(s + 1) * P], conv[:, h, s * P:SEQ],
                                     start=True, stop=True)
                last.then_inc(mqk_ready, 1)
                wait(pe, floor_ready, h)
                wait(pe, dec_ready, 4 * h)
                for s in range(TB):
                    out = causal(3, s)
                    pe.matmul(out, cst("pick_head", ML_HEADS * P, 4)[:, h * P:(h + 1) * P],
                              m_pad[1][:, SEQ + s * P:2 * SEQ], start=True, stop=False)
                    last = pe.matmul(out[:, 0:P], ident, cst("late"), start=False, stop=True)
                last.then_inc(mb_ready, 1)
                pe.wait_ge(wqk_ready, h + 1)
                if h == 0:
                    pe.wait_ge(row_act, 3)
                    pe.wait_ge(u_col_ready, 1)
                    wait(pe, ml_out, h)
                for bank, lhs in ((6, None), (7, ones)):
                    for s in range(TB):
                        o = (0, 512, 1024, 896)[s]
                        lhsT = v_ml[:, s, h * P:(h + 1) * P] if lhs is None else lhs
                        last = pe.matmul(ps[:, bank, s * P:SEQ], lhsT, w_buf[:, h % 2, o:o + SEQ - s * P],
                                         start=s == 0, stop=s == TB - 1)
                last.then_inc(num_ready, 1)
                pe.wait_ge(dec_ready, 4 * (h + 1))
                pe.matmul(ps[:, 3, :], cst("pick_head", ML_HEADS * P, 4)[:, h * P:(h + 1) * P], e_row,
                          start=True, stop=True).then_inc(num_ready, 1)
            norm_sums(pe, n_yml, ones)

            pe.wait_ge(wqk_ready, ML_HEADS)
            pe.wait_ge(floor_ready, ML_HEADS)
            for t in range(DC):
                wait(pe, out_added, t - 3)
                tile1("w_out", TURN["w_out"] + t // 4, t % 4, t % 4, s_mix if t == 0 else None)

            norm_sums(pe, n_in2, ones)
            pe.wait_ge(out_added, DC)

            def q_tiles(i):
                for s in range(RING):
                    t = RING * i + s
                    wait(pe, q_peer_taken, t - 3)
                    tile1("peer_q", TURN["peer_q"] + i, s, s, s_in2 if isinstance(i, int) and i == 0 and s == 0 else None)
            turns(pe, 4, q_tiles)
            pe.wait_ge(q_peer_taken, QH)
            pe.wait_ge(later_in, 32)

            def peer_scores(b):
                wait(pe, score_ready, b)
                for j in range(QH):
                    last = pe.matmul(ps[:, j // 4, (j % 4) * P:(j % 4 + 1) * P], q_peer[:, j, b * P:(b + 1) * P],
                                     keys[:, j, :], start=True, stop=True)
                last.then_inc(score_made, 1)

            def early_tile(j, s, between=None):
                wait(pe, gelu_done, j * RING + (s - 1))
                tile1("experts_u", j + TURN["experts_u"], s, 4 + s % 2, between=between)

            def early_turn(j):
                for s in range(RING):
                    early_tile(j, s)

            peer_scores(0)
            for b in range(TB):
                if b + 1 < TB:
                    peer_scores(b + 1)
                span(pe, 2 * b, 2 * b + 2, early_turn)
                pe.wait_ge(route, ROUTE * (b + 1))
                wait(pe, routed_kept, 3 * b)
                for k in range(3):
                    last = pe.transpose(ps[:, 6, k * P:(k + 1) * P], routed[:, k, :], ident)
                last.then_inc(routed_t, 1)
            pe.wait_ge(routed_kept, 3 * TB)

            def g_batch(n, k):
                pe.wait_ge(hot_ready, n + 1)
                wait(pe, g_kept, n + -1)
                for t in range(BATCH):
                    last = pe.matmul(ps[:, 6 + k, t * P:(t + 1) * P], hot2[:, k, t, :], hot1g[:, k, t, :],
                                     start=True, stop=True)
                last.then_inc(g_made, 1)

            def g_steps(i):
                for half in range(2):
                    for s in range(RING):
                        early_tile(i * 2 + (8 + half), s,
                                   lambda k: g_batch(i * 32 + (16 * half + 4 * s + k), k % 2))
            turns(pe, 4, g_steps)

            def late_tile(i, j, turn, s):
                wait(pe, gelu_done, i * 2 + (TILES + j - 1))
                tile1("experts", turn, s, 4 + j)

            def share(turn, slots, parts, part0):
                for s in slots:
                    split_wait(pe, "experts", turn + s[0], s[1])
                for d in range(DC):
                    wait(pe, y_added, part0 + (d - 3))
                    for j in range(2):
                        h = parts[0][:, j, :], parts[1][:, j, :]
                        for p, (w, v) in enumerate(three(h, weights(slots[j][1], d * P, (d + 1) * P))):
                            last = pe.matmul(ps[:, d % 4, :], w, v, start=j == 0 and p == 0, stop=j == 1 and p == 2)
                        if d == DC - 1:
                            last.then_inc(slot_used, 1)
                    if d < DC - 1:
                        last.then_inc(y_part, 1)

            def late_parts(p):
                return late_hi[:, p], late_lo[:, p]

            def experts(i, turn, r, p, half):
                at_slot = [((r + j) // RING, (r + j) % RING) for j in range(6)]
                for j in range(2):
                    late_tile(i + 1, j, turn + at_slot[j][0], at_slot[j][1])
                pe.wait_ge(act_split, i * 4 + 4)
                share(turn, at_slot[2:4], (early_hi, early_lo), i * 16)
                share(turn, at_slot[4:6], late_parts(p), i * 16 + DC)

            t0, last_step = TURN["experts"], TILES // 2 - 1
            for j in range(2):
                late_tile(0, j, t0, j)
            bodies(pe, experts)
            pe.wait_ge(act_split, last_step * 4 + 4)
            share(t0 + 47, ((0, 0), (0, 1)), (early_hi, early_lo), last_step * 16)
            share(t0 + 47, ((0, 2), (0, 3)), late_parts(last_step % 2), last_step * 16 + DC)

            def tile2(name, turn, s, pair, sp=None):
                split_wait(pe, name, turn, s)
                for c in range(DC):
                    if sp is not None:
                        pe.wait_ge(h_split, sp.q0 + c + 1)
                    h = h_hi[:, c, :], h_lo[:, c, :]
                    for p, (w, v) in enumerate(three(h, weights(s, c * P, (c + 1) * P))):
                        for b, (lo, hi) in enumerate(pieces(L)):
                            last = pe.matmul(ps[:, 2 * pair + b, 0:HALF], w, v[:, lo:hi], start=c == 0 and p == 0,
                                             stop=c == DC - 1 and p == 2)
                return last

            def tile2_plain(s, src, pair, chunks=DC, at0=0, step=P, M=P):
                for c in range(chunks):
                    for b, (lo, hi) in enumerate(pieces(L)):
                        o = at0 + c * step
                        last = pe.matmul(ps[0:M, 2 * pair + b, 0:HALF], slot(s)[:, o:o + M], src[:, c, lo:hi],
                                         start=c == 0, stop=c == chunks - 1)
                return last

            def rot(src, pair, rows=P, name="swap_d"):
                for b, (lo, hi) in enumerate(pieces(L)):
                    last = pe.matmul(ps[0:rows, 2 * pair + b, 0:HALF], tab(name, rows, rows), src[0:rows, lo:hi],
                                     start=True, stop=True)
                return last

            pe.wait_ge(y_added, TILES * DC)
            norm_sums(pe, n_diff, ones)
            pe.wait_ge(tables_in, 16)

            def qk_tiles(i):
                for s in range(RING):
                    t = RING * i + s
                    wait(pe, raw_taken, t + -1)
                    tile2("qk_diff", TURN["qk_diff"] + i, s, s % 2,
                          s_diff if isinstance(i, int) and i == 0 and s == 0 else None).then_inc(slot_used, 1)
                    if s or not isinstance(i, int) or i:
                        pe.wait_ge(raw_taken, t)
                        wait(pe, rope_step, t * 3 + -6)
                        rot(raw_d[:, (s + 1) % 2, :], 2 + (s + 1) % 2).then_inc(rot_ready, 1)
            turns(pe, 4, qk_tiles)
            pe.wait_ge(raw_taken, 16)
            pe.wait_ge(rope_step, 3 * 14)
            rot(raw_d[:, 1, :], 3).then_inc(rot_ready, 1)

            def token_blocks():
                return [(0, P)] + [(META + b * P, META + (b + 1) * P) for b in range(TB)]

            pe.wait_ge(rope_step, 48)
            for half in range(2):
                wait(pe, v_taken, 5 * half)
                for s in range(RING):
                    split_wait(pe, "v_diff", TURN["v_diff"] + half, s)
                    for b, (lo, hi) in enumerate(token_blocks()):
                        for j in range(2):
                            c = 2 * s + j
                            h = h_hi[:, c, lo:hi], h_lo[:, c, lo:hi]
                            for p, (w, v) in enumerate(three(h, weights(s, j * BANK, (j + 1) * BANK))):
                                last = pe.matmul(ps[:, b, :], v, w, start=c == 0 and p == 0, stop=c == DC - 1 and p == 2)
                    last.then_inc(slot_used, 1)

            pe.wait_ge(lam_step, 1)
            pe.matmul(ps[:, 5, 0:2], ones, lam_p, start=True, stop=True).then_inc(lam_sum, 1)
            pe.wait_ge(v_taken, 10)
            for m in range(16):
                r = slice(64 * (m % 2), 64 * (m % 2) + 64)
                last = pe.matmul(ps[0:META, 6 + m % 2, 16 * (m // 2):16 * (m // 2) + META], qk_d[r, m // 2, 0:META],
                                 qk_d[r, 8 + m // 2, 0:META], start=True, stop=True)
            last.then_inc(meta_pe, 1)
            pe.wait_ge(meta_step, 7)
            pe.wait_ge(lam_exp, 1)
            for h in range(8):
                last = pe.transpose(ps[0:META, 5, 16 * h:16 * h + 16], pm[0:META, h, :], ident[0:META, 0:META])
            last.then_inc(meta_pe, 1)
            pe.wait_ge(meta_act, 2)
            for h in range(8):
                last = pe.matmul(ps[:, 7, 16 * h:16 * h + 16], v_d[0:META, 0, h * P:(h + 1) * P], amT[0:META, h, :],
                                 start=True, stop=True)
            last.then_inc(meta_pe, 1)

            def scores(k, lhsT, rhs, b):
                W = META + (b + 1) * P
                if W <= BANK:
                    pe.matmul(ps[:, k, 0:W], lhsT, rhs[:, 0:W], start=True, stop=False)
                    m = ps[:, k, W - CHUNK:W]
                else:
                    pe.matmul(ps[:, k, 0:HALF], lhsT, rhs[:, 0:HALF], start=True, stop=True)
                    pe.matmul(ps[:, k + 1, 0:HALF], lhsT, rhs[:, HALF:L], start=True, stop=False)
                    m = ps[:, k + 1, HALF - CHUNK:HALF]
                return pe.matmul(m, cst("first_half", P, 1), cst("lowest", CHUNK, 1), start=False, stop=True)

            def turn_probs(bank, k, a, b):
                frames, meta = turned_at(bank, k, b)
                for j in range(b + 1):
                    pe.transpose(frames[:, j * P:(j + 1) * P], a[:, META + j * P:META + (j + 1) * P], ident)
                return pe.transpose(meta, a[:, 0:META], ident)

            units = [(h, b) for h in range(DIFF_HEADS) for b in range(TB)]

            def d_scores(u):
                h, b = units[u]
                for m in range(2):
                    wait(pe, p_ready, 2 * (u - 2) + m + 1)
                    wait(pe, aT_kept, 2 * (u - 3) if b == TB - 1 else 0)
                    r = slice(64 * m, 64 * m + 64)
                    scores(D_SCORES[b] + 3 * m, qk_d[r, h, META + b * P:META + (b + 1) * P], qk_d[r, 8 + h, :], b)\
                        .then_inc(s_made, 1)

            def d_turn(u):
                pe.wait_ge(a_ready, u + 1)
                wait(pe, aT_kept, 2 * u)
                turn_probs(6, D_SCORES[units[u][1]], prob[:, u % 3, 0, :], units[u][1]).then_inc(a_turned, 1)

            def d_out(u):
                h, b = units[u]
                pe.wait_ge(aT_kept, 2 * u + 2)
                if b == 0:
                    wait(pe, o_taken, h)
                out = ps[:, 7, b * P:(b + 1) * P]
                pe.matmul(out, v_d[0:META, 0, h * P:(h + 1) * P], aT[0:META, u % 2, 0, :], start=True, stop=False)
                for k in range(1, b + 2):
                    last = pe.matmul(out, v_d[:, k, h * P:(h + 1) * P], aT[:, u % 2, k, :], start=False, stop=k == b + 1)
                last.then_inc(av_done, 1)

            pe.wait_ge(meta_act, 3)
            n = len(units)
            for u in range(n + 3):
                if u < n:
                    d_scores(u)
                if 2 <= u < n + 2:
                    d_turn(u - 2)
                if u >= 3:
                    d_out(u - 3)
            norm_sums(pe, n_sub, ones)

            def out_tiles(name, k, sp):
                for t in range(DC):
                    wait(pe, o_added[k], t - 1)
                    tile2(name, TURN[name] + t // 4, t % 4, t % 2, sp if t == 0 else None).then_inc(slot_used, 1)

            out_tiles("o_diff", 0, s_od)

            def ffn(k, n, sp):
                norm_sums(pe, n, ones)

                def up(i):
                    name = f"ffn_in{k}"
                    for e in range(2):
                        wait(pe, a_taken[k], i * 2 + (e - 1))
                        tile2(name, i + TURN[name], 2 * e, 2 * e, sp if isinstance(i, int) and i == 0 and e == 0 else None)\
                            .then_inc(slot_used, 1)
                        wait(pe, ffn_gated[k], i * 2 + (e - 1))
                        tile2(name, i + TURN[name], 2 * e + 1, 2 * e + 1).then_inc(slot_used, 1)
                turns(pe, FC // 2, up)
                pe.wait_ge(gated_split[k], FC)

                def down(i):
                    for t in range(4):
                        wait(pe, ffn_added[k], i * 4 + (t - 3))
                        for q in range(3):
                            s = 3 * t + q
                            split_wait(pe, f"ffn_out{k}", i * 3 + (TURN[f"ffn_out{k}"] + s // RING), s % RING)
                            for c in range(8):
                                f = 8 * q + c
                                if f >= FC:
                                    continue
                                g = gated_hi[:, f, :], gated_lo[:, f, :]
                                for p, (w, v) in enumerate(three(g, weights(s % RING, c * P, (c + 1) * P))):
                                    for b, (lo, hi) in enumerate(pieces(L)):
                                        last = pe.matmul(ps[:, 2 * t + b, 0:HALF], w, v[:, lo:hi],
                                                         start=f == 0 and p == 0, stop=f == FC - 1 and p == 2)
                            last.then_inc(slot_used, 1)
                turns(pe, 2, down)

            pe.wait_ge(o_added[0], DC)
            ffn(0, n_ffn0, s_ffn0)

            pe.wait_ge(ffn_added[0], DC)
            norm_sums(pe, n_lat, ones)
            pe.wait_ge(normed, n_lat.done)
            turn = TURN["mla"]

            def mla_slot(k):
                slot_wait(pe, turn + k // RING, k % RING)
                return k % RING

            for k in range(3):
                s = mla_slot(k)
                tile2_plain(s, h_kv, k, M=P if k < 2 else QK_MLA).then_inc(slot_used, 1)
            for k in range(QC):
                s = mla_slot(3 + k)
                wait(pe, lat_taken, k)
                tile2_plain(s, h_q, (3 + k) % 4).then_inc(slot_used, 1)
            pe.wait_ge(lat_taken, 6)
            pe.wait_ge(tables_in, 32)
            rot(kr_raw, 0, QK_MLA, "swap_m").then_inc(kr_rot, 1)
            norm_sums(pe, n_ckv, ones)
            norm_sums(pe, n_cq, ones)
            pe.wait_ge(normed, n_ckv.done)
            pe.wait_ge(kr_step, 3)
            for h in range(MLA_HEADS):
                if h % 8 == 0:
                    s = mla_slot(6 + h // 8)
                wait(pe, kn_taken, h - 1)
                last = tile2_plain(s, ckv, h % 2, KVC, (h % 8) * P, NOPE, NOPE)
                last.then_inc(slot_used if h % 8 == 7 else head_made, 1)
            pe.wait_ge(kn_taken, MLA_HEADS)
            pe.wait_ge(normed, n_cq.done)
            for half in range(2):
                wait(pe, vm_taken, 5 * half)
                s = mla_slot(8 + half)
                for b in range(5):
                    lo, hi = (0, META) if b == 0 else (META + (b - 1) * P, META + b * P)
                    for c in range(KVC):
                        last = pe.matmul(ps[0:hi - lo, b, :], ckv[:, c, lo:hi], slot(s)[:, c * BANK:(c + 1) * BANK],
                                         start=c == 0, stop=c == KVC - 1)
                last.then_inc(slot_used, 1)
            pe.wait_ge(vm_taken, 10)
            for h in range(MLA_HEADS + 1):
                if h < MLA_HEADS:
                    if h % 3 == 0:
                        s = mla_slot(10 + h // 3)
                    wait(pe, qraw_taken, h - 1)
                    last = tile2_plain(s, cq, h % 2, QC, (h % 3) * 3 * QK_MLA, QK_MLA, QK_MLA)
                    last.then_inc(slot_used if h % 3 == 2 or h == MLA_HEADS - 1 else head_made, 1)
                if h:
                    pe.wait_ge(qraw_taken, h)
                    wait(pe, qrope_step, 3 * (h - 2))
                    rot(raw_m[:, (h - 1) % 2, :], 2 + (h - 1) % 2, QK_MLA, "swap_m").then_inc(qrot_ready, 1)

            pe.wait_ge(qrope_step, 3 * MLA_HEADS)
            pe.wait_ge(kr_copied, MLA_HEADS)
            for h in range(MLA_HEADS):
                last = pe.matmul(ps[0:META, 7, 16 * h:16 * h + 16], q_m[0:QK_MLA, h, 0:META], k_m[0:QK_MLA, h, 0:META],
                                 start=True, stop=True)
            last.then_inc(m_made, 1)
            pe.wait_ge(mm_step, 5)
            for h in range(MLA_HEADS):
                last = pe.transpose(ps[0:META, 5, 16 * h:16 * h + 16], pmm[0:META, h, :], ident[0:META, 0:META])
            last.then_inc(m_turned, 1)
            pe.wait_ge(mm_act, 2)
            for h in range(MLA_HEADS):
                last = pe.matmul(ps[64 * (h % 2):64 * (h % 2) + 64, 6, 16 * (h // 2):16 * (h // 2) + 16],
                                 v_m[0:META, 0, h * MLA_V:(h + 1) * MLA_V], amTm[0:META, h, :], start=True, stop=True)
            last.then_inc(m_av, 1)

            units = [(h, b) for h in range(MLA_HEADS) for b in range(TB)]
            n = len(units)

            def m_scores(u):
                h, b = units[u]
                wait(pe, m_prob, u - 3)
                wait(pe, m_kept, 2 * (u - 3) if b == TB - 1 else 0)
                scores(M_SCORES[b], q_m[0:QK_MLA, h, META + b * P:META + (b + 1) * P], k_m[0:QK_MLA, h, :], b)\
                    .then_inc(m_made, 1)

            def m_turn(u):
                pe.wait_ge(m_scaled, u + 1)
                wait(pe, m_kept, 2 * (u - 1))
                turn_probs(5 + u % 2, M_SCORES[units[u][1]], probm[:, u % 3, :], units[u][1]).then_inc(m_turned, 1)

            def m_out(u):
                h, b = units[u]
                pe.wait_ge(m_kept, 2 * u + 2)
                if b == 0:
                    wait(pe, m_taken, h - 1)
                r = slice(64 * (h % 2), 64 * (h % 2) + 64)
                out = ps[r, 7, b * P:(b + 1) * P]
                v = slice(h * MLA_V, (h + 1) * MLA_V)
                pe.matmul(out, v_m[0:META, 0, v], aTm[0:META, u % 2, 0, :], start=True, stop=False)
                for k in range(1, b + 2):
                    last = pe.matmul(out, v_m[:, k, v], aTm[:, u % 2, k, :], start=False, stop=k == b + 1)
                last.then_inc(m_av, 1)

            pe.wait_ge(mm_act, 3)
            for u in range(n + 3):
                if u < n:
                    m_scores(u)
                if 2 <= u < n + 2:
                    m_turn(u - 2)
                if u >= 3:
                    m_out(u - 3)
            pe.wait_ge(m_taken, MLA_HEADS)
            out_tiles("o_mla", 1, s_om)
            pe.wait_ge(o_added[1], DC)
            ffn(1, n_ffn1, s_ffn1)
            pe.wait_ge(ffn_added[1], DC)
            norm_sums(pe, n_fin, ones)

        @block.scalar
        def _(act):
            act.dma_start(silu_c, c_d).then_inc(vec_in, 16)
            act.dma_start(vec[:, :], vecs_d).then_inc(vec_in, 16)
            act.dma_start(x[:, :, META:L], x_d).then_inc(x_in, 16)
            act.dma_start(const[:, :], consts_d).then_inc(const_in, 16)
            for k in range(4):
                act.dma_start(ada_w[:, 4 * k:4 * k + 4, :], ada_d[:, 4 * k:4 * k + 4, :]).then_inc(ada_in[k], 16)
            act.dma_start(x[:, :, 0:META], meta_d).then_inc(later_in, 16)
            act.dma_start(keys, keys_d).then_inc(later_in, 16)
            act.wait_ge(vec_in, 32)
            act.activation(silu_c, silu_c, ACT.Silu).then_inc(silu_c_ready, 1)
            exp_log(act)
            act.wait_ge(x_in, 16)
            norm_rstd(act, n_in1, lambda c: xf[:, c, :], 1.0 / D, 0)
            split_slot(act, TURN["qk_sb"], 0)
            for c in range(DC):
                high_normed(act, s_in1, c, lambda c: mod[:, c:c + 1])
            for s in range(1, RING):
                split_slot(act, TURN["qk_sb"], s)

            act.wait_ge(gates_ready, 1)
            act.activation(i_row, ps[0:4, 4, :], ACT.Identity, bias=col("b_igate", 0, 4)).then_inc(gates_taken, 1)
            act.activation(f_row, ps[32:36, 4, :], ACT.Identity, bias=vec[32:36, VEC["b_fgate"]:VEC["b_fgate"] + 1])\
                .then_inc(gates_taken, 1)
            for name, n in (("qk_sb", 8), ("v_sb", 4), ("qk_ml", 8), ("v_ml", 4), ("o_ml", 4)):
                if name == "qk_ml":
                    act.wait_ge(pads_zeroed, 5)
                    act.wait_ge(row_min, 2)
                    act.activation(e_row, e_row, ACT.Exp).then_inc(row_act, 1)
                    act.wait_ge(row_act, 1)
                    act.activation(e_row, e_row, ACT.Ln, bias=1.0).then_inc(row_act, 1)
                for t in range(n):
                    if name.startswith("v"):
                        split_next(act, name, 0, t)
                        continue
                    if name == "qk_sb":
                        wait(act, ada_done, t + 3)
                        act.dma_start(ada_late[:, t % 2], ada_d[:, 4 * (t + 4):4 * (t + 5), :])\
                            .then_inc(ada_late_in[t % 2], 16)
                    act.wait_ge(slot_used, used(TURN[name], t))
                    src = ps[:, t % 4, :]
                    if name == "o_ml":
                        act.activation(sig_o[:, t, :], src, ACT.Sigmoid).then_inc(win_taken, 1)
                    else:
                        dst = qk[:, t, :] if name == "qk_sb" else conv_in[:, t, CONV1 - 1:]
                        act.activation(dst, src, ACT.Copy).then_inc(win_taken, 1)
                        split_next(act, name, t // 4, t % 4)
                if name == "v_sb":
                    act.wait_ge(ada_done, 12)
                for b in range(TB if name.startswith("v") else 0):
                    act.activation((v_sb if name == "v_sb" else v_ml)[:, b, :], ps[:, b, :], ACT.Copy).then_inc(win_taken, 1)
            act.wait_ge(win_taken, 8)
            exp_log(act)
            norm_rstd(act, n_qk, lambda c: qk[:, c, :], 1.0 / SB_DIM, 0)

            def sb_copy(h):
                act.wait_ge(z_ready, h + 1)
                wait(act, logw_ready, h - 1)
                act.activation(z_buf[:, h % 2, :], ps[:, 0:3, :].rearrange("p a b -> p (a b)")[:, 0:1280], ACT.Copy,
                               scale=SB_DIM ** -0.5).then_inc(z_copied, 1)

            def sb_weights(h):
                act.wait_ge(logw_ready, h + 1)
                act.activation(w_buf[:, h % 2, :], w_buf[:, h % 2, :], ACT.Exp).then_inc(w_ready, 1)

            sb_copy(0)
            for h in range(SB_HEADS):
                act.wait_ge(nabs_ready, h + 1)
                act.activation(sp_buf[:, h % 2, :], sp_buf[:, h % 2, :], ACT.Exp).then_inc(e_ready, 1)
                act.wait_ge(e_ready, h + 1)
                act.activation(sp_buf[:, h % 2, :], sp_buf[:, h % 2, :], ACT.Ln, bias=1.0).then_inc(log_ready, 1)
                if h + 1 < SB_HEADS:
                    sb_copy(h + 1)
                if h:
                    sb_weights(h - 1)
            sb_weights(SB_HEADS - 1)
            for c in range(8):
                act.wait_ge(conv_step, 4 * (c + 1))
                act.activation(conv[:, c, :], conv[:, c, :], ACT.Silu).then_inc(conv_silu, 1)
            exp_log(act)
            norm_rstd(act, n_ysb, lambda c: mixed[:, c, :], 1.0 / SB_DIM, 0, lambda c: act.wait_ge(y_taken, c + 1))

            act.wait_ge(max_step, MAX_STEPS)
            act.activation(e_row, e_row, ACT.Exp, scale=-1.0).then_inc(row_act, 1)
            act.wait_ge(u_col_ready, 1)
            for h in range(ML_HEADS):
                act.wait_ge(mb_ready, h + 1)
                wait(act, wqk_ready, h - 1)
                for s in range(TB):
                    o = (0, 512, 1024, 896)[s]
                    act.activation(z_buf[:, h % 2, o:o + SEQ - s * P],
                                   ps[:, 3 + o // BANK, o % BANK:o % BANK + SEQ - s * P], ACT.Exp,
                                   bias=u_col[:, s, h:h + 1], scale=-1.0).then_inc(dec_ready, 1)
                act.wait_ge(num_ready, 2 * h + 2)
                wait(act, ml_out, h - 1)
                act.activation(den_floor[:, h % 2, :], ps[:, 3, :], ACT.Copy).then_inc(floor_ready, 1)
            act.wait_ge(num_ready, 2 * ML_HEADS)
            for s in range(RING):
                split_slot(act, TURN["w_out"], s)
            act.wait_ge(normed, n_ysb.done)

            def high_mixed(c):
                act.activation(h_hi[:, c, META:L], mixed[:, c, :], ACT.Copy).then_inc(h_hi_ready, 1)

            def gated_chunk(c):
                act.wait_ge(mix_gated, c + 1)
                high_mixed(4 + c)

            for c in range(4):
                high_mixed(c)
            norm_rstd(act, n_yml, lambda c: mixed[:, 4 + c, :], 1.0 / ML_DIM, 0, lambda c: act.wait_ge(ml_out, c + 1),
                      lambda g: gated_chunk(g - 1) if g else None)
            gated_chunk(3)
            for t in range(DC):
                split_next(act, "w_out", t // 4, t % 4)
            norm_rstd(act, n_in2, lambda c: xf[:, c, :], 1.0 / D, 0, lambda c: act.wait_ge(out_added, c + 1))
            for c in range(DC):
                high_normed(act, s_in2, c, lambda c: mod[:, 3 * DC + c:3 * DC + c + 1])

            def q_copy(i):
                for s in range(RING):
                    act.wait_ge(slot_used, used(TURN["peer_q"] + i, s))
                    act.activation(at(q_peer, RING * i + s), ps[:, s, :], ACT.Copy).then_inc(q_peer_taken, 1)
                    split_next(act, "peer_q", i, s)
            turns(act, 4, q_copy)

            def score_copy(b):
                act.wait_ge(score_made, b + 1)
                wait(act, route, ROUTE * (b - 1) + 5)
                act.activation(score.rearrange("p a b -> p (a b)"), ps[:, 0:4, :].rearrange("p a b -> p (a b)"),
                               ACT.Copy).then_inc(score_ready, 1)

            def early_gelu(j, s):
                act.wait_ge(slot_used, used(j + TURN["experts_u"], s))
                wait(act, act_saved[s % 2], j * 32 + 16 * (s // 2))
                act.activation(act_u[:, s % 2, :], ps[:, 4 + s % 2, :], ACT.Gelu).then_inc(gelu_done, 1)
                split_next(act, "experts_u", j, s)
                act.wait_ge(gelu_done, j * RING + (s + 1))
                pair_d = act_d[2 * j + s // 2] if isinstance(j, int) else \
                    act_d[bass.ds(j * 2 + s // 2, 1), :, :].rearrange("o p n -> (o p) n")
                act.dma_start(pair_d[:, (s % 2) * SEQ:(s % 2 + 1) * SEQ], act_u[:, s % 2, :])\
                    .then_inc(act_saved[s % 2], 16)

            def early_turn(j):
                for s in range(RING):
                    early_gelu(j, s)

            score_copy(0)
            for b in range(TB):
                span(act, 2 * b, 2 * b + 2, early_turn)
                if b + 1 < TB:
                    score_copy(b + 1)
                act.wait_ge(route, ROUTE * b + 14)
                act.activation(best, best, ACT.Exp).then_inc(gate_exp, 1)

            def g_steps(i):
                for half in range(2):
                    wait(act, g_saved[half], i * 16)
                    for s in range(RING):
                        for k in range(4):
                            if k == 3:
                                early_gelu(i * 2 + (8 + half), s)
                            n = i * 32 + (16 * half + 4 * s + k)
                            act.wait_ge(g_made, n + 1)
                            t0 = BATCH * (4 * s + k)
                            act.activation(g_stage[half][:, :, t0:t0 + BATCH],
                                           ps[:, 6 + k % 2, :].rearrange("p (t i) -> p i t", i=NKEYS), ACT.Copy)\
                                .then_inc(g_kept, 1)
                    act.wait_ge(g_kept, i * 32 + 16 * (half + 1))
                    step_d = gates_d[:, 2 * i + half, :] if isinstance(i, int) else \
                        gates_d[:, bass.ds(i * 2 + half, 1), :].rearrange("p o n -> p (o n)")
                    act.dma_start(step_d, g_stage[half].rearrange("p i t -> p (i t)")).then_inc(g_saved[half], 16)
            turns(act, 4, g_steps)
            for k in range(2):
                act.wait_ge(g_saved[k], 16 * (SEQ // STEP // 2))
                act.wait_ge(act_saved[k], 16 * (TILES // 2))

            def gates_of(first):
                return gates_d[:, :, first] if isinstance(first, slice) else gates_d[:, :, bass.ds(first, 2 * STEP)]

            def fetch(i, p):
                pair_d = act_d[i] if isinstance(i, int) else act_d[bass.ds(i, 1), :, :].rearrange("o p n -> (o p) n")
                rows = 2 * STEP
                for dst, signal, first in ((g_late, late_in, TILES * STEP), (g_early, early_in, 0)):
                    where = slice(first + i * rows, first + (i + 1) * rows) if isinstance(i, int) else i * rows + first
                    act.dma_start(dst[:, p], gates_of(where)).then_inc(signal[p], 16)
                act.dma_start(early[:, p].rearrange("p a b -> p (a b)"), pair_d).then_inc(early_in[p], 16)

            def high_gated(k, dst, src):
                act.wait_ge(act_gated, k + 1)
                act.activation(dst, src, ACT.Copy).then_inc(act_hi, 1)

            def late_gelu(i, j, turn, s):
                act.wait_ge(slot_used, used(turn, s))
                wait(act, act_split, i * 4 + -2)
                act.activation(late[:, j, :], ps[:, 4 + j, :], ACT.Gelu).then_inc(gelu_done, 1)

            def experts(i, turn, r, p, half):
                slots = [((r + j) // RING, (r + j) % RING) for j in range(8)]

                def split_at(j):
                    split_slot(act, turn + slots[j][0], slots[j][1])

                wait(act, act_split, i * 4)
                fetch(i + 1, 1 - p)
                split_at(2)
                split_at(3)
                for j in range(2):
                    high_gated(i * 4 + (2 + j), early_hi[:, j, :], early[:, p, j, :])
                for j in range(2):
                    late_gelu(i + 1, j, turn + slots[j][0], slots[j][1])
                    split_at(4 + j)
                for j in range(2):
                    high_gated(i * 4 + (4 + j), late_hi[:, 1 - p, j, :], late[:, j, :])
                split_at(6)
                split_at(7)

            t0, last_step = TURN["experts"], TILES // 2 - 1
            fetch(0, 0)
            for j in range(2):
                late_gelu(0, j, t0, j)
            for j in range(2):
                high_gated(j, late_hi[:, 0, j, :], late[:, j, :])
            bodies(act, experts)
            for s in (2, 3):
                split_slot(act, t0 + 47, s)
            for j in range(2):
                high_gated(last_step * 4 + 2 + j, early_hi[:, j, :], early[:, last_step % 2, j, :])
            for s in range(RING):
                split_next(act, "experts", 47, s)

            act.wait_ge(y_added, TILES * DC)
            act.dma_start(table, tables_d).then_inc(tables_in, 16)
            exp_log(act)
            act.wait_ge(later_in, 32)
            norm_rstd(act, n_diff, lambda c: x[:, c, :], 1.0 / D, 1)
            for c in range(DC):
                high_normed(act, s_diff, c)

            def pair(k, rows=P):
                return ps[0:rows, 2 * k:2 * k + 2, 0:HALF]

            def qk_copy(i):
                for s in range(RING):
                    t = RING * i + s
                    act.wait_ge(slot_used, used(TURN["qk_diff"] + i, s))
                    wait(act, rope_step, t * 3 + -3)
                    act.activation(split(raw_d[:, s % 2, :]), pair(s % 2), ACT.Copy).then_inc(raw_taken, 1)
                    split_next(act, "qk_diff", i, s)
            turns(act, 4, qk_copy)

            def v_copy(dst, half, done, taken):
                act.wait_ge(slot_used, done)
                for b in range(5):
                    r = META if b == 0 else P
                    act.activation(dst[0:r, b, half * BANK:(half + 1) * BANK], ps[0:r, b, :], ACT.Copy).then_inc(taken, 1)

            for half in range(2):
                for s in range(RING):
                    split_next(act, "v_diff", half, s)
                v_copy(v_d, half, used(TURN["v_diff"] + half, 3), v_taken)
            act.wait_ge(lam_sum, 1)
            act.activation(lam_e, ps[:, 5, 0:2], ACT.Exp).then_inc(lam_exp, 1)
            act.wait_ge(meta_step, 2)
            act.activation(pm[0:META, :, :], pm[0:META, :, :], ACT.Exp, scale=DIFF_DIM ** -0.5).then_inc(meta_act, 1)
            act.wait_ge(meta_pe, 2)
            act.activation(amT[0:META, 0:8, :], ps[0:META, 5, 0:P].rearrange("p (a b) -> p a b", b=META), ACT.Copy)\
                .then_inc(meta_act, 1)
            act.wait_ge(meta_pe, 3)
            act.activation(o_d[:, :, 0:META], ps[:, 7, 0:P].rearrange("p (a b) -> p a b", b=META), ACT.Copy)\
                .then_inc(meta_act, 1)

            def keep(dst, u, b, bank, k, kept):
                frames, meta = turned_at(bank, k, b)
                act.activation(dst[:, u % 2, 1:b + 2, :], frames[:, 0:(b + 1) * P].rearrange("p (a b) -> p a b", b=P),
                               ACT.Copy).then_inc(kept, 1)
                act.activation(dst[0:META, u % 2, 0, :], meta, ACT.Copy).then_inc(kept, 1)

            units = [(h, b) for h in range(DIFF_HEADS) for b in range(TB)]
            n = len(units)
            for u in range(n + 3):
                if u < n:
                    h, b = units[u]
                    wait(act, a_turned, u - 2)
                    for m in range(2):
                        act.wait_ge(nmax_ready, 2 * u + m + 1)
                        dst = prob[:, u % 3, m, 0:META + (b + 1) * P]
                        act.activation(dst if b < TB - 1 else split(dst), score_at(D_SCORES[b] + 3 * m, b), ACT.Exp,
                                       bias=st_nmax[:, u % 3, m:m + 1], scale=DIFF_DIM ** -0.5,
                                       accum_out=st_sum[:, u % 3, m:m + 1]).then_inc(p_ready, 1)
                if 2 <= u < n + 2:
                    act.wait_ge(a_turned, u - 1)
                    wait(act, av_done, u - 3)
                    b = units[u - 2][1]
                    keep(aT, u - 2, b, 6, D_SCORES[b], aT_kept)
                if u >= 3 and units[u - 3][1] == TB - 1:
                    act.wait_ge(av_done, u - 2)
                    act.activation(o_d[:, units[u - 3][0], META:L], ps[:, 7, :], ACT.Copy).then_inc(o_taken, 1)

            def high_head(c):
                act.wait_ge(normed, n_sub.g0 + c + 1)
                act.activation(h_hi[:, c, :], o_d[:, c, :], ACT.Copy).then_inc(h_hi_ready, 1)

            norm_rstd(act, n_sub, lambda c: o_d[:, c, :], 1.0 / DIFF_V, 1, lambda c: act.wait_ge(o_taken, c + 1),
                      lambda g: high_head(g - 1) if g else None)
            high_head(7)
            for t in range(DC):
                split_next(act, "o_diff", t // 4, t % 4)

            def ffn(k, n, sp, ready):
                norm_rstd(act, n, lambda c: x[:, c, :], 1.0 / D, 1, ready)
                for c in range(DC):
                    high_normed(act, sp, c)
                act.wait_ge(ffn_zero, k + 1)

                def up(i):
                    name = f"ffn_in{k}"
                    for e in range(2):
                        act.wait_ge(slot_used, used(i + TURN[name], 2 * e))
                        wait(act, fconv_step[k], i * 6 + (3 * e - 3))
                        act.activation(split(a_pad[:, e, CONV2 - 1:]), pair(2 * e), ACT.Copy).then_inc(a_taken[k], 1)
                        split_next(act, name, i, 2 * e)
                        act.wait_ge(fconv_step[k], i * 6 + (3 * e + 3))
                        act.activation(u_ffn[:, e, :], u_ffn[:, e, :], ACT.Silu).then_inc(fsilu_done[k], 1)
                        split_next(act, name, i, 2 * e + 1)
                        act.wait_ge(ffn_gated[k], i * 2 + (e + 1))
                        act.activation(at(gated_hi, i * 2 + e), u_ffn[:, e, :], ACT.Copy).then_inc(gated_hi_done[k], 1)
                turns(act, FC // 2, up)

                def down(i):
                    for s in range(RING):
                        split_next(act, f"ffn_out{k}", i, s)
                turns(act, 5, down)

            ffn(0, n_ffn0, s_ffn0, lambda c: act.wait_ge(o_added[0], c + 1))

            exp_log(act)
            norm_rstd(act, n_lat, lambda c: x[:, c, :], 1.0 / D, 1, lambda c: act.wait_ge(ffn_added[0], c + 1))
            act.wait_ge(ffn_added[0], DC)
            act.dma_start(table, tables_d).then_inc(tables_in, 16)
            t0 = TURN["mla"]
            for k in range(6):
                act.wait_ge(slot_used, used(t0, k))
                dst = ckv[:, k, :] if k < 2 else kr_raw[0:QK_MLA, :] if k == 2 else cq[:, k - 3, :]
                act.activation(split(dst), pair(k % 4, QK_MLA if k == 2 else P), ACT.Copy).then_inc(lat_taken, 1)
            act.wait_ge(lat_taken, 6)
            norm_rstd(act, n_ckv, lambda c: ckv[:, c, :], 1.0 / KV_LORA, 1)
            norm_rstd(act, n_cq, lambda c: cq[:, c, :], 1.0 / Q_LORA, 1)
            made = 0
            for h in range(MLA_HEADS):
                if h % 8 == 7:
                    act.wait_ge(slot_used, used(t0, 6 + h // 8))
                else:
                    made += 1
                    act.wait_ge(head_made, made)
                act.activation(split(k_m[0:NOPE, h, :]), pair(h % 2, NOPE), ACT.Copy).then_inc(kn_taken, 1)
            for half in range(2):
                v_copy(v_m, half, used(t0, 8 + half), vm_taken)
            for h in range(MLA_HEADS):
                if h % 3 == 2 or h == MLA_HEADS - 1:
                    act.wait_ge(slot_used, used(t0, 10 + h // 3))
                else:
                    made += 1
                    act.wait_ge(head_made, made)
                wait(act, qrope_step, 3 * (h - 1))
                act.activation(split(raw_m[0:QK_MLA, h % 2, :]), pair(h % 2, QK_MLA), ACT.Copy).then_inc(qraw_taken, 1)
            scale = QK_MLA ** -0.5
            act.wait_ge(mm_step, 2)
            act.activation(pmm[0:META, :, :], pmm[0:META, :, :], ACT.Exp, scale=scale).then_inc(mm_act, 1)
            act.wait_ge(m_turned, 1)
            act.activation(amTm[0:META, :, :], ps[0:META, 5, 0:256].rearrange("p (a b) -> p a b", b=META), ACT.Copy)\
                .then_inc(mm_act, 1)
            act.wait_ge(m_av, 1)
            act.activation(o_m[:, :, 0:META], ps[:, 6, 0:P].rearrange("p (a b) -> p a b", b=META), ACT.Copy)\
                .then_inc(mm_act, 1)
            units = [(h, b) for h in range(MLA_HEADS) for b in range(TB)]
            n = len(units)
            for u in range(n + 3):
                if u < n:
                    h, b = units[u]
                    wait(act, m_turned, u - 1)
                    act.wait_ge(m_nmax, u + 1)
                    dst = probm[:, u % 3, 0:META + (b + 1) * P]
                    act.activation(dst if b < TB - 1 else split(dst), score_at(M_SCORES[b], b), ACT.Exp,
                                   bias=sm_nmax[:, u % 4:u % 4 + 1], scale=scale,
                                   accum_out=sm_sum[:, u % 4:u % 4 + 1]).then_inc(m_prob, 1)
                if 2 <= u < n + 2:
                    act.wait_ge(m_turned, u)
                    if u >= 4:
                        act.wait_ge(m_av, u - 2)
                    b = units[u - 2][1]
                    keep(aTm, u - 2, b, 5 + u % 2, M_SCORES[b], m_kept)
                if u >= 3 and units[u - 3][1] == TB - 1:
                    h = units[u - 3][0]
                    r = slice(64 * (h % 2), 64 * (h % 2) + 64)
                    act.wait_ge(m_av, u - 1)
                    act.activation(o_m[r, h // 2, META:L], ps[r, 7, :], ACT.Copy).then_inc(m_taken, 1)
            for s in range(RING):
                split_slot(act, TURN["o_mla"], s)
                act.wait_ge(m_taken, 4 * s + 4)
                for c in (2 * s, 2 * s + 1):
                    act.activation(h_hi[:, c, :], o_m[:, c, :], ACT.Copy).then_inc(h_hi_ready, 1)
            for t in range(DC):
                split_next(act, "o_mla", t // 4, t % 4)
            ffn(1, n_ffn1, s_ffn1, lambda c: act.wait_ge(o_added[1], c + 1))
            exp_log(act)
            norm_rstd(act, n_fin, lambda c: x[:, c, :], 1.0 / D, 1, lambda c: act.wait_ge(ffn_added[1], c + 1))
            act.wait_ge(normed, n_fin.done)
            act.dma_start(out_d, y_out[:, :, META:L]).then_inc(stored, 16)
            act.wait_ge(stored, 16)

        @block.gpsimd
        def _(pool):
            def low_parts(run):
                first, end, unsplit, _ = RUNS[run]
                with pool.Fori(first, end) as i:
                    for s in range(RING):
                        pool.wait_ge(hi_ready, i * RING + (s + 1 - unsplit))
                        pool.tensor_tensor(w_lo[:, s, :], ring[:, s, :], w_hi[:, s, :], ALU.subtract)\
                            .then_inc(lo_ready, 1)

            low_parts(0)
            pool.wait_ge(kr_step, 3)
            for h in range(MLA_HEADS):
                pool.tensor_copy(k_m[NOPE:QK_MLA, h, :], kr[NOPE:QK_MLA, :]).then_inc(kr_copied, 1)
            low_parts(2)

        @block.vector
        def _(dve):
            def modulation(first, n):
                return dve.tensor_tensor(mod[:, first:first + n], mod_sum[:, first:first + n],
                                         vec[:, VEC["b_ada"] + first:VEC["b_ada"] + first + n], ALU.add)

            def modulated_gain(k, name):
                s = (1 + 3 * k) * DC
                dve.scalar_tensor_tensor(gains[:, k, :], mod[:, s:s + DC], 1.0, vec[:, VEC[name]:VEC[name] + DC],
                                         ALU.add, ALU.mult).then_inc(gains_ready, 1)

            def modulate(group, w):
                for j in range(RING):
                    at0 = RING * group + j
                    last = dve.scalar_tensor_tensor(w[:, j, :], w[:, j, :], 1.0, silu_c, ALU.mult, ALU.mult,
                                                    accum_out=mod_sum[:, at0:at0 + 1])
                last.then_inc(ada_done, 1)

            dve.wait_ge(silu_c_ready, 1)
            for k in range(4):
                dve.wait_ge(ada_in[k], 16)
                modulate(k, ada_w[:, 4 * k:4 * k + 4, :])
            dve.wait_ge(ada_done, 4)
            dve.wait_ge(x_in, 16)
            modulation(0, 2 * DC).then_inc(mod_ready, 1)
            dve.wait_ge(mod_ready, 1)
            modulated_gain(0, "g_norm1")
            dve.wait_ge(gains_ready, 1)
            split_normed(dve, s_in1, lambda c: xf[:, c, :], lambda c: gains[:, 0, c:c + 1], lambda c: mod[:, c:c + 1])
            for k in range(8):
                dve.wait_ge(ada_late_in[k % 2], 16 * (k // 2 + 1))
                modulate(4 + k, ada_late[:, k % 2])
            dve.wait_ge(ada_done, 12)
            modulation(2 * DC, 4 * DC).then_inc(mod_ready, 1)
            dve.wait_ge(mod_ready, 2)
            modulated_gain(1, "g_norm2")
            for k in range(2):
                dve.memset(f_pad[k][:, 0:SEQ], 0.0).then_inc(pads_zeroed, 1)
                dve.memset(m_pad[k][:, 0:SEQ], 0.0).then_inc(pads_zeroed, 1)
            dve.memset(conv_in[:, :, 0:CONV1 - 1], 0.0).then_inc(pads_zeroed, 1)
            dve.wait_ge(pads_zeroed, 5)
            dve.wait_ge(gates_taken, 2)
            dve.tensor_scalar(n_row, f_row, 0.0, 2.0, ALU.min, ALU.mult).then_inc(row_min, 1)
            dve.wait_ge(row_min, 1)
            dve.tensor_tensor(e_row, n_row, f_row, ALU.subtract).then_inc(row_min, 1)
            dve.wait_ge(row_act, 2)
            dve.tensor_scalar(f_row, f_row, 0.0, None, ALU.min).then_inc(row_step, 1)
            dve.wait_ge(row_step, 1)
            dve.tensor_tensor(f_pad[0][:, SEQ:], f_row, e_row, ALU.subtract).then_inc(row_step, 1)
            for k in range(LOG_SEQ):
                dve.wait_ge(row_step, k + 2)
                src, dst = f_pad[k % 2], f_pad[(k + 1) % 2]
                dve.tensor_tensor(dst[:, SEQ:], src[:, SEQ:], src[:, SEQ - (1 << k):2 * SEQ - (1 << k)], ALU.add)\
                    .then_inc(row_step, 1)
            dve.wait_ge(row_step, LOG_SEQ + 2)
            dve.tensor_tensor(n_row, i_row, f_pad[1][:, SEQ:], ALU.subtract).then_inc(row_step, 1)
            norm_apply(dve, n_qk, lambda c: qk[:, c, :], lambda c: col("g_q_sb" if c < 4 else "g_k_sb"),
                       lambda c: qk[:, c, :])

            def sb_logw(h):
                dve.wait_ge(between_ready, h + 1)
                wait(dve, y_ready, h - 1)
                dve.tensor_tensor(w_buf[:, h % 2, :], ps[:, 3:6, :].rearrange("p a b -> p (a b)")[:, 0:1280],
                                  z_buf[:, h % 2, :], ALU.add).then_inc(logw_ready, 1)

            def sb_take(pair):
                dve.wait_ge(y_ready, 2 * pair + 2)
                dve.tensor_copy(mixed[:, pair, :], ps[:, 6, :]).then_inc(y_taken, 1)

            dve.wait_ge(normed, n_qk.done)
            for h in range(SB_HEADS):
                z, sp = z_buf[:, h % 2, :], sp_buf[:, h % 2, :]
                dve.wait_ge(z_copied, h + 1)
                wait(dve, between_ready, h - 1)
                dve.scalar_tensor_tensor(sp, z, -1.0, z, ALU.mult, ALU.min).then_inc(nabs_ready, 1)
                if h:
                    sb_logw(h - 1)
                dve.wait_ge(log_ready, h + 1)
                dve.scalar_tensor_tensor(sp, z, 0.0, sp, ALU.max, ALU.add).then_inc(sp_ready, 1)
                if h >= 2 and h % 2 == 0:
                    sb_take(h // 2 - 1)
                if h == 3:
                    dve.wait_ge(row_step, ROW_STEPS)
                    dve.tensor_scalar(m_pad[0][:, SEQ:], n_row, 0.0, None, ALU.max).then_inc(max_step, 1)
                    for k in range(LOG_SEQ):
                        dve.wait_ge(max_step, k + 1)
                        src, dst = m_pad[k % 2], m_pad[(k + 1) % 2]
                        dve.tensor_tensor(dst[:, SEQ:], src[:, SEQ:], src[:, SEQ - (1 << k):2 * SEQ - (1 << k)], ALU.max)\
                            .then_inc(max_step, 1)
                    dve.wait_ge(max_step, LOG_SEQ + 1)
                    dve.tensor_tensor(e_row, m_pad[1][:, SEQ:], f_pad[1][:, SEQ:], ALU.add).then_inc(max_step, 1)
                dve.wait_ge(win_taken, 20)
                for j in range(CONV1):
                    src = conv_in[:, h, j:j + SEQ]
                    w = col("conv_w", CONV1 * h + j)
                    if j == 0:
                        dve.tensor_scalar(conv[:, h, :], src, w, None, ALU.mult).then_inc(conv_step, 1)
                    else:
                        dve.wait_ge(conv_step, CONV1 * h + j)
                        dve.scalar_tensor_tensor(conv[:, h, :], src, w, conv[:, h, :], ALU.mult, ALU.add)\
                            .then_inc(conv_step, 1)
            sb_logw(SB_HEADS - 1)
            sb_take(3)
            norm_apply(dve, n_ysb, lambda c: mixed[:, c, :], lambda c: col("g_out_sb", c), lambda c: mixed[:, c, :])

            dve.wait_ge(u_turned, 1)
            dve.tensor_copy(u_col, ps[:, 6, 0:16].rearrange("p (a b) -> p a b", b=ML_HEADS)).then_inc(u_col_ready, 1)
            for h in range(ML_HEADS):
                dve.wait_ge(mqk_ready, h + 1)
                dve.wait_ge(dec_ready, 4 * h + 4)
                wait(dve, num_ready, 2 * h - 2)
                dve.scalar_tensor_tensor(w_buf[:, h % 2, :], ps[:, 0:3, :].rearrange("p a b -> p (a b)")[:, 0:1280],
                                         ML_DIM ** -0.5, z_buf[:, h % 2, :], ALU.mult, ALU.mult).then_inc(wqk_ready, 1)
                d = den[:, h % 2, :]
                dve.wait_ge(num_ready, 2 * h + 2)
                dve.tensor_scalar(d, ps[:, 7, :], -1.0, None, ALU.mult).then_inc(den_step, 1)
                dve.wait_ge(den_step, 4 * h + 1)
                dve.tensor_tensor(d, ps[:, 7, :], d, ALU.max).then_inc(den_step, 1)
                dve.wait_ge(den_step, 4 * h + 2)
                dve.wait_ge(floor_ready, h + 1)
                dve.tensor_tensor(d, d, den_floor[:, h % 2, :], ALU.max).then_inc(den_step, 1)
                dve.wait_ge(den_step, 4 * h + 3)
                dve.reciprocal(d, d).then_inc(den_step, 1)
                dve.wait_ge(den_step, 4 * h + 4)
                dve.tensor_tensor(mixed[:, 4 + h, :], ps[:, 6, :], d, ALU.mult).then_inc(ml_out, 1)
            for c in range(4):
                gi = n_yml.g0 + c
                dve.wait_ge(rstd_ready, gi + 1)
                y = mixed[:, 4 + c, :]
                dve.scalar_tensor_tensor(y, y, col("g_out_ml", c), rstd1[:, gi % 2, :], ALU.mult, ALU.mult)\
                    .then_inc(normed, 1)
                dve.wait_ge(normed, gi + 1)
                dve.tensor_tensor(y, y, sig_o[:, c, :], ALU.mult).then_inc(mix_gated, 1)
                low_part(dve, s_mix, c, mixed[:, c, :], META)
            for c in range(4, DC):
                low_part(dve, s_mix, c, mixed[:, c, :], META)

            for t in range(DC):
                dve.wait_ge(slot_used, used(TURN["w_out"], t))
                dve.scalar_tensor_tensor(xf[:, t, :], ps[:, t % 4, :], mod[:, 2 * DC + t:2 * DC + t + 1], xf[:, t, :],
                                         ALU.mult, ALU.add).then_inc(out_added, 1)
            dve.wait_ge(out_added, DC)
            dve.wait_ge(gains_ready, 2)
            split_normed(dve, s_in2, lambda c: xf[:, c, :], lambda c: gains[:, 1, c:c + 1],
                         lambda c: mod[:, 3 * DC + c:3 * DC + c + 1])

            def route_block(b):
                at0 = b * ROUTE
                steps = [0]

                def end(instruction):
                    instruction.then_inc(route, 1)
                    steps[0] += 1

                def after(k):
                    dve.wait_ge(route, at0 + k)

                dve.wait_ge(score_ready, b + 1)
                for j in range(QH):
                    last = dve.max(top_v[:, j, 0:8], score[:, j, :])
                end(last)
                after(1)
                for j in range(QH):
                    last = dve.max_index(top_i[:, j, 0:8], top_v[:, j, 0:8], score[:, j, :])
                end(last)
                after(2)
                for j in range(QH):
                    last = dve.match_replace(score[:, j, :], top_v[:, j, 0:8], score[:, j, :], LOWEST)
                end(last)
                after(3)
                for j in range(QH):
                    last = dve.max(top_v[:, j, 8:16], score[:, j, :])
                end(last)
                after(4)
                for j in range(QH):
                    last = dve.max_index(top_i[:, j, 8:16], top_v[:, j, 8:16], score[:, j, :])
                end(last)
                after(5)
                end(dve.tensor_copy(top_if, top_i))
                pairs = top_v.rearrange("p (h t) k -> p h t k", t=2)
                grid = [P, PEER_HEADS, TOPK, TOPK]
                end(dve.tensor_tensor(cand.rearrange("p h (a b) -> p h a b", b=TOPK),
                                      pairs[:, :, 0, :].unsqueeze(3).broadcast_to(grid),
                                      pairs[:, :, 1, :].unsqueeze(2).broadcast_to(grid), ALU.add))
                after(7)
                for h in range(PEER_HEADS):
                    last = dve.max(best[:, h, 0:8], cand[:, h, :])
                end(last)
                after(8)
                for h in range(PEER_HEADS):
                    last = dve.max_index(pos[:, h, 0:8], best[:, h, 0:8], cand[:, h, :])
                end(last)
                after(9)
                for h in range(PEER_HEADS):
                    last = dve.match_replace(cand[:, h, :], best[:, h, 0:8], cand[:, h, :], LOWEST)
                end(last)
                after(10)
                for h in range(PEER_HEADS):
                    last = dve.max(best[:, h, 8:16], cand[:, h, :])
                end(last)
                after(11)
                for h in range(PEER_HEADS):
                    last = dve.max_index(pos[:, h, 8:16], best[:, h, 8:16], cand[:, h, :])
                end(last)
                after(12)
                end(dve.tensor_copy(gate_sum[:, 0, :], best[:, :, 0]))
                after(13)
                end(dve.tensor_tensor(best, best, gate_sum[:, 0, :].unsqueeze(2)
                                      .broadcast_to([P, PEER_HEADS, TOPK]), ALU.subtract))
                where = pos.rearrange("p h k -> p (h k)")
                end(dve.tensor_scalar(pos_ab[:, 0, :], where, 4, None, ALU.logical_shift_right))
                end(dve.tensor_scalar(pos_ab[:, 1, :], where, TOPK - 1, None, ALU.bitwise_and))
                after(16)
                end(dve.tensor_copy(pos_abf, pos_ab))
                halves = top_if.rearrange("p (h t) k -> p h t k", t=2)
                flat = onehot.rearrange("p h k a -> p (h k) a")
                for t in range(2):
                    after(17 + 3 * t)
                    end(dve.tensor_tensor(flat, pos_abf[:, t, :].unsqueeze(2).broadcast_to([P, NSEL, TOPK]),
                                          cst("iota", TOPK).unsqueeze(1).broadcast_to([P, NSEL, TOPK]),
                                          ALU.is_equal))
                    after(18 + 3 * t)
                    end(dve.tensor_tensor(onehot, onehot, halves[:, :, t, :].unsqueeze(2).broadcast_to(grid),
                                          ALU.mult))
                    after(19 + 3 * t)
                    end(dve.tensor_reduce(routed[:, t, :], flat, AX, ALU.add))
                dve.wait_ge(gate_exp, b + 1)
                end(dve.tensor_reduce(gate_sum[:, 0, :], best, AX, ALU.add))
                after(24)
                end(dve.reciprocal(gate_sum[:, 1, :], gate_sum[:, 0, :]))
                after(25)
                end(dve.tensor_tensor(routed[:, 2, :].rearrange("p (h k) -> p h k", k=TOPK), best,
                                      gate_sum[:, 1, :].unsqueeze(2).broadcast_to([P, PEER_HEADS, TOPK]),
                                      ALU.mult))
                assert steps[0] == ROUTE
                dve.wait_ge(routed_t, b + 1)
                for k, dst in enumerate((idx1, idx2, gate_t)):
                    here = dst[:, b * P:(b + 1) * P] if isinstance(b, int) else dst[:, bass.ds(b * P, P)]
                    dve.tensor_copy(here, ps[:, 6, k * P:(k + 1) * P]).then_inc(routed_kept, 1)

            for b in range(TB):
                route_block(b)

            def hot_batch(n, k, t0):
                def token(row, t):
                    return row[:, t0 + t:t0 + t + 1] if isinstance(t0, int) else row[:, bass.ds(t0 + t, 1)]

                wait(dve, g_made, n + -1)
                here = idx2[:, t0:t0 + BATCH] if isinstance(t0, int) else idx2[:, bass.ds(t0, BATCH)]
                dve.tensor_tensor(hot2[:, k, :, :], here.unsqueeze(2).broadcast_to([P, BATCH, NKEYS]),
                                  cst("iota").unsqueeze(1).broadcast_to([P, BATCH, NKEYS]), ALU.is_equal)
                for t in range(BATCH):
                    last = dve.tensor_scalar(hot1g[:, k, t, :], cst("iota"), token(idx1, t), token(gate_t, t),
                                             ALU.is_equal, ALU.mult)
                last.then_inc(hot_ready, 1)

            dve.wait_ge(routed_kept, 3 * TB)

            def g_step(i):
                for k in range(4):
                    hot_batch(i * 4 + k, k % 2, i * 4 * BATCH + k * BATCH)
            turns(dve, SEQ // BATCH // 4, g_step)

            def gated_pair(i, j, act_e, gates):
                a = act_e[:, j, :].rearrange("p (a t) -> p a t", t=STEP)
                dve.tensor_tensor(a, a, gates[:, :, j * STEP:(j + 1) * STEP], ALU.mult).then_inc(act_gated, 1)

            def low_pair(k, lo, src, hi):
                for j in range(2):
                    dve.wait_ge(act_hi, k + j + 1)
                    dve.tensor_tensor(lo[:, j, :], src[:, j, :], hi[:, j, :], ALU.subtract).then_inc(act_split, 1)

            def late_pair(i, k, p, uses):
                dve.wait_ge(late_in[p], uses * 16 + 16)
                for j in range(2):
                    dve.wait_ge(gelu_done, i * 2 + (TILES + j + 1))
                    gated_pair(i, j, late, g_late[:, p])
                low_pair(k, late_lo[:, p], late, late_hi[:, p])

            def early_pair(i, k, p, uses):
                dve.wait_ge(early_in[p], uses * 32 + 32)
                for j in range(2):
                    gated_pair(i, j, early[:, p], g_early[:, p])
                low_pair(k, early_lo, early[:, p], early_hi)

            def add_share(turn, s, part0, whole0):
                for d in range(DC):
                    if d < DC - 1:
                        dve.wait_ge(y_part, part0 + (d + 1))
                    else:
                        dve.wait_ge(slot_used, used(turn, s))
                    wait(dve, y_added, whole0 + (d + 1 - DC))
                    dve.scalar_tensor_tensor(xf[:, d, :], ps[:, d % 4, :], mod[:, 5 * DC + d:5 * DC + d + 1],
                                             xf[:, d, :], ALU.mult, ALU.add).then_inc(y_added, 1)

            def experts(i, turn, r, p, half):
                early_pair(i, i * 4 + 2, p, half)
                late_pair(i + 1, i * 4 + 4, 1 - p, half + p)
                for k, j in ((0, 3), (1, 5)):
                    add_share(turn + (r + j) // RING, (r + j) % RING, i * 14 + 7 * k, i * 16 + DC * k)

            t0, last_step = TURN["experts"], TILES // 2 - 1
            late_pair(0, 0, 0, 0)
            bodies(dve, experts)
            early_pair(last_step, last_step * 4 + 2, last_step % 2, last_step // 2)
            for k in range(2):
                add_share(t0 + 47, 2 * k + 1, last_step * 14 + 7 * k, last_step * 16 + DC * k)

            dve.wait_ge(y_added, TILES * DC)
            split_normed(dve, s_diff, lambda c: x[:, c, :], lambda c: col("a_attn_norm", c))
            o = VEC["lambdas"]
            dve.tensor_tensor(lam_p, vec[:, o:o + 2], vec[:, o + 2:o + 4], ALU.mult).then_inc(lam_step, 1)

            def pair(k, rows=P):
                return ps[0:rows, 2 * k:2 * k + 2, 0:HALF]

            def rope(dst, raw, rotated, tmp, cos, sin, step, step0):
                dve.tensor_tensor(dst, raw, cos, ALU.mult).then_inc(step, 1)
                dve.tensor_tensor(split(tmp), rotated, split(sin), ALU.mult).then_inc(step, 1)
                dve.wait_ge(step, step0 + 2)
                dve.tensor_tensor(dst, dst, tmp, ALU.add).then_inc(step, 1)

            dve.wait_ge(tables_in, 16)

            def rope_tiles(i):
                for s in range(RING):
                    t = RING * i + s
                    dve.wait_ge(raw_taken, t + 1)
                    dve.wait_ge(rot_ready, t + 1)
                    rope(at(qk_d, t), raw_d[:, s % 2, :], pair(2 + s % 2), tmp_d[:, s % 2, :], tab("cos_d"),
                         tab("sin_d"), rope_step, t * 3)
            turns(dve, 4, rope_tiles)
            dve.wait_ge(lam_exp, 1)
            dve.scalar_tensor_tensor(neg_lam, lam_e[:, 1:2], LAM_INIT, lam_e[:, 0:1], ALU.subtract, ALU.subtract)\
                .then_inc(lam_step, 1)
            pm4 = pm[0:META, :, :].rearrange("p (m h) k -> p m h k", m=2)
            src4 = ps[0:META, 6:8, 0:P].rearrange("p m (h k) -> p m h k", k=META)
            wide = [META, 16, META]
            dve.wait_ge(meta_pe, 1)
            for m in range(2):
                last = dve.tensor_reduce(pm_max[0:META, 8 * m:8 * m + 8], src4[:, m], AX, ALU.max)
            last.then_inc(meta_step, 1)
            dve.wait_ge(meta_step, 1)
            for m in range(2):
                last = dve.tensor_tensor(pm4[:, m], src4[:, m], pm_max[0:META, 8 * m:8 * m + 8].unsqueeze(2)
                                         .broadcast_to([META, 8, META]), ALU.subtract)
            last.then_inc(meta_step, 1)
            dve.wait_ge(meta_act, 1)
            dve.tensor_reduce(pm_sum[0:META, :], pm[0:META, :, :], AX, ALU.add).then_inc(meta_step, 1)
            dve.wait_ge(meta_step, 3)
            dve.reciprocal(pm_rec[0:META, :], pm_sum[0:META, :]).then_inc(meta_step, 1)
            dve.wait_ge(meta_step, 4)
            dve.wait_ge(lam_step, 2)
            dve.tensor_scalar(pm_rec[0:META, 8:16], pm_rec[0:META, 8:16], neg_lam[0:META, :], None, ALU.mult)\
                .then_inc(meta_step, 1)
            dve.wait_ge(meta_step, 5)
            dve.tensor_tensor(pm[0:META, :, :], pm[0:META, :, :], pm_rec[0:META, :].unsqueeze(2).broadcast_to(wide),
                              ALU.mult).then_inc(meta_step, 1)
            dve.wait_ge(meta_step, 6)
            dve.tensor_tensor(pm[0:META, 0:8, :], pm[0:META, 0:8, :], pm[0:META, 8:16, :], ALU.add)\
                .then_inc(meta_step, 1)

            def row_max(dst, src, b):
                return dve.tensor_reduce(dst, src, AX if b < TB - 1 else mybir.AxisListType.XY, ALU.max)

            units = [(h, b) for h in range(DIFF_HEADS) for b in range(TB)]
            n = len(units)
            scale = DIFF_DIM ** -0.5
            for u in range(n + 1):
                if u < n:
                    b = units[u][1]
                    for m in range(2):
                        k = 2 * u + m
                        dve.wait_ge(s_made, k + 1)
                        row_max(st_max[:, u % 3, m:m + 1], score_at(D_SCORES[b] + 3 * m, b), b).then_inc(max_ready, 1)
                        dve.wait_ge(max_ready, k + 1)
                        wait(dve, p_ready, k - 5)
                        dve.tensor_scalar(st_nmax[:, u % 3, m:m + 1], st_max[:, u % 3, m:m + 1], -scale, None, ALU.mult)\
                            .then_inc(nmax_ready, 1)
                if u:
                    v = u - 1
                    W = META + (units[v][1] + 1) * P
                    dve.wait_ge(p_ready, 2 * v + 2)
                    dve.reciprocal(st_rec[:, v % 3, :], st_sum[:, v % 3, :]).then_inc(rec_step, 1)
                    dve.wait_ge(rec_step, 3 * v + 1)
                    dve.tensor_tensor(st_rec[:, v % 3, 1:2], st_rec[:, v % 3, 1:2], neg_lam, ALU.mult).then_inc(rec_step, 1)
                    p0, p1 = prob[:, v % 3, 0, 0:W], prob[:, v % 3, 1, 0:W]
                    dve.tensor_scalar(p0, p0, st_rec[:, v % 3, 0:1], None, ALU.mult).then_inc(rec_step, 1)
                    dve.wait_ge(rec_step, 3 * v + 3)
                    dve.scalar_tensor_tensor(p0, p1, st_rec[:, v % 3, 1:2], p0, ALU.mult, ALU.add).then_inc(a_ready, 1)
            for c in range(8):
                gi = n_sub.g0 + c
                dve.wait_ge(rstd_ready, gi + 1)
                r = rstd2[:, gi % 2, :]
                dve.tensor_scalar(r, r, 1.0 - LAM_INIT, None, ALU.mult).then_inc(lam_step, 1)
                dve.wait_ge(lam_step, 3 + c)
                dve.scalar_tensor_tensor(o_d[:, c, :], o_d[:, c, :], col("a_sub_norm"), r, ALU.mult, ALU.mult)\
                    .then_inc(normed, 1)
                if c:
                    low_part(dve, s_od, c - 1, o_d[:, c - 1, :], 0)
            low_part(dve, s_od, DC - 1, o_d[:, DC - 1, :], 0)

            def out_add(name, k):
                for t in range(DC):
                    dve.wait_ge(slot_used, used(TURN[name], t))
                    dve.tensor_tensor(split(x[:, t, :]), split(x[:, t, :]), pair(t % 2), ALU.add).then_inc(o_added[k], 1)
                dve.wait_ge(o_added[k], DC)

            def ffn(k, n, sp):
                split_normed(dve, sp, lambda c: x[:, c, :], lambda c: col("ffn_norm", DC * k + c))
                dve.memset(a_pad[:, :, 0:CONV2 - 1], 0.0).then_inc(ffn_zero, 1)

                def up(i):
                    for e in range(2):
                        f = i * 2 + e
                        s0 = i * 6 + 3 * e
                        u = u_ffn[:, e, :]

                        def column(name, width, j, f=f):
                            o = VEC[name] + FC * width * k + j
                            if isinstance(f, int):
                                return vec[:, o + width * f:o + width * f + 1]
                            return vec[:, bass.ds(f * width + o, 1)]

                        dve.wait_ge(a_taken[k], f + 1)
                        wait(dve, gated_split[k], i * 2 + (e - 1))
                        dve.tensor_scalar(u, a_pad[:, e, 0:L], column("ffn_conv_w", CONV2, 0), column("ffn_conv_b", 1, 0),
                                          ALU.mult, ALU.add).then_inc(fconv_step[k], 1)
                        for j in range(1, CONV2):
                            dve.wait_ge(fconv_step[k], s0 + j)
                            dve.scalar_tensor_tensor(u, a_pad[:, e, j:j + L], column("ffn_conv_w", CONV2, j), u,
                                                     ALU.mult, ALU.add).then_inc(fconv_step[k], 1)
                        dve.wait_ge(fsilu_done[k], f + 1)
                        dve.wait_ge(slot_used, used(i + TURN[f"ffn_in{k}"], 2 * e + 1))
                        dve.tensor_tensor(split(u), split(u), pair(2 * e + 1), ALU.mult).then_inc(ffn_gated[k], 1)
                        dve.wait_ge(gated_hi_done[k], f + 1)
                        dve.tensor_tensor(at(gated_lo, f), u, at(gated_hi, f), ALU.subtract).then_inc(gated_split[k], 1)
                turns(dve, FC // 2, up)

                for t in range(DC):
                    dve.wait_ge(slot_used, used(TURN[f"ffn_out{k}"], 3 * t + 2))
                    dve.tensor_tensor(split(x[:, t, :]), split(x[:, t, :]), pair(t % 4), ALU.add).then_inc(ffn_added[k], 1)
                dve.wait_ge(ffn_added[k], DC)

            out_add("o_diff", 0)
            ffn(0, n_ffn0, s_ffn0)

            dve.wait_ge(rstd_ready, n_lat.done)
            r = rstd2[:, n_lat.g0 % 2, :]
            for c in range(DC):
                dve.scalar_tensor_tensor(h_kv[:, c, :], x[:, c, :], col("kv_norm", c), r, ALU.mult, ALU.mult)
            for c in range(DC):
                last = dve.scalar_tensor_tensor(h_q[:, c, :], x[:, c, :], col("b_attn_norm", c), r, ALU.mult, ALU.mult)
            last.then_inc(normed, 1)
            R = QK_MLA
            dve.wait_ge(kr_rot, 1)
            dve.wait_ge(tables_in, 32)
            rope(kr[0:R, :], kr_raw[0:R, :], pair(0, R), tmp_m[0:R, 0, :], tab("cos_m", L, R), tab("sin_m", L, R),
                 kr_step, 0)
            norm_apply(dve, n_ckv, lambda c: ckv[:, c, :], lambda c: col("kv_a_norm", c), lambda c: ckv[:, c, :])
            norm_apply(dve, n_cq, lambda c: cq[:, c, :], lambda c: col("b_q_a_norm", c), lambda c: cq[:, c, :])
            for h in range(MLA_HEADS):
                dve.wait_ge(qraw_taken, h + 1)
                dve.wait_ge(qrot_ready, h + 1)
                rope(q_m[0:R, h, :], raw_m[0:R, h % 2, :], pair(2 + h % 2, R), tmp_m[0:R, h % 2, :],
                     tab("cos_m", L, R), tab("sin_m", L, R), qrope_step, 3 * h)
            dve.wait_ge(m_made, 1)
            src = ps[0:META, 7, 0:256].rearrange("p (h k) -> p h k", k=META)
            dve.tensor_reduce(pmm_max[0:META, :], src, AX, ALU.max).then_inc(mm_step, 1)
            dve.wait_ge(mm_step, 1)
            dve.tensor_tensor(pmm[0:META, :, :], src, pmm_max[0:META, :].unsqueeze(2).broadcast_to(wide), ALU.subtract)\
                .then_inc(mm_step, 1)
            dve.wait_ge(mm_act, 1)
            dve.tensor_reduce(pmm_sum[0:META, :], pmm[0:META, :, :], AX, ALU.add).then_inc(mm_step, 1)
            dve.wait_ge(mm_step, 3)
            dve.reciprocal(pmm_rec[0:META, :], pmm_sum[0:META, :]).then_inc(mm_step, 1)
            dve.wait_ge(mm_step, 4)
            dve.tensor_tensor(pmm[0:META, :, :], pmm[0:META, :, :], pmm_rec[0:META, :].unsqueeze(2).broadcast_to(wide),
                              ALU.mult).then_inc(mm_step, 1)
            units = [(h, b) for h in range(MLA_HEADS) for b in range(TB)]
            n = len(units)
            scale = QK_MLA ** -0.5
            for u in range(n + 1):
                if u < n:
                    b = units[u][1]
                    dve.wait_ge(m_made, u + 2)
                    row_max(sm_max[:, u % 4:u % 4 + 1], score_at(M_SCORES[b], b), b).then_inc(m_max, 1)
                    dve.wait_ge(m_max, u + 1)
                    wait(dve, m_prob, u - 3)
                    dve.tensor_scalar(sm_nmax[:, u % 4:u % 4 + 1], sm_max[:, u % 4:u % 4 + 1], -scale, None, ALU.mult)\
                        .then_inc(m_nmax, 1)
                if u:
                    v = u - 1
                    p = probm[:, v % 3, 0:META + (units[v][1] + 1) * P]
                    dve.wait_ge(m_prob, v + 1)
                    dve.reciprocal(sm_rec[:, v % 4:v % 4 + 1], sm_sum[:, v % 4:v % 4 + 1]).then_inc(m_rec, 1)
                    dve.wait_ge(m_rec, v + 1)
                    dve.tensor_scalar(p, p, sm_rec[:, v % 4:v % 4 + 1], None, ALU.mult).then_inc(m_scaled, 1)
            for c in range(DC):
                low_part(dve, s_om, c, o_m[:, c, :], 0)
            out_add("o_mla", 1)
            ffn(1, n_ffn1, s_ffn1)
            norm_apply(dve, n_fin, lambda c: x[:, c, :], lambda c: col("final_norm", c), lambda c: y_out[:, c, :])


def feature_slots(w):
    K, N = w.shape
    return w.reshape(K // P, P, N // P, P).transpose(2, 1, 0, 3).reshape(N // P, P, (K // P) * P)


def token_slots(w):
    return w.reshape(-1, 2, P, BANK).transpose(0, 2, 1, 3).reshape(-1, P, SLOT)


def pad_slot(a):
    out = np.zeros((a.shape[0], P, SLOT), np.float32)
    out[:, :, :a.shape[2]] = a
    return out


def columns(v):
    return np.ascontiguousarray(v).reshape(-1, P).T


def kernel(**inp):
    import concourse.bacc as bacc
    from concourse.bass_utils import run_bass_kernel_spmd

    a = {k: np.asarray(v) for k, v in inp.items()}
    f32 = np.float32
    ada = np.ascontiguousarray(a["w_ada"][0].T.reshape(6 * DC, P, D).transpose(1, 0, 2))
    w_in = a["w_in"][0]
    eu = a["expert_u"][0].reshape(NKEYS, P, DC, P).transpose(0, 3, 2, 1).reshape(NKEYS, P, SLOT)
    ev = a["expert_v"][0].reshape(NKEYS, P, SLOT)
    eu, ev = eu.reshape(2, TILES // 2, 2, P, SLOT), ev.reshape(2, TILES // 2, 2, P, SLOT)
    steps = np.stack([eu[1, 1:], ev[0, :-1], ev[1, :-1]], 1).reshape(-1, P, SLOT)
    experts = np.concatenate([eu[0].reshape(-1, P, SLOT), eu[1, 0], steps, ev[0, -1], ev[1, -1]], 0)
    qkv = a["a_w_qkv_2"][0]

    def ffn_slots(k):
        w = feature_slots(a["ffn_w_in_2"][k])
        up = np.stack([w[:FC], w[FC:]], 1).reshape(2 * FC, P, SLOT)
        down = np.zeros((DC, P, 3 * SLOT), f32)
        down[:, :, :FC * P] = feature_slots(a["ffn_w_out_2"][k])
        return [up, down.reshape(DC, P, 3, SLOT).transpose(0, 2, 1, 3).reshape(3 * DC, P, SLOT)]

    dkv, ukv, uq = a["kv_w_dkv_2"], a["kv_w_ukv_2"], a["b_w_uq_2"][0]
    rope_tile = np.zeros((1, P, DC, P), f32)
    rope_tile[0, :, :, :QK_MLA] = dkv[:, KV_LORA - NOPE:].reshape(DC, P, QK_MLA).transpose(1, 0, 2)
    ukv4 = ukv.reshape(KVC, P, MLA_HEADS, NOPE + MLA_V)
    k_part = ukv4[..., :NOPE].transpose(2, 1, 0, 3).reshape(2, 8, P, KVC * NOPE).transpose(0, 2, 1, 3).reshape(2, P, SLOT)
    v_part = ukv4[..., NOPE:].reshape(KVC, P, 2, BANK).transpose(2, 1, 0, 3).reshape(2, P, SLOT)
    uq_h = uq.reshape(QC, P, MLA_HEADS, QK_MLA).transpose(2, 1, 0, 3).reshape(MLA_HEADS, P, QC * QK_MLA)
    uq_pad = np.zeros((18, P, QC * QK_MLA), f32)
    uq_pad[:MLA_HEADS] = uq_h
    uq_part = pad_slot(uq_pad.reshape(6, 3, P, QC * QK_MLA).transpose(0, 2, 1, 3).reshape(6, P, 3 * QC * QK_MLA))
    parts = [feature_slots(w_in[:, 0:1024]), token_slots(w_in[:, 1024:1536]),
             feature_slots(w_in[:, 1536:2560]), token_slots(w_in[:, 2560:3072]), feature_slots(w_in[:, 3072:3584]),
             feature_slots(a["w_out"][0]), feature_slots(a["w_q_peer"][0]), experts,
             feature_slots(qkv[:, 0:2048]), token_slots(qkv[:, 2048:2560]), token_slots(qkv[:, 2560:3072]),
             feature_slots(a["a_w_o_2"][0]), *ffn_slots(0),
             feature_slots(dkv[:, :KV_LORA]), rope_tile.reshape(1, P, SLOT), feature_slots(a["b_w_dq_2"][0]),
             k_part, v_part, uq_part, feature_slots(a["b_w_o_2"][0]), *ffn_slots(1)]
    stream = np.concatenate(parts, 0)
    assert stream.shape == (TURNS * RING, P, SLOT), stream.shape

    vec = np.zeros((P, NVEC), f32)

    def put(name, v, rows=P):
        vec[:rows, VEC[name]:VEC[name] + v.shape[1]] = v

    for name, key in (("b_ada", "b_ada"), ("g_norm1", "g_norm1"), ("g_out_sb", "g_out_sb"),
                      ("g_out_ml", "g_out_ml"), ("g_norm2", "g_norm2"), ("a_attn_norm", "a_attn_norm_2"),
                      ("a_sub_norm", "a_sub_norm_2"), ("kv_norm", "kv_norm_2"), ("kv_a_norm", "kv_a_norm_2"),
                      ("b_attn_norm", "b_attn_norm_2"), ("b_q_a_norm", "b_q_a_norm_2"), ("ffn_norm", "ffn_norm_2"),
                      ("ffn_conv_b", "ffn_conv_b_2"), ("final_norm", "final_norm_2")):
        put(name, columns(a[key]))
    put("conv_w", a["conv_w"][0].reshape(CONV1, DC, P).transpose(2, 1, 0).reshape(P, DC * CONV1))
    put("ffn_conv_w", a["ffn_conv_w_2"].reshape(2, CONV2, FC, P).transpose(3, 0, 2, 1).reshape(P, 2 * FC * CONV2))
    put("g_q_sb", np.tile(a["g_q_sb"][0], 2)[:, None])
    put("g_k_sb", np.tile(a["g_k_sb"][0], 2)[:, None])
    put("b_igate", a["b_igate"][0][:, None], 4)
    vec[32:36, VEC["b_fgate"]] = a["b_fgate"][0]
    gates = np.zeros((P, DC, 36), f32)
    gates[:, :, 0:4] = w_in[:, 3584:3588].reshape(DC, P, 4).transpose(1, 0, 2)
    gates[:, :, 32:36] = w_in[:, 3588:3592].reshape(DC, P, 4).transpose(1, 0, 2)
    put("w_gates", gates.reshape(P, DC * 36))
    for j, key in enumerate(("a_lambda_q1_2", "a_lambda_q2_2", "a_lambda_k1_2", "a_lambda_k2_2")):
        vec[:DIFF_DIM, VEC["lambdas"] + j] = a[key][0]
    vec[:, VEC["eps"]] = EPS1
    vec[:, VEC["eps"] + 1] = EPS2

    const = np.zeros((P, NCONST), f32)

    def constant(name, v):
        const[:v.shape[0], CONST[name]:CONST[name] + v.shape[1]] = v

    i, j = np.meshgrid(np.arange(P), np.arange(P), indexing="ij")
    constant("ident", np.eye(P, dtype=f32))
    constant("ones", np.ones((P, P), f32))
    constant("ones64", (i // 64 == j // 64).astype(f32))
    constant("tri", -(i >= j).astype(f32))
    constant("neg_ones", -np.ones((P, P), f32))
    constant("iota", j.astype(f32))
    constant("late", np.where(j < i, f32(BIG), f32(0)))
    constant("hidden", np.where(j <= i, f32(-BIG), f32(0)))
    constant("pick_head", np.repeat(np.eye(ML_HEADS, dtype=f32), P, 1))
    constant("first_half", (j[:1] < CHUNK).astype(f32))
    constant("lowest", np.full((1, CHUNK), -BIG, f32))
    table = np.zeros((P, NTABLE), f32)

    def rotary(kind, theta, rot_dim, heads, rows):
        half = rot_dim // 2
        inv = (1.0 / (f32(theta) ** (np.arange(half, dtype=f32) / f32(half)))).astype(f32)
        ang = np.arange(L, dtype=f32)[:, None] * inv[None, :]
        cos, sin, swap = np.ones((rows, L), f32), np.zeros((rows, L), f32), np.zeros((rows, rows), f32)
        for r0 in heads:
            for k in range(half):
                lo, hi = r0 + k, r0 + half + k
                cos[lo] = cos[hi] = np.cos(ang[:, k])
                sin[lo] = sin[hi] = np.sin(ang[:, k])
                swap[hi, lo] = -1.0
                swap[lo, hi] = 1.0
        for name, v in (("cos_", cos), ("sin_", sin), ("swap_", swap)):
            table[:rows, TABLE[name + kind]:TABLE[name + kind] + v.shape[1]] = v

    rotary("d", 500000.0, DIFF_DIM // 4, (0, DIFF_DIM), P)
    rotary("m", 10000.0, ROPE, (NOPE,), QK_MLA)

    arrays = {
        "c_rows": np.ascontiguousarray(np.broadcast_to(a["c"], (P, D))),
        "w_modulation": ada,
        "weight_stream": stream,
        "constants": const,
        "vectors": vec,
        "tables": table,
        "x_t": np.ascontiguousarray(a["x"][0].reshape(SEQ, DC, P).transpose(2, 1, 0)),
        "meta_t": np.ascontiguousarray(a["meta_tokens_2"].reshape(META, DC, P).transpose(2, 1, 0)),
        "keys_t": np.ascontiguousarray(a["sub_keys"][0].reshape(QH, NKEYS, P).transpose(2, 0, 1)),
    }
    nc = bacc.Bacc("TRN2", target_bir_lowering=False, num_devices=1)
    args = [nc.dram_tensor(k, v.shape, F32, kind="ExternalInput").ap() for k, v in arrays.items()]
    out = nc.dram_tensor("out_t", (P, DC, SEQ), F32, kind="ExternalOutput").ap()
    acts = nc.dram_tensor("early_acts", (TILES // 2, P, 2 * SEQ), F32, kind="Internal").ap()
    gates = nc.dram_tensor("gates", (P, SEQ // STEP, NKEYS * STEP), F32, kind="Internal").ap()
    build(nc, *args, acts, gates, out)
    r = run_bass_kernel_spmd(nc, [arrays], core_ids=[0])
    return r.results[0]["out_t"].transpose(2, 1, 0).reshape(1, SEQ, D)
```
